# Optimizing a Trainium2 kernel written in Bass

```python
import math
import jax, jax.numpy as jnp
from jax import lax
import numpy as np

D_MODEL = 1024
BATCH = 1
SEQ = 1024
DEPTH = 1

FOURIER_GROUPS = 8
FOURIER_GROUP_DIM = 128
FOURIER_WIDTH = FOURIER_GROUPS * FOURIER_GROUP_DIM
ATTN_HEAD_DIM = 64
N_HEADS = D_MODEL // (2 * ATTN_HEAD_DIM)
QK_WIDTH = N_HEADS * 2 * ATTN_HEAD_DIM
V_WIDTH = N_HEADS * 2 * ATTN_HEAD_DIM
IN_WIDTH = FOURIER_WIDTH + 2 * QK_WIDTH + V_WIDTH
N_BRANCHES = 2
D_FF = ((-(-8 * D_MODEL // 3) + 255) // 256) * 256
PLE_DIM = 256
Q_BLOCK = 128
RMS_EPS = 1e-6

kernel_name = "hybrid_fnet_diffattn_encoder_block"

def rmsnorm(x, g):
    xf = x.astype(jnp.float32)
    y = xf * lax.rsqrt(jnp.mean(xf * xf, axis=-1, keepdims=True) + RMS_EPS)
    return (y * g.astype(jnp.float32)).astype(x.dtype)

def alibi_slopes(n_heads):
    return 2.0 ** (-8.0 * jnp.arange(1, n_heads + 1, dtype=jnp.float32) / n_heads)

def lambda_init_fn(layer_idx):
    return 0.8 - 0.6 * math.exp(-0.3 * layer_idx)

def fourier_mix(u):
    b, s, _ = u.shape
    ug = u.reshape(b, s, FOURIER_GROUPS, FOURIER_GROUP_DIM).astype(jnp.float32)
    f = jnp.fft.fftn(ug, axes=(1, 3), norm="ortho").real
    return f.reshape(b, s, FOURIER_WIDTH).astype(u.dtype)

def diff_attention(q, k, v, lam, slopes, subln_g, lambda_init):
    b, s = q.shape[0], q.shape[1]
    nblk = s // Q_BLOCK
    qb = q.reshape(b, nblk, Q_BLOCK, N_HEADS, 2, ATTN_HEAD_DIM).transpose(1, 0, 2, 3, 4, 5)
    kpos = jnp.arange(s, dtype=jnp.float32)
    scale = ATTN_HEAD_DIM ** -0.5

    def block(args):
        qi, i = args
        qpos = (i * Q_BLOCK).astype(jnp.float32) + jnp.arange(Q_BLOCK, dtype=jnp.float32)
        bias = -slopes[:, None, None] * jnp.abs(qpos[:, None] - kpos[None, :])[None]
        sc = jnp.einsum('bqhcd,bkhcd->bhcqk', qi, k).astype(jnp.float32) * scale
        a = jax.nn.softmax(sc + bias[None, :, None], axis=-1)
        w = a[:, :, 0] - lam.astype(jnp.float32) * a[:, :, 1]
        return jnp.einsum('bhqk,bkhe->bqhe', w.astype(v.dtype), v)

    o = lax.map(block, (qb, jnp.arange(nblk, dtype=jnp.int32)))
    o = o.transpose(1, 0, 2, 3, 4).reshape(b, s, N_HEADS, 2 * ATTN_HEAD_DIM)
    o = rmsnorm(o, subln_g) * (1.0 - lambda_init)
    return o.reshape(b, s, V_WIDTH)

def setup_inputs(seed: int = 0) -> dict:
    key = jax.random.key(seed)
    ks = jax.random.split(key, 24)
    f32 = jnp.float32

    def w(k, shape, fan_in):
        return jax.random.normal(k, shape, f32) * (fan_in ** -0.5)

    def gain(k, shape):
        return 1.0 + 0.02 * jax.random.normal(k, shape, f32)

    L = DEPTH
    return {
        "x": jax.random.normal(ks[0], (BATCH, SEQ, D_MODEL), f32),
        "p": jax.random.normal(ks[1], (DEPTH, BATCH, SEQ, PLE_DIM), f32),
        "g_mix": gain(ks[2], (L, D_MODEL)),
        "w_in": w(ks[3], (L, D_MODEL, IN_WIDTH), D_MODEL),
        "lambda_q1": 0.1 * jax.random.normal(ks[4], (L, ATTN_HEAD_DIM), f32),
        "lambda_k1": 0.1 * jax.random.normal(ks[5], (L, ATTN_HEAD_DIM), f32),
        "lambda_q2": 0.1 * jax.random.normal(ks[6], (L, ATTN_HEAD_DIM), f32),
        "lambda_k2": 0.1 * jax.random.normal(ks[7], (L, ATTN_HEAD_DIM), f32),
        "g_subln": gain(ks[8], (L, 2 * ATTN_HEAD_DIM)),
        "w_fourier_out": w(ks[9], (L, FOURIER_WIDTH, D_MODEL), FOURIER_WIDTH),
        "w_attn_out": w(ks[10], (L, V_WIDTH, D_MODEL), V_WIDTH),
        "w_branch_gate": w(ks[11], (L, D_MODEL, N_BRANCHES * D_MODEL), D_MODEL),
        "b_branch_gate": 0.02 * jax.random.normal(ks[12], (L, N_BRANCHES * D_MODEL), f32),
        "w_o": w(ks[13], (L, D_MODEL, D_MODEL), D_MODEL),
        "g_ffn": gain(ks[14], (L, D_MODEL)),
        "w_ffn_gate": w(ks[15], (L, D_MODEL, D_FF), D_MODEL),
        "w_ffn_up": w(ks[16], (L, D_MODEL, D_FF), D_MODEL),
        "w_ffn_down": w(ks[17], (L, D_FF, D_MODEL), D_FF),
        "g_ple": gain(ks[18], (L, D_MODEL)),
        "w_ple_gate": w(ks[19], (L, D_MODEL, D_MODEL), D_MODEL),
        "w_ple_proj": w(ks[20], (L, PLE_DIM, D_MODEL), PLE_DIM),
        "g_final": gain(ks[21], (D_MODEL,)),
    }

def reference(x, p, g_mix, w_in, lambda_q1, lambda_k1, lambda_q2, lambda_k2, g_subln,
              w_fourier_out, w_attn_out, w_branch_gate, b_branch_gate, w_o,
              g_ffn, w_ffn_gate, w_ffn_up, w_ffn_down, g_ple, w_ple_gate, w_ple_proj,
              g_final):
    b, s, d = x.shape
    slopes = alibi_slopes(N_HEADS)
    for i in range(DEPTH):
        lam_init = lambda_init_fn(i)
        h = rmsnorm(x, g_mix[i])
        u = h @ w_in[i]
        u_f = u[..., :FOURIER_WIDTH]
        q = u[..., FOURIER_WIDTH:FOURIER_WIDTH + QK_WIDTH].reshape(b, s, N_HEADS, 2, ATTN_HEAD_DIM)
        k = u[..., FOURIER_WIDTH + QK_WIDTH:FOURIER_WIDTH + 2 * QK_WIDTH].reshape(b, s, N_HEADS, 2, ATTN_HEAD_DIM)
        v = u[..., FOURIER_WIDTH + 2 * QK_WIDTH:].reshape(b, s, N_HEADS, 2 * ATTN_HEAD_DIM)

        y_f = fourier_mix(u_f) @ w_fourier_out[i]

        lam = (jnp.exp(jnp.sum(lambda_q1[i].astype(jnp.float32) * lambda_k1[i].astype(jnp.float32)))
               - jnp.exp(jnp.sum(lambda_q2[i].astype(jnp.float32) * lambda_k2[i].astype(jnp.float32)))
               + lam_init)
        y_a = diff_attention(q, k, v, lam, slopes, g_subln[i], lam_init) @ w_attn_out[i]

        gates = jax.nn.sigmoid(h @ w_branch_gate[i] + b_branch_gate[i]).reshape(b, s, N_BRANCHES, d)
        merged = gates[:, :, 0] * y_f + gates[:, :, 1] * y_a
        x = x + merged @ w_o[i]

        h2 = rmsnorm(x, g_ffn[i])
        x = x + (jax.nn.silu(h2 @ w_ffn_gate[i]) * (h2 @ w_ffn_up[i])) @ w_ffn_down[i]

        h3 = rmsnorm(x, g_ple[i])
        x = x + jax.nn.sigmoid(h3 @ w_ple_gate[i]) * (p[i] @ w_ple_proj[i])
    return rmsnorm(x, g_final)


_drawn_inputs = setup_inputs


def setup_inputs(seed=0):
    import zlib

    import numpy as np

    out = dict(_drawn_inputs(seed))
    spreads = {}
    factors = {'g_mix': 3.477,
     'lambda_k1': 4.497,
     'lambda_q2': 4.742,
     'g_subln': 6.993,
     'b_branch_gate': 8.0,
     'g_ffn': 4.655,
     'g_ple': 8.0,
     'g_final': 2.75}
    for name, (base, spread) in spreads.items():
        noise = np.random.default_rng([zlib.crc32(name.encode()), seed]).standard_normal(out[name].shape)
        drawn = base * np.exp(spread * noise) if base else spread * noise
        out[name] = __import__('jax').numpy.asarray(drawn.astype(out[name].dtype))
    for name, factor in factors.items():
        out[name] = (out[name] * factor).astype(out[name].dtype)
    return out
```

```python
from contextlib import ExitStack

import concourse.bass as bass
from concourse import mybir

F32 = mybir.dt.float32
F32R = mybir.dt.float32r
ALU = mybir.AluOpType
ACT = mybir.ActivationFunctionType

P = 128
SEQ = 1024
D = 1024
KT = D // P
TT = SEQ // P
HALF = 512
GROUPS = 8
HEADS = 8
HD = 64
D_FF = 2816
FT = D_FF // P
PLE = 256
EPS = 1e-6
LAMBDA_INIT = 0.8 - 0.6
KW = 130
QUART = 256
ALIBI_W = 2 * SEQ - P
ALIBI_0 = SEQ - P
PAIRS = HEADS // 2

N_FOURIER = 0
N_ATTN = N_FOURIER + GROUPS
N_GATE = N_ATTN + 3 * HEADS
N_OUT = N_GATE + 4 * KT
N_FFN = N_OUT + KT
FFN_TURNS = FT // 2
N_PLE = N_FFN + 6 * FFN_TURNS


def ge(eng, sem, value):
    if isinstance(value, int) and value <= 0:
        return
    eng.wait_ge(sem, value)


def encoder_layer(nc, x, p, g_mix, w_in, lambda_q1, lambda_k1, lambda_q2, lambda_k2, g_subln,
                  w_fourier_out, w_attn_out, w_branch_gate, b_branch_gate, w_o, g_ffn,
                  w_ffn_gate, w_ffn_up, w_ffn_down, g_ple, w_ple_gate, w_ple_proj, g_final,
                  ident_in, chan_dft_in, pos_dft_in, distance_in, head_consts_in, out):
    x_t = x[0].rearrange("(t p) d -> t p d", p=P)
    p_t = p[0, 0].rearrange("(t p) d -> t p d", p=P)
    out_t = out[0].rearrange("(t p) d -> t p d", p=P)
    branch_scr = [nc.dram_tensor(f"branch{b}_scratch", (KT, P, SEQ), F32, kind="Internal").ap()
                  for b in range(2)]

    ctx = ExitStack()
    with ctx:
        arena_bytes = 212736
        arena = ctx.enter_context(nc.sbuf_tensor("arena", [P, arena_bytes // 4], F32))
        base = 16512
        del arena

        def place(name, at, shape, dt=F32):
            size = 4
            for n in shape[1:]:
                size *= n
            assert at % 32 == 0 and at + size <= arena_bytes, (name, at, size)
            return nc.alloc_sbuf_tensor_at(name, shape, dt, offset=base + at)

        def sem(name):
            return ctx.enter_context(nc.semaphore(name))

        K = 1024
        R1 = 64 * K
        R2 = 128 * K
        RING = 160 * K
        MISC = 184 * K
        h_hi = place("h_hi", 0, [P, KT, SEQ], F32R)
        h_lo = place("h_lo", 32 * K, [P, KT, SEQ], F32R)
        raw = [place(f"raw{r}", RING + 4 * K * r, [P, KT, P]) for r in range(2)]
        st_hi = [place(f"st_hi{r}", RING + (8 + 4 * r) * K, [P, KT, P], F32R) for r in range(2)]
        st_lo = [place(f"st_lo{r}", RING + (16 + 4 * r) * K, [P, KT, P], F32R) for r in range(2)]
        raw_row = [place(f"raw_row{r}", RING + 4 * K * r, [P, D]) for r in range(2)]
        stage = [place(f"stage{r}", MISC + 4 * K * r, [P, SEQ]) for r in range(2)]
        gain = place("gain", MISC + 8 * K, [P, D])
        xn = [place(f"xn{r}", MISC + (12 + 4 * r) * K, [P, D]) for r in range(2)]
        distance = place("distance", MISC + 12 * K, [P, ALIBI_W])
        ident = place("ident", MISC + 20 * K, [P, P])
        C = MISC + 20 * K + 512
        gate_bias = place("gate_bias", C, [P, 16])
        head_consts = place("head_consts", C + 64, [P, 24])
        mean_sq = place("mean_sq", C + 160, [P, 2])
        shifted = place("shifted", C + 192, [P, 2])
        rstd = place("rstd", C + 224, [P, 2])
        neg_half = place("neg_half", C + 256, [P, 2])
        mean_col = place("mean_col", C + 288, [P, 1])
        eps_col = place("eps_col", C + 320, [P, 2])
        lam_dot = place("lam_dot", C + 1856, [P, 2])
        lam_exp = place("lam_exp", C + 352, [P, 2])
        neg_lam = place("neg_lam", C + 384, [P, 1])
        sub_gain = place("sub_gain", C + 416, [P, 1])
        row_max = place("row_max", C + 448, [P, 2])
        neg_max = place("neg_max", C + 480, [P, 4])
        exp_sum = place("exp_sum", C + 512, [P, 4])
        inv_sum = place("inv_sum", C + 544, [P, 4])
        o_mean_sq = place("o_mean_sq", C + 576, [P, 2])
        o_rstd = place("o_rstd", C + 608, [P, 2])
        o_shifted = place("o_shifted", C + 640, [P, 2])
        f_mean_sq = place("f_mean_sq", C + 672, [P, 2])
        f_shifted = place("f_shifted", C + 704, [P, 2])
        f_rstd = place("f_rstd", C + 736, [P, 2])
        inv_raw = place("inv_raw", C + 768, [P, 1])
        lam_rows = place("lam_rows", C + 800, [P, 4, HD])
        qscale = head_consts[:, 0:8]
        slope = head_consts[:, 8:16]
        neg_slope = head_consts[:, 16:24]

        u_hi = [place(f"u_hi{r}", R1 + 8 * K * r, [P, SEQ], F32R) for r in range(2)]
        u_lo = [place(f"u_lo{r}", R1 + 8 * K * r + 4 * K, [P, SEQ], F32R) for r in range(2)]
        fold_hi = place("fold_hi", R1 + 16 * K, [P, 2, 4, 256], F32R)
        fold_lo = place("fold_lo", R1 + 24 * K, [P, 2, 4, 256], F32R)
        TAB = 16 * KW * 4
        pos_hi = place("pos_hi", R1 + 32 * K, [P, 16, KW], F32R)
        pos_lo = place("pos_lo", R1 + 32 * K + TAB, [P, 16, KW], F32R)
        F0 = R1 + 32 * K + 2 * TAB
        chan_hi = place("chan_hi", F0, [P, 256], F32R)
        chan_lo = place("chan_lo", F0 + K, [P, 256], F32R)
        far_half = [place(f"far_half{r}", F0 + 2 * K + K * r, [P, 256]) for r in range(2)]
        folded = [place(f"folded{r}", F0 + 4 * K + 2 * K * r, [P, 2, 256]) for r in range(2)]
        sin_part = [place(f"sin_part{r}", F0 + 8 * K + 1056 * r, [P, 258]) for r in range(2)]
        combo = [[place(f"combo{a}{b}", F0 + 10 * K + 64 + 1056 * (2 * a + b), [P, 258])
                  for b in range(2)] for a in range(2)]
        y_out = [place(f"y_out{r}", F0 + 16 * K + 4 * K * r, [P, SEQ]) for r in range(2)]
        pos_raw = place("pos_raw", F0 + 16 * K, [P, 16, KW])
        chan_raw = place("chan_raw", F0 + 16 * K + 8 * K + 512, [P, 256])

        q_hi = [place(f"q_hi{r}", R1 + 16 * K * r, [P, SEQ], F32R) for r in range(2)]
        q_lo = [place(f"q_lo{r}", R1 + 16 * K * r + 4 * K, [P, SEQ], F32R) for r in range(2)]
        k_hi = [place(f"k_hi{r}", R1 + 16 * K * r + 8 * K, [P, SEQ], F32R) for r in range(2)]
        k_lo = [place(f"k_lo{r}", R1 + 16 * K * r + 12 * K, [P, SEQ], F32R) for r in range(2)]
        v_hi = place("v_hi", R1 + 32 * K, [P, TT, P], F32R)
        v_lo = place("v_lo", R1 + 36 * K, [P, TT, P], F32R)
        v_t = place("v_t", R1 + 40 * K, [P, SEQ])
        probs = [[place(f"probs{r}{c}", R1 + 44 * K + 4 * K * (2 * r + c), [P, SEQ])
                  for c in range(2)] for r in range(2)]
        wt_hi = [place(f"wt_hi{r}", R1 + 60 * K + 16 * K * r, [P, TT, 2 * P], F32R) for r in range(2)]
        wt_lo = [place(f"wt_lo{r}", R1 + 68 * K + 16 * K * r, [P, TT, 2 * P], F32R) for r in range(2)]
        o_raw = place("o_raw", R1 + 92 * K, [P, 2 * P])
        o_sq = place("o_sq", R1 + 93 * K, [P, 2 * P])

        b_hi = place("b_hi", R1, [P, KT, SEQ], F32R)
        b_lo = place("b_lo", R1 + 32 * K, [P, KT, SEQ], F32R)
        merged = place("merged", R2, [P, TT, KT, P])
        sig = [place(f"sig{n}", MISC + 12 * K + 2 * K * n, [P, HALF]) for n in range(2)]
        gated = [place(f"gated{n}", MISC + 16 * K + 2 * K * n, [P, HALF]) for n in range(2)]
        wo_hi = place("wo_hi", R1, [P, KT, D], F32R)
        wo_lo = place("wo_lo", R1 + 32 * K, [P, KT, D], F32R)
        resid = place("resid", R2, [P, TT, D])

        gu_hi = [place(f"gu_hi{r}", R1 + 16 * K * r, [P, 2, SEQ], F32R) for r in range(2)]
        gu_lo = [place(f"gu_lo{r}", R1 + 16 * K * r + 8 * K, [P, 2, SEQ], F32R) for r in range(2)]
        wd_hi = place("wd_hi", R1 + 32 * K, [P, 2, D], F32R)
        wd_lo = place("wd_lo", R1 + 40 * K, [P, 2, D], F32R)
        silu = [place(f"silu{n}", R1 + 48 * K + 2 * K * n, [P, HALF]) for n in range(2)]
        gu = [place(f"gu{n}", R1 + 52 * K + 2 * K * n, [P, HALF]) for n in range(2)]

        wpg_hi = place("wpg_hi", 0, [P, KT, D], F32R)
        wpg_lo = place("wpg_lo", 32 * K, [P, KT, D], F32R)
        wpp_hi = place("wpp_hi", R1 + 16 * K, [P, 2, D], F32R)
        wpp_lo = place("wpp_lo", R1 + 24 * K, [P, 2, D], F32R)
        pt_hi = [place(f"pt_hi{r}", R1 + 56 * K + 2 * K * r, [P, 2, P], F32R) for r in range(2)]
        pt_lo = [place(f"pt_lo{r}", R1 + 57 * K + 2 * K * r, [P, 2, P], F32R) for r in range(2)]
        p_raw = [place(f"p_raw{r}", R1 + 60 * K + K * r, [P, PLE]) for r in range(2)]
        gain_final = place("gain_final", R1, [P, D])
        pgate = place("pgate", R1 + 4 * K, [P, D])
        x3 = [place(f"x3_{r}", R1 + 32 * K + 4 * K * r, [P, D]) for r in range(2)]
        sq_junk = place("sq_junk", R1 + 40 * K, [P, D])

        banks = ctx.enter_context(nc.psum_tensor("banks", [P, 8, HALF], F32))

        def bank(i, lo=0, hi=HALF):
            return banks[:, i, lo:hi]

        ident_ld = sem("ident_ld")
        consts_in = sem("consts_in")
        dft_in = sem("dft_in")
        dft_hi = sem("dft_hi")
        dft_lo = sem("dft_lo")
        gain_in = sem("gain_in")
        distance_ld = sem("distance_ld")
        raw_in = [sem(f"raw_in{r}") for r in range(2)]
        w_hi = sem("w_hi")
        w_lo = sem("w_lo")
        stage_in = [sem(f"stage_in{r}") for r in range(2)]
        pool_ready = sem("pool_ready")
        lam_dots = sem("lam_dots")
        lam_exped = sem("lam_exped")
        lam_ready = sem("lam_ready")
        n_sq = sem("n_sq")
        n_ms = sem("n_ms")
        n_rstd = sem("n_rstd")
        n_xn = sem("n_xn")
        n_tp = sem("n_tp")
        n_hi = sem("n_hi")
        n_lo = sem("n_lo")
        u_done = sem("u_done")
        u_his = sem("u_his")
        u_los = sem("u_los")
        chan_done = sem("chan_done")
        far_copied = sem("far_copied")
        fold_done = sem("fold_done")
        fold_his = sem("fold_his")
        fold_los = sem("fold_los")
        pos_done = sem("pos_done")
        sin_copied = sem("sin_copied")
        combo_done = sem("combo_done")
        y_quarters = sem("y_quarters")
        y_stored = [sem(f"y_stored{r}") for r in range(2)]
        proj_done = sem("proj_done")
        proj_hi = sem("proj_hi")
        proj_lo = sem("proj_lo")
        vt_done = sem("vt_done")
        v_his = sem("v_his")
        v_los = sem("v_los")
        score_done = sem("score_done")
        biased = sem("biased")
        max_ready = sem("max_ready")
        exped = sem("exped")
        inv_ready = sem("inv_ready")
        inv_step = sem("inv_step")
        scaled = sem("scaled")
        diff_done = sem("diff_done")
        wt_done = sem("wt_done")
        wt_his = sem("wt_his")
        wt_los = sem("wt_los")
        pv_done = sem("pv_done")
        o_squared = sem("o_squared")
        o_copied = sem("o_copied")
        o_ss_done = sem("o_ss_done")
        o_ss_read = sem("o_ss_read")
        o_ms_ready = sem("o_ms_ready")
        o_rstd_ready = sem("o_rstd_ready")
        o_bcast = sem("o_bcast")
        o_done = sem("o_done")
        o_stored = [sem(f"o_stored{r}") for r in range(2)]
        b_his = sem("b_his")
        b_los = sem("b_los")
        gate_done = sem("gate_done")
        branch_done = sem("branch_done")
        sig_done = sem("sig_done")
        gated_done = sem("gated_done")
        merged_done = sem("merged_done")
        m_hi = sem("m_hi")
        m_lo = sem("m_lo")
        wo_done = sem("wo_done")
        x1_done = sem("x1_done")
        g_done = sem("g_done")
        up_done = sem("up_done")
        silu_done = sem("silu_done")
        gu_done = sem("gu_done")
        gu_his = sem("gu_his")
        gu_los = sem("gu_los")
        down_done = sem("down_done")
        down_added = sem("down_added")
        p_in = [sem(f"p_in{r}") for r in range(2)]
        p_tp = sem("p_tp")
        p_his = sem("p_his")
        p_los = sem("p_los")
        pg_done = sem("pg_done")
        pp_done = sem("pp_done")
        pg_sig = sem("pg_sig")
        ple_mul = sem("ple_mul")
        x3_done = sem("x3_done")
        f_sq = sem("f_sq")
        f_ms = sem("f_ms")
        f_rstd_ready = sem("f_rstd_ready")
        y_final = sem("y_final")
        out_stored = [sem(f"out_stored{r}") for r in range(2)]

        block = ctx.enter_context(nc.Block())

        def slab_cols(w, c0):
            return w[:, bass.ds(c0, P)].rearrange("(t p) n -> p t n", p=P)

        def slab_rows(w, r0):
            return w[bass.ds(r0, P), :]

        def one(ap):
            return ap.rearrange("o p n -> (o p) n")

        def one_mid(ap):
            return ap.rearrange("p o a c -> p (o a) c")

        def in_order(i):
            return bank(i, 0, 2 * KW).rearrange("p (k m) -> p m k", k=2)[:, 0:KW - 1, :]

        FILL = {0: (0, range(KT)), 1: (1, range(KT)), 3: (2, range(KT)), 4: (3, range(KT)),
                5: (4, range(KT // 2)), 6: (4, range(KT // 2, KT)), 7: (5, range(KT))}
        FILL_END = {i: g for i, (g, ks) in FILL.items() if ks[-1] == KT - 1}

        @block.sync
        def _(sp):
            def load_slab(turn, slot, src, dst=raw):
                ge(sp, w_hi, 2 * turn + slot - 1)
                ge(sp, w_lo, 2 * turn + slot - 1)
                sp.dma_start(dst[slot][:], src).then_inc(raw_in[slot], 16)

            sp.dma_start(stage[0][:], x_t[0]).then_inc(stage_in[0], 16)
            sp.dma_start(stage[1][:], x_t[1]).then_inc(stage_in[1], 16)
            sp.dma_start(gain[:], g_mix.to_broadcast([P, D])).then_inc(gain_in, 16)
            sp.dma_start(ident[:], ident_in).then_inc(ident_ld, 16)
            load_slab(0, 0, slab_cols(w_in[0], 0))
            load_slab(0, 1, slab_cols(w_in[0], P))
            for t in range(2, TT):
                sp.wait_ge(n_xn, t - 1)
                sp.dma_start(stage[t % 2][:], x_t[t]).then_inc(stage_in[t % 2], 16)
                if t == 3:
                    sp.dma_start(chan_raw[:], chan_dft_in).then_inc(dft_in, 16)
                    sp.dma_start(pos_raw[:], pos_dft_in).then_inc(dft_in, 16)
            sp.dma_start(head_consts[:], head_consts_in).then_inc(consts_in, 16)
            sp.dma_start(sub_gain[:], g_subln.rearrange("a e -> e a"),
                         allow_slow_non_contiguous=True).then_inc(consts_in, 16)
            for r, lam in enumerate((lambda_q1, lambda_k1, lambda_q2, lambda_k2)):
                sp.dma_start(lam_rows[:, r, :], lam.to_broadcast([P, HD])).then_inc(consts_in, 16)
            sp.dma_start(gate_bias[:], b_branch_gate[0].rearrange("(c p) -> p c", p=P),
                         allow_slow_non_contiguous=True).then_inc(consts_in, 16)
            sp.wait_ge(n_xn, TT)
            sp.wait_ge(n_tp, 2 * TT)
            sp.dma_start(gain[:], g_ffn.to_broadcast([P, D])).then_inc(gain_in, 16)
            sp.dma_start(distance[:], distance_in).then_inc(distance_ld, 16)

            with sp.Fori(1, GROUPS // 2) as m:
                for j in range(2):
                    load_slab(m, j, slab_cols(w_in[0], (2 * m + j) * P))

            with sp.Fori(0, PAIRS) as m:
                for s in range(6):
                    j, which = s // 3, s % 3
                    load_slab(3 * m + N_ATTN // 2 + s // 2, s % 2,
                              slab_cols(w_in[0], (2 * m + GROUPS + HEADS * which + j) * P))

            for b, w_b in ((0, w_fourier_out[0]), (1, w_attn_out[0])):
                def pair(d):
                    turn = d + (N_GATE // 2 + KT * b)
                    load_slab(turn, 0, slab_cols(w_branch_gate[0], (KT * b + d) * P))
                    load_slab(turn, 1, slab_cols(w_b, d * P))
                pair(0)
                for r in range(2):
                    if b == 0:
                        sp.wait_ge(y_stored[r], 16 * GROUPS // 2)
                    sp.wait_ge(o_stored[r], 16 * HEADS // 2)
                for t in range(KT):
                    ge(sp, b_his, KT * b + t - 1)
                    ge(sp, b_los, KT * b + t - 1)
                    sp.dma_start(stage[t % 2][:], branch_scr[b][t]).then_inc(stage_in[t % 2], 16)
                with sp.Fori(1, KT) as d:
                    pair(d)

            for k in range(2):
                load_slab(N_OUT // 2, k, slab_rows(w_o[0], k * P), raw_row)
            for t in range(2):
                ge(sp, b_his, 2 * KT)
                ge(sp, b_los, 2 * KT)
                sp.dma_start(stage[t][:], x_t[t]).then_inc(stage_in[t], 16)
            with sp.Fori(1, KT // 2) as m:
                for j in range(2):
                    load_slab(m + N_OUT // 2, j, slab_rows(w_o[0], (2 * m + j) * P), raw_row)
            def ffn_turn(i):
                for e in range(2):
                    load_slab(3 * i + N_FFN // 2 + e, 0, slab_cols(w_ffn_gate[0], (2 * i + e) * P))
                    load_slab(3 * i + N_FFN // 2 + e, 1, slab_cols(w_ffn_up[0], (2 * i + e) * P))
                for e in range(2):
                    load_slab(3 * i + N_FFN // 2 + 2, e, slab_rows(w_ffn_down[0], (2 * i + e) * P), raw_row)
            load_slab(N_FFN // 2, 0, slab_cols(w_ffn_gate[0], 0))
            load_slab(N_FFN // 2, 1, slab_cols(w_ffn_up[0], 0))
            for t in range(2, TT):
                sp.wait_ge(x1_done, 2 * (t - 1))
                sp.dma_start(stage[t % 2][:], x_t[t]).then_inc(stage_in[t % 2], 16)
            load_slab(N_FFN // 2 + 1, 0, slab_cols(w_ffn_gate[0], P))
            load_slab(N_FFN // 2 + 1, 1, slab_cols(w_ffn_up[0], P))
            for e in range(2):
                load_slab(N_FFN // 2 + 2, e, slab_rows(w_ffn_down[0], e * P), raw_row)
            sp.wait_ge(n_xn, 2 * TT)
            sp.dma_start(gain[:], g_ple.to_broadcast([P, D])).then_inc(gain_in, 16)
            with sp.Fori(1, FFN_TURNS) as i:
                ffn_turn(i)

            with sp.Fori(0, KT // 2) as m:
                for j in range(2):
                    load_slab(m + N_PLE // 2, j, slab_rows(w_ple_gate[0], (2 * m + j) * P), raw_row)
            for k in range(2):
                load_slab(N_PLE // 2 + KT // 2, k, slab_rows(w_ple_proj[0], k * P), raw_row)
            sp.wait_ge(down_done, 16 * FFN_TURNS)
            sp.dma_start(gain_final[:], g_final.rearrange("(a d) -> a d", a=1).to_broadcast([P, D]))\
              .then_inc(gain_in, 16)
            for t in range(2):
                sp.dma_start(p_raw[t][:], p_t[t]).then_inc(p_in[t], 16)
            for t in range(TT):
                if t + 2 < TT:
                    sp.wait_ge(p_tp, t + 1)
                    sp.dma_start(p_raw[t % 2][:], p_t[t + 2]).then_inc(p_in[t % 2], 16)
                sp.wait_ge(y_final, t + 1)
                sp.dma_start(out_t[t], stage[t % 2][:]).then_inc(out_stored[t % 2], 16)
            for r in range(2):
                sp.wait_ge(out_stored[r], 16 * TT // 2)

        @block.gpsimd
        def _(pool):
            def split_lo(turn, slot, dst=None):
                pool.wait_ge(w_hi, 2 * turn + slot + 1)
                src = (raw if dst is None else raw_row)[slot][:]
                hi, lo = (st_hi[slot][:], st_lo[slot][:]) if dst is None else dst
                nc.gpsimd.tensor_tensor(lo, src, hi.bitcast(F32), ALU.subtract).then_inc(w_lo, 1)

            def inv_rms(count, means, shifted, outs, summed, shift_ready, done):
                width = means.shape[1]
                pool.wait_ge(summed, count)
                nc.gpsimd.tensor_tensor(shifted, means, eps_col[:, 0:width], ALU.add)\
                    .then_inc(shift_ready, 1)
                pool.wait_ge(shift_ready, count)
                nc.gpsimd.tensor_tensor(outs, shifted, neg_half[:, 0:width], ALU.pow)\
                    .then_inc(done, 1)

            def tile_norm(t, j):
                sl = slice(j, j + 1)
                inv_rms(t + 1, mean_sq[:, sl], shifted[:, sl], rstd[:, sl], n_sq, n_ms, n_rstd)

            nc.gpsimd.memset(neg_half[:], -0.5).then_inc(pool_ready, 1)
            nc.gpsimd.memset(mean_col[:], 1.0 / P).then_inc(pool_ready, 1)
            nc.gpsimd.memset(eps_col[:], EPS).then_inc(pool_ready, 1)
            pool.wait_ge(pool_ready, 3)
            for j in range(2):
                tile_norm(j, j)
                split_lo(0, j)
            with pool.Fori(1, TT // 2) as m:
                for j in range(2):
                    tile_norm(2 * m + j, j)

            def mirror(g2, j):
                g = 2 * g2 + j
                pool.wait_ge(combo_done, 4 * g + 4)
                ge(pool, y_stored[j], 16 * g2)
                (em, om), (ep, op) = combo
                y = y_out[j]
                near, back = slice(0, QUART), slice(QUART, 0, -1)
                quarters = ((em, om, near, ALU.add), (ep, op, back, ALU.subtract),
                            (em, om, near, ALU.subtract), (ep, op, back, ALU.add))
                for q, (a, b, part, op_) in enumerate(quarters):
                    nc.gpsimd.tensor_tensor(y[:, q * QUART:(q + 1) * QUART], a[:, part], b[:, part], op_)\
                        .then_inc(y_quarters, 1)
                pool.wait_ge(y_quarters, 4 * g + 4)
                pool.dma_start(one(branch_scr[0][bass.ds(g, 1)]), y[:]).then_inc(y_stored[j], 16)

            def fourier_pair(g2):
                for j in range(2):
                    split_lo(g2 + 1, j)
                    mirror(g2, j)
            fourier_pair(0)
            with pool.Fori(1, GROUPS // 2) as m:
                fourier_pair(m)

            split_lo(5, 0)
            split_lo(5, 1)

            def sub_norm(count):
                inv_rms(count, o_mean_sq[:], o_shifted[:], o_rstd[:], o_ss_read, o_ms_ready, o_rstd_ready)

            def store_o(h, j):
                pool.wait_ge(o_done, PAIRS * (h + 1))
                pool.dma_start(one(branch_scr[1][bass.ds(h, 1)]), stage[j][:])\
                    .then_inc(o_stored[j], 16)

            def head(h2, j, first=False, last=False):
                h = 2 * h2 + j
                slab = lambda s: (3 * h2 + 6 + (3 * j + s) // 2, (3 * j + s) % 2)
                split_lo(*slab(0))
                if not first:
                    sub_norm(PAIRS * h - 1)
                if not last:
                    split_lo(*slab(1))
                if not first:
                    sub_norm(PAIRS * h)
                    store_o(h - 1, 1 - j)
                sub_norm(PAIRS * h + 1)
                if not last:
                    split_lo(*slab(2))
                sub_norm(PAIRS * h + 2)
            head(0, 0, first=True)
            with pool.Fori(0, 3) as m:
                head(m, 1)
                head(m + 1, 0)
            head(3, 1, last=True)
            sub_norm(PAIRS * HEADS - 1)
            sub_norm(PAIRS * HEADS)
            store_o(HEADS - 1, 1)

            with pool.Fori(1, 2 * KT) as e:
                for s in range(2):
                    split_lo(e + N_GATE // 2, s)

            for k in range(KT):
                split_lo(N_OUT // 2 + k // 2, k % 2, (wo_hi[:, k, :], wo_lo[:, k, :]))
            with pool.Fori(TT // 2, TT) as m:
                for j in range(2):
                    tile_norm(2 * m + j, j)

            with pool.Fori(0, FFN_TURNS) as i:
                for e in range(2):
                    for s in range(2):
                        split_lo(3 * i + N_FFN // 2 + e, s)
                for e in range(2):
                    split_lo(3 * i + N_FFN // 2 + 2, e, (wd_hi[:, e, :], wd_lo[:, e, :]))

            for k in range(KT):
                split_lo(N_PLE // 2 + k // 2, k % 2, (wpg_hi[:, k, :], wpg_lo[:, k, :]))
            for k in range(2):
                split_lo(N_PLE // 2 + KT // 2, k, (wpp_hi[:, k, :], wpp_lo[:, k, :]))

            def final_norm(t, j):
                sl = slice(j, j + 1)
                inv_rms(t + 1, f_mean_sq[:, sl], f_shifted[:, sl], f_rstd[:, sl], f_sq, f_ms, f_rstd_ready)
            tile_norm(2 * TT, 0)
            tile_norm(2 * TT + 1, 1)
            final_norm(0, 0)
            with pool.Fori(0, TT // 2 - 1) as m:
                tile_norm(2 * m + 2 * TT + 2, 0)
                final_norm(2 * m + 1, 1)
                tile_norm(2 * m + 2 * TT + 3, 1)
                final_norm(2 * m + 2, 0)
            final_norm(TT - 1, 1)

        @block.scalar
        def _(act):
            def split_hi(turn, slot, free=None, dst=None):
                act.wait_ge(raw_in[slot], 16 * (turn + 1))
                if free is not None:
                    ge(act, *free)
                if dst is None:
                    nc.scalar.copy(st_hi[slot][:], raw[slot][:]).then_inc(w_hi, 1)
                else:
                    nc.scalar.copy(dst, raw_row[slot][:]).then_inc(w_hi, 1)

            def square(src, junk, mean, done):
                nc.scalar.activation(junk, src, ACT.Square, scale=D ** -0.5, accum_out=mean)\
                    .then_inc(done, 1)

            def split_wait():
                act.nop(nofuse=True)

            def transposed_hi(t, dst, bank0):
                for n in range(2):
                    act.wait_ge(n_tp, 2 * t + n + 1)
                    nc.scalar.copy(dst(4 * n), bank(bank0 + n).rearrange("p (f c) -> p f c", f=4))\
                        .then_inc(n_hi, 1)

            def h_cols(t):
                return lambda f: h_hi[:, f:f + 4, bass.ds(t * P, P)]

            def norm_square(m, j):
                t = 2 * m + j
                act.wait_ge(stage_in[j], 16 * (m + 1))
                ge(act, n_tp, 4 * m + 2 * j - 2)
                square(stage[j][:], xn[j][:], mean_sq[:, j:j + 1], n_sq)
            norm_square(0, 0)
            split_hi(0, 0)
            norm_square(0, 1)
            split_hi(0, 1)
            transposed_hi(0, h_cols(0), 0)
            with act.Fori(1, TT // 2) as m:
                norm_square(m, 0)
                transposed_hi(2 * m - 1, h_cols(2 * m - 1), 2)
                norm_square(m, 1)
                transposed_hi(2 * m, h_cols(2 * m), 0)
            transposed_hi(TT - 1, h_cols(TT - 1), 2)
            act.wait_ge(dft_in, 32)
            nc.scalar.copy(chan_hi[:], chan_raw[:]).then_inc(dft_hi, 1)
            nc.scalar.copy(pos_hi[:], pos_raw[:]).then_inc(dft_hi, 1)
            act.wait_ge(lam_dots, 2)
            nc.scalar.activation(lam_exp[:], lam_dot[:], ACT.Exp).then_inc(lam_exped, 1)

            def u_evac(g, j, n):
                act.wait_ge(u_done, 2 * g + n + 1)
                nc.scalar.copy(u_hi[j][:, n * HALF:(n + 1) * HALF], bank(n)).then_inc(u_his, 1)

            def fold_split(g, c):
                act.wait_ge(fold_done, 4 * g + c + 1)
                ge(act, pos_done, 2 * g)
                nc.scalar.copy(fold_hi[:, :, c, :], folded[c % 2][:]).then_inc(fold_his, 1)

            def fourier_group(g2, j, last=False):
                g = 2 * g2 + j
                split_hi(g2 + 1, j, (u_done, 2 * g + 2))
                if not last:
                    u_evac(g + 1, 1 - j, 0)
                for c in range(4):
                    act.wait_ge(chan_done, 4 * g + c + 1)
                    ge(act, fold_done, 4 * g + c - 1)
                    nc.scalar.copy(far_half[c % 2][:], bank(2 + c % 2, 256, 512)).then_inc(far_copied, 1)
                    if c >= 1:
                        fold_split(g, c - 1)
                fold_split(g, 3)
                if not last:
                    u_evac(g + 1, 1 - j, 1)
                for par in range(2):
                    act.wait_ge(pos_done, 2 * g + par + 1)
                    ge(act, combo_done, 4 * g)
                    nc.scalar.copy(sin_part[par][:].rearrange("p (m k) -> p m k", k=2),
                                   in_order(5 + 2 * par)).then_inc(sin_copied, 1)

            u_evac(0, 0, 0)
            u_evac(0, 0, 1)
            fourier_group(0, 0)
            with act.Fori(0, 3) as m:
                fourier_group(m, 1)
                fourier_group(m + 1, 0)
            fourier_group(3, 1, last=True)

            def proj_evac(h, j, g, src):
                which, n = g // 2, g % 2
                act.wait_ge(proj_done, 6 * h + g + 1)
                dst = ((q_hi[j], k_hi[j], v_t)[which])[:, n * HALF:(n + 1) * HALF]
                if which == 0:
                    split_wait()
                    nc.scalar.activation(dst, src, ACT.Copy, scale=qscale[:, bass.ds(h, 1)])\
                        .then_inc(proj_hi, 1)
                else:
                    nc.scalar.copy(dst, src).then_inc(proj_hi, 1)

            def wt_evac(s, i):
                pair = (i // 2) % 2
                for n in range(2):
                    act.wait_ge(wt_done, 2 * s + n + 1)
                    nc.scalar.copy(wt_hi[pair][:, 4 * n:4 * n + 4, (i % 2) * P:(i % 2 + 1) * P],
                                   bank(4 + n).rearrange("p (f c) -> p f c", f=4)).then_inc(wt_his, 1)

            def out_square(pair_no):
                act.wait_ge(pv_done, pair_no + 1)
                ge(act, o_ss_done, pair_no)
                nc.scalar.activation(o_sq[:], bank(7, 0, 2 * P), ACT.Square).then_inc(o_squared, 1)

            def head(h2, j, first=False, last=False):
                h = 2 * h2 + j
                slab = lambda r: (3 * h2 + 6 + (3 * j + r) // 2, (3 * j + r) % 2)
                for i in range(TT):
                    s = TT * h + i
                    pr = probs[i % 2]
                    if i == 0:
                        split_hi(*slab(0), (proj_done, 6 * h + 6))
                    if i == 2 and not last:
                        split_hi(*slab(1), (proj_done, 6 * h + 8))
                    if i == 5 and not last:
                        split_hi(*slab(2), (proj_done, 6 * h + 10))
                    for c in range(2):
                        col = slice(2 * (i % 2) + c, 2 * (i % 2) + c + 1)
                        act.wait_ge(max_ready, 2 * s + c + 1)
                        ge(act, inv_ready, 2 * s + c - 3)
                        split_wait()
                        nc.scalar.activation(pr[c][:], pr[c][:], ACT.Exp, bias=neg_max[:, col],
                                             scale=slope[:, bass.ds(h, 1)], accum_out=exp_sum[:, col])\
                            .then_inc(exped, 1)
                    act.wait_ge(inv_ready, 2 * s + 1)
                    nc.scalar.activation(pr[0][:], pr[0][:], ACT.Copy,
                                         scale=inv_sum[:, 2 * (i % 2):2 * (i % 2) + 1]).then_inc(scaled, 1)
                    if i == 2:
                        for k in range(2):
                            act.wait_ge(vt_done, 2 * h + k + 1)
                            nc.scalar.copy(v_hi[:, 4 * k:4 * k + 4, :],
                                           bank(6).rearrange("p (f c) -> p f c", f=4)).then_inc(v_his, 1)
                    if not last and i in FILL_END:
                        proj_evac(h + 1, 1 - j, FILL_END[i], bank(6))
                    if not (first and i == 0):
                        wt_evac(s - 1, (i - 1) % TT)
                    if i % 2 == 1 and not (first and i == 1):
                        out_square(PAIRS * h + (i - 3) // 2)

            for r in range(2):
                act.wait_ge(y_stored[r], 16 * GROUPS // 2)
            for g in range(6):
                proj_evac(0, 0, g, bank(6 + g % 2))
                if g == 1:
                    split_hi(5, 0, (proj_done, 2))
                if g == 3:
                    split_hi(5, 1, (proj_done, 4))
            head(0, 0, first=True)
            with act.Fori(0, 3) as m:
                head(m, 1)
                head(m + 1, 0)
            head(3, 1, last=True)
            wt_evac(TT * HEADS - 1, TT - 1)
            out_square(PAIRS * HEADS - 1)

            def branch_split(b):
                act.wait_ge(branch_done, 2 * KT * b)if b else \
                    act.wait_ge(pv_done, PAIRS * HEADS)
                for t in range(KT):
                    act.wait_ge(stage_in[t % 2], 16 * (KT // 2 * (b + 1) + t // 2 + 1))
                    nc.scalar.copy(b_hi[:, t, :], stage[t % 2][:]).then_inc(b_his, 1)

            def gate_tile(e2, j, last=False):
                e = 2 * e2 + j
                for n in range(2):
                    act.wait_ge(gate_done, 2 * e + n + 1)
                    ge(act, gated_done, 2 * e + n - 1)
                    split_wait()
                    nc.scalar.activation(sig[n][:], bank(4 * j + n), ACT.Sigmoid,
                                         bias=gate_bias[:, bass.ds(e, 1)]).then_inc(sig_done, 1)
                if not last:
                    split_hi(e + N_GATE // 2 + 1, 0)
                    split_hi(e + N_GATE // 2 + 1, 1, (branch_done, 2 * e + 2))

            branch_split(0)
            for j in range(2):
                gate_tile(0, j)
            with act.Fori(1, KT // 2) as m:
                for j in range(2):
                    gate_tile(m, j)
            branch_split(1)
            with act.Fori(KT // 2, KT - 1) as m:
                for j in range(2):
                    gate_tile(m, j)
            gate_tile(KT - 1, 0)
            gate_tile(KT - 1, 1, last=True)

            act.wait_ge(branch_done, 4 * KT)
            for k in range(KT):
                split_hi(N_OUT // 2 + k // 2, k % 2, dst=wo_hi[:, k, :])

            def merged_hi(t, j, free):
                ge(act, *free)
                nc.scalar.copy(st_hi[j][:], one_mid(merged[:, bass.ds(t, 1), :, :])).then_inc(m_hi, 1)

            def out_tile(m, j, more=True):
                t = 2 * m + j
                act.wait_ge(x1_done, 2 * t + 2)
                ge(act, n_tp, 2 * t + 2 * TT - 2)
                split_wait()
                square(resid[:, bass.ds(t, 1), :].rearrange("p o n -> p (o n)"), xn[j][:],
                       mean_sq[:, j:j + 1], n_sq)
                if more:
                    merged_hi(t + 2, j, (wo_done, 2 * t + 2))
                transposed_hi(t + TT, h_cols(t), 4 + 2 * j)

            act.wait_ge(merged_done, 2 * KT)
            merged_hi(0, 0, (gate_done, 4 * KT))
            merged_hi(1, 1, (branch_done, 4 * KT))
            with act.Fori(0, TT // 2 - 1) as m:
                for j in range(2):
                    out_tile(m, j)
            out_tile(TT // 2 - 1, 0, more=False)
            split_hi(N_FFN // 2, 0, (wo_done, 2 * TT - 2))
            out_tile(TT // 2 - 1, 1, more=False)
            split_hi(N_FFN // 2, 1, (wo_done, 2 * TT))

            def ffn_turn(i, parity, last=False):
                turn = 3 * i + N_FFN // 2
                for e in range(2):
                    f = 2 * i + e
                    for n in range(2):
                        act.wait_ge(g_done, 2 * f + n + 1)
                        ge(act, gu_done, 2 * f + n - 1)
                        nc.scalar.activation(silu[n][:], bank(n), ACT.Silu).then_inc(silu_done, 1)
                    if e == 0:
                        split_hi(turn + 1, 0)
                    for n in range(2):
                        act.wait_ge(gu_done, 2 * f + n + 1)
                        nc.scalar.copy(gu_hi[parity][:, e, n * HALF:(n + 1) * HALF], gu[n][:])\
                            .then_inc(gu_his, 1)
                    if e == 0:
                        split_hi(turn + 1, 1)
                for e in range(2):
                    split_hi(turn + 2, e, (down_done, 2 * TT * i), wd_hi[:, e, :])
                if not last:
                    for s in range(2):
                        split_hi(turn + 3, s)

            ffn_turn(0, 0)
            with act.Fori(0, FFN_TURNS // 2 - 1) as m:
                ffn_turn(2 * m + 1, 1)
                ffn_turn(2 * m + 2, 0)
            ffn_turn(FFN_TURNS - 2, 1)
            ffn_turn(FFN_TURNS - 1, 0, last=True)

            for k in range(KT):
                split_hi(N_PLE // 2 + k // 2, k % 2, (up_done, 2 * FT), wpg_hi[:, k, :])
            for k in range(2):
                split_hi(N_PLE // 2 + KT // 2, k, (down_done, 2 * TT * (FFN_TURNS - 1)), wpp_hi[:, k, :])

            def ple_square(t, j):
                act.wait_ge(down_added, 2 * TT * (FFN_TURNS - 1) + 2 * t + 2)
                ge(act, n_tp, 2 * t + 4 * TT - 2)
                split_wait()
                square(resid[:, bass.ds(t, 1), :].rearrange("p o n -> p (o n)"), xn[j][:],
                       mean_sq[:, j:j + 1], n_sq)

            def ple_hi(t, j):
                transposed_hi(t + 2 * TT, lambda f: st_hi[j][:, f:f + 4, :], 6)
                act.wait_ge(p_tp, t + 1)
                nc.scalar.copy(pt_hi[j][:], bank(6, 0, PLE).rearrange("p (k c) -> p k c", k=2))\
                    .then_inc(p_his, 1)

            def ple_tile(m, j, more=True):
                t = 2 * m + j
                if more:
                    ple_square(t + 1, 1 - j)
                for n in range(2):
                    act.wait_ge(pg_done, 2 * t + n + 1)
                    ge(act, x3_done, t)
                    nc.scalar.activation(pgate[:, n * HALF:(n + 1) * HALF], bank(2 * j + n),
                                         ACT.Sigmoid).then_inc(pg_sig, 1)
                if more:
                    ple_hi(t + 1, 1 - j)
                act.wait_ge(x3_done, t + 1)
                ge(act, f_rstd_ready, t)
                square(x3[j][:], sq_junk[:], f_mean_sq[:, j:j + 1], f_sq)

            ple_square(0, 0)
            ple_hi(0, 0)
            ple_tile(0, 0)
            ple_tile(0, 1)
            ple_tile(1, 0)
            with act.Fori(1, TT // 2 - 1) as m:
                ple_tile(m, 1)
                ple_tile(m + 1, 0)
            ple_tile(TT // 2 - 1, 1, more=False)

        @block.vector
        def _(dve):
            sub = ALU.subtract

            def lo(dst, src, hi, done):
                nc.vector.tensor_tensor(dst, src, hi.bitcast(F32), sub).then_inc(done, 1)

            def normed(t, j, src, gains):
                dve.wait_ge(n_rstd, t + 1)
                dve.wait_ge(gain_in, 16 * gains)
                nc.vector.scalar_tensor_tensor(xn[j][:], src, rstd[:, j:j + 1], gain[:],
                                               ALU.mult, ALU.mult).then_inc(n_xn, 1)

            def transposed_lo(t, dst_lo, dst_hi, bank0):
                for n in range(2):
                    dve.wait_ge(n_hi, 2 * t + n + 1)
                    lo(dst_lo(4 * n), bank(bank0 + n).rearrange("p (f c) -> p f c", f=4),
                       dst_hi(4 * n), n_lo)

            def h_cols(buf, t):
                return lambda f: buf[:, f:f + 4, bass.ds(t * P, P)]

            def tile_of(buf, t):
                return buf[:, bass.ds(t, 1), :].rearrange("p o n -> p (o n)")

            normed(0, 0, stage[0][:], 1)
            normed(1, 1, stage[1][:], 1)
            transposed_lo(0, h_cols(h_lo, 0), h_cols(h_hi, 0), 0)
            with dve.Fori(1, TT // 2) as m:
                normed(2 * m, 0, stage[0][:], 1)
                transposed_lo(2 * m - 1, h_cols(h_lo, 2 * m - 1), h_cols(h_hi, 2 * m - 1), 2)
                normed(2 * m + 1, 1, stage[1][:], 1)
                transposed_lo(2 * m, h_cols(h_lo, 2 * m), h_cols(h_hi, 2 * m), 0)
            transposed_lo(TT - 1, h_cols(h_lo, TT - 1), h_cols(h_hi, TT - 1), 2)
            dve.wait_ge(dft_hi, 2)
            lo(chan_lo[:], chan_raw[:], chan_hi[:], dft_lo)
            lo(pos_lo[:], pos_raw[:], pos_hi[:], dft_lo)

            dve.wait_ge(consts_in, 16 * 7)
            for r in range(2):
                nc.vector.tensor_tensor_reduce(lam_rows[:, 2 * r, :], lam_rows[:, 2 * r, :],
                                               lam_rows[:, 2 * r + 1, :], 1.0, 0.0, ALU.mult, ALU.add,
                                               lam_dot[:, r:r + 1]).then_inc(lam_dots, 1)
            dve.wait_ge(lam_exped, 1)
            nc.vector.scalar_tensor_tensor(neg_lam[:], lam_exp[:, 1:2], -LAMBDA_INIT, lam_exp[:, 0:1],
                                           ALU.add, sub).then_inc(lam_ready, 1)
            nc.vector.tensor_scalar(sub_gain[:], sub_gain[:], 1.0 - LAMBDA_INIT, None, ALU.mult)\
                .then_inc(lam_ready, 1)

            def u_split(g, j, n):
                dve.wait_ge(u_his, 2 * g + n + 1)
                half = slice(n * HALF, (n + 1) * HALF)
                lo(u_lo[j][:, half], bank(n), u_hi[j][:, half], u_los)

            def fold_split(g, c):
                dve.wait_ge(fold_his, 4 * g + c + 1)
                lo(fold_lo[:, :, c, :], folded[c % 2][:], fold_hi[:, :, c, :], fold_los)

            def fourier_group(g2, j, last=False):
                g = 2 * g2 + j
                if not last:
                    u_split(g + 1, 1 - j, 0)
                for c in range(4):
                    dve.wait_ge(far_copied, 4 * g + c + 1)
                    ge(dve, fold_los, 4 * g + c - 1)
                    near = bank(2 + c % 2, 0, 256)
                    nc.vector.tensor_tensor(folded[c % 2][:, 0, :], near, far_half[c % 2][:], ALU.add)
                    nc.vector.tensor_tensor(folded[c % 2][:, 1, :], near, far_half[c % 2][:], sub)\
                        .then_inc(fold_done, 1)
                    if c >= 1:
                        fold_split(g, c - 1)
                fold_split(g, 3)
                if not last:
                    u_split(g + 1, 1 - j, 1)
                for par in range(2):
                    dve.wait_ge(sin_copied, 2 * g + par + 1)
                    ge(dve, y_quarters, 4 * g)
                    for a, op in enumerate((sub, ALU.add)):
                        nc.vector.tensor_tensor(combo[a][par][:].rearrange("p (m k) -> p m k", k=2),
                                                in_order(4 + 2 * par),
                                                sin_part[par][:].rearrange("p (m k) -> p m k", k=2), op)\
                            .then_inc(combo_done, 1)

            u_split(0, 0, 0)
            u_split(0, 0, 1)
            fourier_group(0, 0)
            with dve.Fori(0, 3) as m:
                fourier_group(m, 1)
                fourier_group(m + 1, 0)
            fourier_group(3, 1, last=True)

            def proj_split(h, j, g, src):
                which, n = g // 2, g % 2
                half = slice(n * HALF, (n + 1) * HALF)
                dve.wait_ge(proj_hi, 6 * h + g + 1)
                if which == 0:
                    nc.vector.scalar_tensor_tensor(q_lo[j][:, half], src, qscale[:, bass.ds(h, 1)],
                                                   q_hi[j][:, half].bitcast(F32), ALU.mult, sub)\
                        .then_inc(proj_lo, 1)
                else:
                    lo(k_lo[j][:, half], src, k_hi[j][:, half], proj_lo)

            def wt_split(s, i):
                pair = (i // 2) % 2
                for n in range(2):
                    dve.wait_ge(wt_his, 2 * s + n + 1)
                    part = (slice(None), slice(4 * n, 4 * n + 4), slice((i % 2) * P, (i % 2 + 1) * P))
                    lo(wt_lo[pair][part], bank(4 + n).rearrange("p (f c) -> p f c", f=4),
                       wt_hi[pair][part], wt_los)

            def out_copy(pair_no):
                dve.wait_ge(pv_done, pair_no + 1)
                dve.wait_ge(o_squared, pair_no + 1)
                nc.vector.tensor_scalar(o_raw[:], bank(7, 0, 2 * P), sub_gain[:], None, ALU.mult)\
                    .then_inc(o_copied, 1)

            def sums_read(pair_no):
                dve.wait_ge(o_ss_done, pair_no + 1)
                nc.vector.tensor_copy(o_mean_sq[:], bank(7, 2 * P, 2 * P + 2)).then_inc(o_ss_read, 1)

            def out_norm(pair_no, slot, p, stored):
                dve.wait_ge(o_bcast, pair_no + 1)
                if p == 0:
                    ge(dve, o_stored[slot], stored)
                nc.vector.tensor_tensor(stage[slot][:, 2 * P * p:2 * P * (p + 1)], o_raw[:],
                                        bank(7, 2 * P, 4 * P), ALU.mult).then_inc(o_done, 1)

            def head(h2, j, first=False, last=False):
                h = 2 * h2 + j
                for i in range(TT):
                    s = TT * h + i
                    pr = probs[i % 2]
                    start = ALIBI_0 - P * i
                    for c in range(2):
                        col = slice(2 * (i % 2) + c, 2 * (i % 2) + c + 1)
                        dve.wait_ge(score_done, 2 * s + c + 1)
                        ge(dve, wt_done, 2 * s - 2)
                        dve.nop(nofuse=True)
                        nc.vector.tensor_tensor_reduce(
                            pr[c][:], banks[:, 2 * c:2 * c + 2, :].rearrange("p b n -> p (b n)"),
                            distance[:, start:start + SEQ], 1.0, -3.0e38, ALU.add, ALU.max,
                            row_max[:, c:c + 1]).then_inc(biased, 1)
                        dve.wait_ge(biased, 2 * s + c + 1)
                        nc.vector.tensor_tensor(neg_max[:, col], row_max[:, c:c + 1],
                                                neg_slope[:, bass.ds(h, 1)], ALU.mult)\
                            .then_inc(max_ready, 1)
                    pair_even = PAIRS * h + (i - 4) // 2
                    if i % 2 == 0 and not (first and i < 4):
                        sums_read(pair_even)
                    dve.wait_ge(exped, 2 * s + 1)
                    col = 2 * (i % 2)
                    nc.vector.reciprocal(inv_sum[:, col:col + 1], exp_sum[:, col:col + 1])\
                        .then_inc(inv_ready, 1)
                    dve.wait_ge(exped, 2 * s + 2)
                    nc.vector.reciprocal(inv_raw[:], exp_sum[:, col + 1:col + 2]).then_inc(inv_step, 1)
                    dve.wait_ge(inv_step, s + 1)
                    nc.vector.tensor_tensor(inv_sum[:, col + 1:col + 2], neg_lam[:], inv_raw[:],
                                            ALU.mult).then_inc(inv_ready, 1)
                    dve.wait_ge(inv_ready, 2 * s + 2)
                    dve.wait_ge(scaled, s + 1)
                    nc.vector.scalar_tensor_tensor(pr[0][:], pr[1][:], inv_sum[:, col + 1:col + 2],
                                                   pr[0][:], ALU.mult, ALU.add).then_inc(diff_done, 1)
                    if i == 2:
                        for k in range(2):
                            dve.wait_ge(v_his, 2 * h + k + 1)
                            lo(v_lo[:, 4 * k:4 * k + 4, :], bank(6).rearrange("p (f c) -> p f c", f=4),
                               v_hi[:, 4 * k:4 * k + 4, :], v_los)
                    if not last and FILL_END.get(i, 4) < 4:
                        proj_split(h + 1, 1 - j, FILL_END[i], bank(6))
                    if not (first and i == 0):
                        wt_split(s - 1, (i - 1) % TT)
                    if i % 2 == 1 and not (first and i == 1):
                        out_copy(PAIRS * h + (i - 3) // 2)
                    if i % 2 == 0 and not (first and i < 4):
                        if i < 4:
                            out_norm(pair_even, 1 - j, 2 + i // 2, 0)
                        else:
                            out_norm(pair_even, j, i // 2 - 2, 16 * h2)

            for r in range(2):
                dve.wait_ge(y_stored[r], 16 * GROUPS // 2)
            dve.wait_ge(distance_ld, 16)
            for g in range(4):
                proj_split(0, 0, g, bank(6 + g % 2))
            dve.wait_ge(lam_ready, 2)
            head(0, 0, first=True)
            with dve.Fori(0, 3) as m:
                head(m, 1)
                head(m + 1, 0)
            head(3, 1, last=True)
            last_pair = PAIRS * HEADS - 1
            wt_split(TT * HEADS - 1, TT - 1)
            sums_read(last_pair - 1)
            out_norm(last_pair - 1, 1, 2, 0)
            out_copy(last_pair)
            sums_read(last_pair)
            out_norm(last_pair, 1, 3, 0)

            def branch_split(b):
                for t in range(KT):
                    dve.wait_ge(b_his, KT * b + t + 1)
                    lo(b_lo[:, t, :], stage[t % 2][:], b_hi[:, t, :], b_los)

            def gate_tile(b, e2, j, d):
                e = 2 * e2 + j
                for n in range(2):
                    dst = merged[:, 4 * n:4 * n + 4, bass.ds(d, 1), :].rearrange("p t o c -> p t (o c)")
                    dve.wait_ge(sig_done, 2 * e + n + 1)
                    dve.wait_ge(branch_done, 2 * e + n + 1)
                    src = bank(4 * j + 2 + n)
                    if b == 0:
                        nc.vector.tensor_tensor(dst, src.rearrange("p (t c) -> p t c", c=P),
                                                sig[n][:].rearrange("p (t c) -> p t c", c=P), ALU.mult)\
                            .then_inc(gated_done, 1)
                    else:
                        nc.vector.tensor_tensor(gated[n][:], src, sig[n][:], ALU.mult)\
                            .then_inc(gated_done, 1)
                        dve.wait_ge(gated_done, 2 * e + n + 1)
                        nc.vector.tensor_tensor(dst, dst, gated[n][:].rearrange("p (t c) -> p t c", c=P),
                                                ALU.add).then_inc(merged_done, 1)
                        dve.wait_ge(merged_done, 2 * d + n + 1)

            for b in range(2):
                branch_split(b)
                with dve.Fori(0, KT // 2) as m:
                    for j in range(2):
                        gate_tile(b, m + KT // 2 * b, j, 2 * m + j)

            def merged_lo(t, j):
                dve.wait_ge(m_hi, t + 1)
                lo(st_lo[j][:], one_mid(merged[:, bass.ds(t, 1), :, :]), st_hi[j][:], m_lo)

            def out_tile(m, j, more=True):
                t = 2 * m + j
                for n in range(2):
                    half = slice(n * HALF, (n + 1) * HALF)
                    dve.wait_ge(wo_done, 2 * t + n + 1)
                    dve.wait_ge(stage_in[j], 16 * (m + 3 * TT // 2 + 1))
                    nc.vector.tensor_tensor(resid[:, bass.ds(t, 1), half].rearrange("p o n -> p (o n)"),
                                            bank(2 * j + n), stage[j][:, half], ALU.add)\
                        .then_inc(x1_done, 1)
                if more:
                    merged_lo(t + 2, j)
                normed(t + TT, j, tile_of(resid, t), 2)
                transposed_lo(t + TT, h_cols(h_lo, t), h_cols(h_hi, t), 4 + 2 * j)

            dve.wait_ge(merged_done, 2 * KT)
            merged_lo(0, 0)
            merged_lo(1, 1)
            with dve.Fori(0, TT // 2 - 1) as m:
                for j in range(2):
                    out_tile(m, j)
            for j in range(2):
                out_tile(TT // 2 - 1, j, more=False)

            def hidden(i, e, parity):
                f = 2 * i + e
                for n in range(2):
                    dve.wait_ge(silu_done, 2 * f + n + 1)
                    dve.wait_ge(up_done, 2 * f + n + 1)
                    ge(dve, gu_his, 2 * f + n - 1)
                    ge(dve, gu_los, 2 * f + n - 1)
                    nc.vector.tensor_tensor(gu[n][:], bank(2 + n), silu[n][:], ALU.mult)\
                        .then_inc(gu_done, 1)
                for n in range(2):
                    half = slice(n * HALF, (n + 1) * HALF)
                    dve.wait_ge(gu_his, 2 * f + n + 1)
                    lo(gu_lo[parity][:, e, half], gu[n][:], gu_hi[parity][:, e, half], gu_los)

            def down_add(i):
                for t in range(TT):
                    for n in range(2):
                        dst = resid[:, t, n * HALF:(n + 1) * HALF]
                        dve.wait_ge(down_done, 2 * TT * i + 2 * t + n + 1)
                        nc.vector.tensor_tensor(dst, bank(4 + (2 * t + n) % 4), dst, ALU.add)\
                            .then_inc(down_added, 1)

            def ffn_turn(i, parity):
                hidden(i, 0, parity)
                down_add(i - 1)
                hidden(i, 1, parity)
            hidden(0, 0, 0)
            hidden(0, 1, 0)
            with dve.Fori(0, FFN_TURNS // 2) as m:
                ffn_turn(2 * m + 1, 1)
                ffn_turn(2 * m + 2, 0)
            down_add(FFN_TURNS - 1)

            def ple_lo(t, j):
                transposed_lo(t + 2 * TT, lambda f: st_lo[j][:, f:f + 4, :],
                              lambda f: st_hi[j][:, f:f + 4, :], 6)
                dve.wait_ge(p_his, t + 1)
                lo(pt_lo[j][:], bank(6, 0, PLE).rearrange("p (k c) -> p k c", k=2), pt_hi[j][:], p_los)

            def ple_tile(m, j, more=True):
                t = 2 * m + j
                if more:
                    normed(t + 1 + 2 * TT, 1 - j, tile_of(resid, t + 1), 3)
                    ple_lo(t + 1, 1 - j)
                for n in range(2):
                    half = slice(n * HALF, (n + 1) * HALF)
                    dve.wait_ge(pg_sig, 2 * t + n + 1)
                    dve.wait_ge(pp_done, 2 * t + n + 1)
                    nc.vector.tensor_tensor(pgate[:, half], bank(4 + n), pgate[:, half], ALU.mult)\
                        .then_inc(ple_mul, 1)
                dve.wait_ge(ple_mul, 2 * t + 2)
                ge(dve, y_final, t - 1)
                nc.vector.tensor_tensor(x3[j][:], tile_of(resid, t), pgate[:], ALU.add)\
                    .then_inc(x3_done, 1)
                dve.wait_ge(f_rstd_ready, t + 1)
                dve.wait_ge(gain_in, 16 * 4)
                ge(dve, out_stored[j], 16 * m)
                nc.vector.scalar_tensor_tensor(stage[j][:], x3[j][:], f_rstd[:, j:j + 1], gain_final[:],
                                               ALU.mult, ALU.mult).then_inc(y_final, 1)

            normed(2 * TT, 0, tile_of(resid, 0), 3)
            ple_lo(0, 0)
            ple_tile(0, 0)
            ple_tile(0, 1)
            ple_tile(1, 0)
            with dve.Fori(1, TT // 2 - 1) as m:
                ple_tile(m, 1)
                ple_tile(m + 1, 0)
            ple_tile(TT // 2 - 1, 1, more=False)

        @block.tensor
        def _(pe):
            def passes(out_ap, a_hi, a_lo, b_hi_, b_lo_, first, last):
                terms = ((a_hi, b_hi_), (a_hi, b_lo_), (a_lo, b_hi_))
                for q, (a, b) in enumerate(terms):
                    ins = nc.tensor.matmul(out_ap, a, b, start=first and q == 0, stop=last and q == 2)
                return ins

            def weights(n):
                pe.wait_ge(w_hi, n + 1)
                pe.wait_ge(w_lo, n + 1)

            def slab_product(out_ap, slot, n, ks=range(KT)):
                half = slice(n * HALF, (n + 1) * HALF)
                for k in ks:
                    ins = passes(out_ap, st_hi[slot][:, k, :], st_lo[slot][:, k, :],
                                 h_hi[:, k, half], h_lo[:, k, half], k == 0, k == KT - 1)
                return ins

            def norm_transpose(t, j, bank0):
                pe.wait_ge(n_xn, t + 1)
                for n in range(2):
                    for f in range(4):
                        ins = nc.tensor.transpose(bank(bank0 + n, f * P, (f + 1) * P),
                                                  xn[j][:, (4 * n + f) * P:(4 * n + f + 1) * P], ident[:])
                    ins.then_inc(n_tp, 1)

            pe.wait_ge(ident_ld, 16)
            for j in range(2):
                norm_transpose(j, j, 2 * j)
            with pe.Fori(1, TT // 2) as m:
                for j in range(2):
                    pe.wait_ge(n_lo, 4 * m + 2 * j - 2)
                    norm_transpose(2 * m + j, j, 2 * j)

            def project_u(g, j, n):
                weights(g)
                ge(pe, u_los, 2 * g + n - 1)
                slab_product(bank(n), j, n).then_inc(u_done, 1)

            def channel_dft(g, j):
                pe.wait_ge(u_los, 2 * g + 2)
                for c in range(4):
                    par, tile = c // 2, c % 2
                    ge(pe, fold_done, 4 * g + c - 1)
                    for far in range(2):
                        at = 2 * P * (tile + 2 * far) + par
                        tok = slice(at, at + 2 * P - 1, 2)
                        ins = passes(bank(2 + c % 2, 256 * far, 256 * far + 256),
                                     u_hi[j][:, tok], u_lo[j][:, tok], chan_hi[:], chan_lo[:],
                                     True, True)
                    ins.then_inc(chan_done, 1)

            def position_dft(g):
                pe.wait_ge(fold_los, 4 * g + 4)
                ge(pe, combo_done, 4 * g)
                for par in range(2):
                    for trig in range(2):
                        for k_odd in range(2):
                            for tile in range(2):
                                c = 2 * par + tile
                                chans = slice(P * trig, P * (trig + 1))
                                tab = 4 * c + 2 * k_odd + trig
                                ins = passes(bank(4 + 2 * par + trig, KW * k_odd, KW * (k_odd + 1)),
                                             fold_hi[:, k_odd, c, chans], fold_lo[:, k_odd, c, chans],
                                             pos_hi[:, tab, :], pos_lo[:, tab, :],
                                             tile == 0, tile == 1)
                    ins.then_inc(pos_done, 1)

            for n in range(2):
                pe.wait_ge(n_lo, 2 * TT)
                project_u(0, 0, n)
            pe.wait_ge(dft_lo, 2)

            def fourier_group(g2, j, last=False):
                g = 2 * g2 + j
                if not last:
                    project_u(g + 1, 1 - j, 0)
                channel_dft(g, j)
                if not last:
                    project_u(g + 1, 1 - j, 1)
                position_dft(g)
            fourier_group(0, 0)
            with pe.Fori(0, 3) as m:
                fourier_group(m, 1)
                fourier_group(m + 1, 0)
            fourier_group(3, 1, last=True)

            def project(h, n_slab, slot, g, out_bank, ks=range(KT)):
                if ks[0] == 0:
                    weights(n_slab)
                ins = slab_product(bank(out_bank), slot, g % 2, ks)
                if ks[-1] == KT - 1:
                    ins.then_inc(proj_done, 1)

            def scores(s, j, i):
                for c in range(2):
                    rows = slice(HD * c, HD * (c + 1))
                    tok = slice(i * P, (i + 1) * P)
                    ge(pe, biased, 2 * s + c - 1)
                    for n in range(2):
                        half = slice(n * HALF, (n + 1) * HALF)
                        ins = passes(bank(2 * c + n), q_hi[j][rows, tok], q_lo[j][rows, tok],
                                     k_hi[j][rows, half], k_lo[j][rows, half], True, True)
                    ins.then_inc(score_done, 1)

            def transpose_diff(s, i):
                pe.wait_ge(diff_done, s + 1)
                for n in range(2):
                    ge(pe, wt_los, 2 * s + n - 1)
                    for f in range(4):
                        kt = 4 * n + f
                        ins = nc.tensor.transpose(bank(4 + n, f * P, (f + 1) * P),
                                                  probs[i % 2][0][:, kt * P:(kt + 1) * P], ident[:])
                    ins.then_inc(wt_done, 1)

            def values(pair_no, p):
                pe.wait_ge(wt_los, 4 * pair_no + 4)
                ge(pe, o_done, pair_no)
                for kt in range(TT):
                    ins = passes(bank(7, 0, 2 * P), v_hi[:, kt, :], v_lo[:, kt, :],
                                 wt_hi[p % 2][:, kt, :], wt_lo[p % 2][:, kt, :], kt == 0, kt == TT - 1)
                ins.then_inc(pv_done, 1)

            def sums_of_squares(pair_no):
                pe.wait_ge(o_squared, pair_no + 1)
                pe.wait_ge(o_copied, pair_no + 1)
                for q in range(2):
                    ins = nc.tensor.matmul(bank(7, 2 * P + q, 2 * P + q + 1), o_sq[:, q * P:(q + 1) * P],
                                           mean_col[:], start=True, stop=True)
                ins.then_inc(o_ss_done, 1)

            def spread_rstd(pair_no):
                pe.wait_ge(o_rstd_ready, pair_no + 1)
                for q in range(2):
                    ins = nc.tensor.transpose(bank(7, (2 + q) * P, (3 + q) * P),
                                              o_rstd[:, q:q + 1].to_broadcast([P, P]), ident[:])
                ins.then_inc(o_bcast, 1)

            def transpose_v(h, k):
                for f in range(4):
                    tok = (4 * k + f) * P
                    ins = nc.tensor.transpose(bank(6, f * P, (f + 1) * P), v_t[:, tok:tok + P], ident[:])
                ins.then_inc(vt_done, 1)

            def fill(h2, j, i):
                h1 = 2 * h2 + j + 1
                g, ks = FILL[i]
                which = g // 2
                r = 3 * (j + 1) + which
                if ks[0] == 0:
                    pe.wait_ge(proj_hi, 6 * h1 + g)
                    pe.wait_ge(proj_lo, 4 * h1 + min(g, 4))
                    if g == 2:
                        pe.wait_ge(v_los, 2 * h1)
                project(h1, N_ATTN + 6 * h2 + r, r % 2, g, 6, ks)

            def head(h2, j, first=False, last=False):
                h = 2 * h2 + j
                for i in range(TT):
                    s = TT * h + i
                    if i == 0:
                        pe.wait_ge(proj_lo, 4 * h + 4)
                    scores(s, j, i)
                    pair_even = PAIRS * h + (i - 4) // 2
                    if i % 2 == 0 and not (first and i < 4):
                        sums_of_squares(pair_even)
                    if i == 2:
                        if last:
                            pe.wait_ge(proj_hi, 6 * HEADS)
                        else:
                            pe.wait_ge(proj_hi, 6 * h + 8)
                            pe.wait_ge(proj_lo, 4 * h + 6)
                        transpose_v(h, 0)
                    if not last and i in FILL:
                        fill(h2, j, i)
                    if not (first and i == 0):
                        transpose_diff(s - 1, (i - 1) % TT)
                    if i == 2:
                        pe.wait_ge(v_los, 2 * h + 1)
                        transpose_v(h, 1)
                    if i % 2 == 1 and not (first and i == 1):
                        if i == 3:
                            pe.wait_ge(v_los, 2 * h + 2)
                        values(PAIRS * h + (i - 3) // 2, (i - 3) // 2)
                    if i % 2 == 0 and not (first and i < 4):
                        spread_rstd(pair_even)

            pe.wait_ge(combo_done, 4 * GROUPS)
            for g in range(6):
                if g >= 2:
                    pe.wait_ge(proj_hi, g - 1)
                    pe.wait_ge(proj_lo, min(g - 1, 4))
                project(0, N_ATTN + g // 2, (g // 2) % 2, g, 6 + g % 2)
            pe.wait_ge(proj_hi, 6)
            head(0, 0, first=True)
            with pe.Fori(0, 3) as m:
                head(m, 1)
                head(m + 1, 0)
            head(3, 1, last=True)
            last_pair = PAIRS * HEADS - 1
            sums_of_squares(last_pair - 1)
            transpose_diff(TT * HEADS - 1, TT - 1)
            spread_rstd(last_pair - 1)
            values(last_pair, 1)
            sums_of_squares(last_pair)
            spread_rstd(last_pair)

            def gate_tile(b, e2, j):
                e = 2 * e2 + j
                weights(2 * e + N_GATE)
                for n in range(2):
                    ge(pe, sig_done, 2 * e + n - 3)
                    slab_product(bank(4 * j + n), 0, n).then_inc(gate_done, 1)
                weights(2 * e + N_GATE + 1)
                for n in range(2):
                    half = slice(n * HALF, (n + 1) * HALF)
                    ge(pe, gated_done, 2 * e + n - 3)
                    for k in range(KT):
                        if isinstance(e2, int) and e2 == b * KT // 2 and j == 0 and n == 0:
                            pe.wait_ge(b_los, KT * b + k + 1)
                        ins = passes(bank(4 * j + 2 + n), st_hi[1][:, k, :], st_lo[1][:, k, :],
                                     b_hi[:, k, half], b_lo[:, k, half], k == 0, k == KT - 1)
                    ins.then_inc(branch_done, 1)

            pe.wait_ge(biased, 2 * TT * HEADS)
            gate_tile(0, 0, 0)
            pe.wait_ge(o_done, PAIRS * HEADS)
            pe.wait_ge(wt_los, 2 * TT * HEADS)
            gate_tile(0, 0, 1)
            with pe.Fori(1, KT // 2) as m:
                for j in range(2):
                    gate_tile(0, m, j)
            gate_tile(1, KT // 2, 0)
            gate_tile(1, KT // 2, 1)
            with pe.Fori(KT // 2 + 1, KT) as m:
                for j in range(2):
                    gate_tile(1, m, j)

            def out_tile(m, j, first=False):
                t = 2 * m + j
                pe.wait_ge(m_lo, t + 1)
                for n in range(2):
                    half = slice(n * HALF, (n + 1) * HALF)
                    ge(pe, x1_done, 2 * t + n - 3)
                    for k in range(KT):
                        if first and n == 0:
                            weights(N_OUT + k)
                        ins = passes(bank(2 * j + n), st_hi[j][:, k, :], st_lo[j][:, k, :],
                                     wo_hi[:, k, half], wo_lo[:, k, half], k == 0, k == KT - 1)
                    ins.then_inc(wo_done, 1)

            def out_transpose(t, j):
                ge(pe, n_lo, 2 * t + 2 * TT - 2)
                norm_transpose(t + TT, j, 4 + 2 * j)

            pe.wait_ge(gated_done, 4 * KT)
            out_tile(0, 0, first=True)
            out_tile(0, 1)
            out_transpose(0, 0)
            out_tile(1, 0)
            out_transpose(1, 1)
            with pe.Fori(1, TT // 2 - 1) as m:
                out_tile(m, 1)
                out_transpose(2 * m, 0)
                out_tile(m + 1, 0)
                out_transpose(2 * m + 1, 1)
            out_tile(TT // 2 - 1, 1)
            out_transpose(TT - 2, 0)
            out_transpose(TT - 1, 1)

            def hidden(i, e, first=False):
                f = 2 * i + e
                n_slab = 6 * i + N_FFN + 2 * e
                weights(n_slab)
                for n in range(2):
                    if first:
                        pe.wait_ge(n_lo, 2 * TT + 2 * (TT // 2) * (n + 1))
                    ge(pe, silu_done, 2 * f + n - 1)
                    slab_product(bank(n), 0, n).then_inc(g_done, 1)
                weights(n_slab + 1)
                for n in range(2):
                    ge(pe, gu_done, 2 * f + n - 1)
                    slab_product(bank(2 + n), 1, n).then_inc(up_done, 1)

            def down(i, parity):
                weights(6 * i + N_FFN + 5)
                pe.wait_ge(gu_los, 4 * i + 4)
                for t in range(TT):
                    for n in range(2):
                        half = slice(n * HALF, (n + 1) * HALF)
                        ge(pe, down_added, 2 * TT * i + 2 * t + n - 3)
                        for e in range(2):
                            tok = slice(t * P, (t + 1) * P)
                            ins = passes(bank(4 + (2 * t + n) % 4), gu_hi[parity][:, e, tok],
                                         gu_lo[parity][:, e, tok], wd_hi[:, e, half], wd_lo[:, e, half],
                                         e == 0, e == 1)
                        ins.then_inc(down_done, 1)

            def ffn_turn(i, parity):
                hidden(i, 0)
                down(i - 1, 1 - parity)
                hidden(i, 1)
            pe.wait_ge(x1_done, 2 * TT)
            hidden(0, 0, first=True)
            hidden(0, 1)
            ffn_turn(1, 1)
            ffn_turn(2, 0)
            with pe.Fori(1, FFN_TURNS // 2) as m:
                ffn_turn(2 * m + 1, 1)
                ffn_turn(2 * m + 2, 0)
            down(FFN_TURNS - 1, 0)

            def ple_transpose(t, j):
                ge(pe, p_los, t)
                norm_transpose(t + 2 * TT, j, 6)
                pe.wait_ge(n_lo, 2 * t + 4 * TT + 1)
                if isinstance(t, int):
                    pe.wait_ge(p_in[j], 16 * (t // 2 + 1))
                else:
                    pe.wait_ge(p_in[j], 8 * (t - j) + 16)
                for k in range(2):
                    ins = nc.tensor.transpose(bank(6, k * P, (k + 1) * P), p_raw[j][:, k * P:(k + 1) * P],
                                              ident[:])
                ins.then_inc(p_tp, 1)

            def ple_tile(m, j, more=True, first=False):
                t = 2 * m + j
                pe.wait_ge(n_lo, 2 * t + 4 * TT + 2)
                for n in range(2):
                    half = slice(n * HALF, (n + 1) * HALF)
                    ge(pe, pg_sig, 2 * t + n - 3)
                    for k in range(KT):
                        if first and n == 0:
                            weights(N_PLE + k)
                        ins = passes(bank(2 * j + n), st_hi[j][:, k, :], st_lo[j][:, k, :],
                                     wpg_hi[:, k, half], wpg_lo[:, k, half], k == 0, k == KT - 1)
                    ins.then_inc(pg_done, 1)
                if more:
                    ple_transpose(t + 1, 1 - j)
                pe.wait_ge(p_los, t + 1)
                if first:
                    weights(N_PLE + KT + 1)
                for n in range(2):
                    half = slice(n * HALF, (n + 1) * HALF)
                    ge(pe, ple_mul, 2 * t + n - 1)
                    for k in range(2):
                        ins = passes(bank(4 + n), pt_hi[j][:, k, :], pt_lo[j][:, k, :],
                                     wpp_hi[:, k, half], wpp_lo[:, k, half], k == 0, k == 1)
                    ins.then_inc(pp_done, 1)

            pe.wait_ge(gu_done, 2 * FT)
            pe.wait_ge(down_added, 2 * TT * FFN_TURNS)
            ple_transpose(0, 0)
            ple_tile(0, 0, first=True)
            ple_tile(0, 1)
            ple_tile(1, 0)
            with pe.Fori(1, TT // 2 - 1) as m:
                ple_tile(m, 1)
                ple_tile(m + 1, 0)
            ple_tile(TT // 2 - 1, 1, more=False)


_INS = ['x', 'p', 'g_mix', 'w_in', 'lambda_q1', 'lambda_k1', 'lambda_q2', 'lambda_k2', 'g_subln',
        'w_fourier_out', 'w_attn_out', 'w_branch_gate', 'b_branch_gate', 'w_o', 'g_ffn',
        'w_ffn_gate', 'w_ffn_up', 'w_ffn_down', 'g_ple', 'w_ple_gate', 'w_ple_proj', 'g_final']


def shape_constants():
    import numpy as np
    row = np.arange(P)
    turn = 2 * np.pi * np.outer(row, row) / P
    chan = np.concatenate([np.cos(turn), np.sin(turn)], 1) / np.sqrt(P)
    pos = np.zeros((P, 16, KW))
    for parity in range(2):
        for tile in range(2):
            s = 2 * (P * tile + row) + parity
            for k_odd in range(2):
                k = 2 * np.arange(KW) + k_odd
                turn = 2 * np.pi * (np.outer(s, k) % SEQ) / SEQ
                for trig, table in enumerate((np.cos(turn), np.sin(turn))):
                    pos[:, 4 * (2 * parity + tile) + 2 * k_odd + trig] = table / np.sqrt(SEQ)
    distance = -np.abs(row[:, None] + ALIBI_0 - np.arange(ALIBI_W)[None])
    slope = 2.0 ** (-8.0 * np.arange(1, HEADS + 1) / HEADS)
    consts = np.concatenate([HD ** -0.5 / slope, slope, -slope])
    out = {"ident": np.eye(P), "chan_dft": chan, "pos_dft": pos, "distance": distance,
           "head_consts": np.repeat(consts[None], P, 0)}
    return {k: np.ascontiguousarray(v, dtype=np.float32) for k, v in out.items()}


def kernel(**inputs):
    import numpy as _np
    import concourse.bacc as _bacc
    from concourse import mybir as _mybir
    from concourse.bass_utils import run_bass_kernel_spmd as _run

    nc = _bacc.Bacc("TRN2", target_bir_lowering=False, num_devices=1)
    arrays = {f"in_{n}_dram": _np.ascontiguousarray(inputs[n]) for n in _INS}
    arrays.update({f"const_{n}_dram": v for n, v in shape_constants().items()})
    args = [nc.dram_tensor(n, a.shape, _mybir.dt.from_np(a.dtype), kind="ExternalInput").ap()
            for n, a in arrays.items()]
    args.append(nc.dram_tensor("out_0_dram", (1, SEQ, D), _mybir.dt.float32, kind="ExternalOutput").ap())
    encoder_layer(nc, *args)
    r = _run(nc, [arrays], core_ids=[0])
    return r.results[0]["out_0_dram"]
```

```python
from contextlib import ExitStack

import concourse.bass as bass
from concourse import mybir

F32 = mybir.dt.float32
F32R = mybir.dt.float32r
ALU = mybir.AluOpType
ACT = mybir.ActivationFunctionType

P = 128
SEQ = 1024
D = 1024
KT = D // P
TT = SEQ // P
HALF = 512
GROUPS = 8
HEADS = 8
HD = 64
D_FF = 2816
FT = D_FF // P
PLE = 256
EPS = 1e-6
LAMBDA_INIT = 0.8 - 0.6
KW = 130
QUART = 256
ALIBI_W = 2 * SEQ - P
ALIBI_0 = SEQ - P
PAIRS = HEADS // 2

N_FOURIER = 0
N_ATTN = N_FOURIER + GROUPS
N_GATE = N_ATTN + 3 * HEADS
N_OUT = N_GATE + 4 * KT
N_FFN = N_OUT + KT
FFN_TURNS = FT // 2
N_PLE = N_FFN + 6 * FFN_TURNS


def ge(eng, sem, value):
    if isinstance(value, int) and value <= 0:
        return
    eng.wait_ge(sem, value)


def encoder_layer(nc, x, p, g_mix, w_in, lambda_q1, lambda_k1, lambda_q2, lambda_k2, g_subln,
                  w_fourier_out, w_attn_out, w_branch_gate, b_branch_gate, w_o, g_ffn,
                  w_ffn_gate, w_ffn_up, w_ffn_down, g_ple, w_ple_gate, w_ple_proj, g_final,
                  ident_in, chan_dft_in, pos_dft_in, distance_in, head_consts_in, out):
    x_t = x[0].rearrange("(t p) d -> t p d", p=P)
    p_t = p[0, 0].rearrange("(t p) d -> t p d", p=P)
    out_t = out[0].rearrange("(t p) d -> t p d", p=P)
    branch_scr = [nc.dram_tensor(f"branch{b}_scratch", (KT, P, SEQ), F32, kind="Internal").ap()
                  for b in range(2)]

    ctx = ExitStack()
    with ctx:
        arena_bytes = 212736
        arena = ctx.enter_context(nc.sbuf_tensor("arena", [P, arena_bytes // 4], F32))
        base = 16512
        del arena

        def place(name, at, shape, dt=F32):
            size = 4
            for n in shape[1:]:
                size *= n
            assert at % 32 == 0 and at + size <= arena_bytes, (name, at, size)
            return nc.alloc_sbuf_tensor_at(name, shape, dt, offset=base + at)

        def sem(name):
            return ctx.enter_context(nc.semaphore(name))

        K = 1024
        R1 = 64 * K
        R2 = 128 * K
        RING = 160 * K
        MISC = 184 * K
        h_hi = place("h_hi", 0, [P, KT, SEQ], F32R)
        h_lo = place("h_lo", 32 * K, [P, KT, SEQ], F32R)
        raw = [place(f"raw{r}", RING + 4 * K * r, [P, KT, P]) for r in range(2)]
        st_hi = [place(f"st_hi{r}", RING + (8 + 4 * r) * K, [P, KT, P], F32R) for r in range(2)]
        st_lo = [place(f"st_lo{r}", RING + (16 + 4 * r) * K, [P, KT, P], F32R) for r in range(2)]
        raw_row = [place(f"raw_row{r}", RING + 4 * K * r, [P, D]) for r in range(2)]
        stage = [place(f"stage{r}", MISC + 4 * K * r, [P, SEQ]) for r in range(2)]
        gain = place("gain", MISC + 8 * K, [P, D])
        xn = [place(f"xn{r}", MISC + (12 + 4 * r) * K, [P, D]) for r in range(2)]
        distance = place("distance", MISC + 12 * K, [P, ALIBI_W])
        ident = place("ident", MISC + 20 * K, [P, P])
        C = MISC + 20 * K + 512
        gate_bias = place("gate_bias", C, [P, 16])
        head_consts = place("head_consts", C + 64, [P, 24])
        mean_sq = place("mean_sq", C + 160, [P, 2])
        shifted = place("shifted", C + 192, [P, 2])
        rstd = place("rstd", C + 224, [P, 2])
        neg_half = place("neg_half", C + 256, [P, 2])
        mean_col = place("mean_col", C + 288, [P, 1])
        eps_col = place("eps_col", C + 320, [P, 2])
        lam_dot = place("lam_dot", C + 1856, [P, 2])
        lam_exp = place("lam_exp", C + 352, [P, 2])
        neg_lam = place("neg_lam", C + 384, [P, 1])
        sub_gain = place("sub_gain", C + 416, [P, 1])
        row_max = place("row_max", C + 448, [P, 2])
        neg_max = place("neg_max", C + 480, [P, 4])
        exp_sum = place("exp_sum", C + 512, [P, 4])
        inv_sum = place("inv_sum", C + 544, [P, 4])
        o_mean_sq = place("o_mean_sq", C + 576, [P, 2])
        o_rstd = place("o_rstd", C + 608, [P, 2])
        o_shifted = place("o_shifted", C + 640, [P, 2])
        f_mean_sq = place("f_mean_sq", C + 672, [P, 2])
        f_shifted = place("f_shifted", C + 704, [P, 2])
        f_rstd = place("f_rstd", C + 736, [P, 2])
        inv_raw = place("inv_raw", C + 768, [P, 1])
        lam_rows = place("lam_rows", C + 800, [P, 4, HD])
        qscale = head_consts[:, 0:8]
        slope = head_consts[:, 8:16]
        neg_slope = head_consts[:, 16:24]

        x_tiles = place("x_tiles", R2, [P, TT, D])

        u_hi = [place(f"u_hi{r}", R1 + 8 * K * r, [P, SEQ], F32R) for r in range(2)]
        u_lo = [place(f"u_lo{r}", R1 + 8 * K * r + 4 * K, [P, SEQ], F32R) for r in range(2)]
        fold_hi = place("fold_hi", R1 + 16 * K, [P, 2, 4, 256], F32R)
        fold_lo = place("fold_lo", R1 + 24 * K, [P, 2, 4, 256], F32R)
        TAB = 16 * KW * 4
        pos_hi = place("pos_hi", R1 + 32 * K, [P, 16, KW], F32R)
        pos_lo = place("pos_lo", R1 + 32 * K + TAB, [P, 16, KW], F32R)
        F0 = R1 + 32 * K + 2 * TAB
        chan_hi = place("chan_hi", F0, [P, 256], F32R)
        chan_lo = place("chan_lo", F0 + K, [P, 256], F32R)
        far_half = [place(f"far_half{r}", F0 + 2 * K + K * r, [P, 256]) for r in range(2)]
        folded = [place(f"folded{r}", F0 + 4 * K + 2 * K * r, [P, 2, 256]) for r in range(2)]
        sin_part = [place(f"sin_part{r}", F0 + 8 * K + 1056 * r, [P, 258]) for r in range(2)]
        combo = [[place(f"combo{a}{b}", F0 + 10 * K + 64 + 1056 * (2 * a + b), [P, 258])
                  for b in range(2)] for a in range(2)]
        y_out = [place(f"y_out{r}", F0 + 16 * K + 4 * K * r, [P, SEQ]) for r in range(2)]
        pos_raw = place("pos_raw", F0 + 16 * K, [P, 16, KW])
        chan_raw = place("chan_raw", F0 + 16 * K + 8 * K + 512, [P, 256])

        q_hi = [place(f"q_hi{r}", R1 + 16 * K * r, [P, SEQ], F32R) for r in range(2)]
        q_lo = [place(f"q_lo{r}", R1 + 16 * K * r + 4 * K, [P, SEQ], F32R) for r in range(2)]
        k_hi = [place(f"k_hi{r}", R1 + 16 * K * r + 8 * K, [P, SEQ], F32R) for r in range(2)]
        k_lo = [place(f"k_lo{r}", R1 + 16 * K * r + 12 * K, [P, SEQ], F32R) for r in range(2)]
        v_hi = place("v_hi", R1 + 32 * K, [P, TT, P], F32R)
        v_lo = place("v_lo", R1 + 36 * K, [P, TT, P], F32R)
        v_t = place("v_t", R1 + 40 * K, [P, SEQ])
        probs = [[place(f"probs{r}{c}", R1 + 44 * K + 4 * K * (2 * r + c), [P, SEQ])
                  for c in range(2)] for r in range(2)]
        wt_hi = [place(f"wt_hi{r}", R1 + 60 * K + 16 * K * r, [P, TT, 2 * P], F32R) for r in range(2)]
        wt_lo = [place(f"wt_lo{r}", R1 + 68 * K + 16 * K * r, [P, TT, 2 * P], F32R) for r in range(2)]
        o_raw = place("o_raw", R1 + 92 * K, [P, 2 * P])
        o_sq = place("o_sq", R1 + 93 * K, [P, 2 * P])

        b_hi = place("b_hi", R1, [P, KT, SEQ], F32R)
        b_lo = place("b_lo", R1 + 32 * K, [P, KT, SEQ], F32R)
        merged = place("merged", R2, [P, TT, KT, P])
        sig = [[place(f"sig{j}{n}", MISC + 12 * K + 2 * K * (2 * j + n), [P, HALF])
                for n in range(2)] for j in range(2)]
        wo_hi = place("wo_hi", R1, [P, KT, D], F32R)
        wo_lo = place("wo_lo", R1 + 32 * K, [P, KT, D], F32R)
        resid = place("resid", R2, [P, TT, D])

        gu_hi = [place(f"gu_hi{r}", R1 + 16 * K * r, [P, 2, SEQ], F32R) for r in range(2)]
        gu_lo = [place(f"gu_lo{r}", R1 + 16 * K * r + 8 * K, [P, 2, SEQ], F32R) for r in range(2)]
        wd_hi = place("wd_hi", R1 + 32 * K, [P, 2, D], F32R)
        wd_lo = place("wd_lo", R1 + 40 * K, [P, 2, D], F32R)
        silu = [place(f"silu{n}", R1 + 48 * K + 2 * K * n, [P, HALF]) for n in range(2)]
        gu = [place(f"gu{n}", R1 + 52 * K + 2 * K * n, [P, HALF]) for n in range(2)]

        wpg_hi = place("wpg_hi", 0, [P, KT, D], F32R)
        wpg_lo = place("wpg_lo", 32 * K, [P, KT, D], F32R)
        wpp_hi = place("wpp_hi", R1 + 16 * K, [P, 2, D], F32R)
        wpp_lo = place("wpp_lo", R1 + 24 * K, [P, 2, D], F32R)
        pt_hi = [place(f"pt_hi{r}", R1 + 56 * K + 2 * K * r, [P, 2, P], F32R) for r in range(2)]
        pt_lo = [place(f"pt_lo{r}", R1 + 57 * K + 2 * K * r, [P, 2, P], F32R) for r in range(2)]
        p_raw = [place(f"p_raw{r}", R1 + 60 * K + K * r, [P, PLE]) for r in range(2)]
        gain_final = place("gain_final", R1, [P, D])
        pgate = place("pgate", R1 + 4 * K, [P, D])
        x3 = [place(f"x3_{r}", R1 + 32 * K + 4 * K * r, [P, D]) for r in range(2)]
        sq_junk = place("sq_junk", R1 + 40 * K, [P, D])

        banks = ctx.enter_context(nc.psum_tensor("banks", [P, 8, HALF], F32))

        def bank(i, lo=0, hi=HALF):
            return banks[:, i, lo:hi]

        ident_ld = sem("ident_ld")
        consts_in = sem("consts_in")
        dft_in = sem("dft_in")
        dft_hi = sem("dft_hi")
        dft_lo = sem("dft_lo")
        gain_in = sem("gain_in")
        distance_ld = sem("distance_ld")
        raw_in = [sem(f"raw_in{r}") for r in range(2)]
        w_hi = sem("w_hi")
        w_lo = sem("w_lo")
        x_in = [sem(f"x_in{t}") for t in range(TT)]
        stage_in = [sem(f"stage_in{r}") for r in range(2)]
        pool_ready = sem("pool_ready")
        lam_dots = sem("lam_dots")
        lam_exped = sem("lam_exped")
        lam_ready = sem("lam_ready")
        n_sq = sem("n_sq")
        n_ms = sem("n_ms")
        n_rstd = sem("n_rstd")
        n_xn = sem("n_xn")
        n_tp = sem("n_tp")
        n_hi = sem("n_hi")
        n_lo = sem("n_lo")
        u_done = sem("u_done")
        u_his = sem("u_his")
        u_los = sem("u_los")
        chan_done = sem("chan_done")
        far_copied = sem("far_copied")
        fold_done = sem("fold_done")
        fold_his = sem("fold_his")
        fold_los = sem("fold_los")
        pos_done = sem("pos_done")
        sin_copied = sem("sin_copied")
        combo_done = sem("combo_done")
        y_quarters = sem("y_quarters")
        y_stored = [sem(f"y_stored{r}") for r in range(2)]
        proj_done = sem("proj_done")
        proj_hi = sem("proj_hi")
        proj_lo = sem("proj_lo")
        vt_done = sem("vt_done")
        v_his = sem("v_his")
        v_los = sem("v_los")
        score_done = sem("score_done")
        biased = sem("biased")
        max_ready = sem("max_ready")
        exped = sem("exped")
        inv_ready = sem("inv_ready")
        inv_step = sem("inv_step")
        scaled = sem("scaled")
        diff_done = sem("diff_done")
        wt_done = sem("wt_done")
        wt_his = sem("wt_his")
        wt_los = sem("wt_los")
        pv_done = sem("pv_done")
        o_squared = sem("o_squared")
        o_copied = sem("o_copied")
        o_ss_done = sem("o_ss_done")
        o_ss_read = sem("o_ss_read")
        o_ms_ready = sem("o_ms_ready")
        o_rstd_ready = sem("o_rstd_ready")
        o_bcast = sem("o_bcast")
        o_done = sem("o_done")
        o_stored = [sem(f"o_stored{r}") for r in range(2)]
        b_his = sem("b_his")
        b_los = sem("b_los")
        gate_done = sem("gate_done")
        branch_done = sem("branch_done")
        sig_done = sem("sig_done")
        gated_done = sem("gated_done")
        sig_read = sem("sig_read")
        m_hi = sem("m_hi")
        m_lo = sem("m_lo")
        wo_done = sem("wo_done")
        x1_done = sem("x1_done")
        g_done = sem("g_done")
        up_done = sem("up_done")
        silu_done = sem("silu_done")
        gu_done = sem("gu_done")
        gu_his = sem("gu_his")
        gu_los = sem("gu_los")
        down_done = sem("down_done")
        down_added = sem("down_added")
        p_in = [sem(f"p_in{r}") for r in range(2)]
        p_tp = sem("p_tp")
        p_his = sem("p_his")
        p_los = sem("p_los")
        pg_done = sem("pg_done")
        pp_done = sem("pp_done")
        pg_sig = sem("pg_sig")
        ple_mul = sem("ple_mul")
        x3_done = sem("x3_done")
        f_sq = sem("f_sq")
        f_ms = sem("f_ms")
        f_rstd_ready = sem("f_rstd_ready")
        y_final = sem("y_final")
        out_stored = [sem(f"out_stored{r}") for r in range(2)]

        block = ctx.enter_context(nc.Block())

        def slab_cols(w, c0):
            return w[:, bass.ds(c0, P)].rearrange("(t p) n -> p t n", p=P)

        def slab_rows(w, r0):
            return w[bass.ds(r0, P), :]

        def one(ap):
            return ap.rearrange("o p n -> (o p) n")

        def one_mid(ap):
            return ap.rearrange("p o a c -> p (o a) c")

        def in_order(i):
            return bank(i, 0, 2 * KW).rearrange("p (k m) -> p m k", k=2)[:, 0:KW - 1, :]

        FILL = {0: (0, range(KT)), 1: (1, range(KT // 2)), 2: (1, range(KT // 2, KT)),
                3: (2, range(KT)), 4: (3, range(KT)), 5: (4, range(KT // 2)),
                6: (4, range(KT // 2, KT)), 7: (5, range(KT))}
        FILL_END = {i: g for i, (g, ks) in FILL.items() if ks[-1] == KT - 1}

        row_buf = stage + raw_row
        row_in = stage_in + raw_in
        STAGED = KT // 4
        DOWN_STAGED = KT // 2 + STAGED + TT // 2
        FIRST_STAGED = {N_OUT: KT // 2, N_PLE: DOWN_STAGED + FFN_TURNS}
        FIRST_RAW = {N_OUT: N_OUT // 2, N_PLE: N_FFN // 2 - STAGED + 2 * FFN_TURNS}

        def row_landed(base, k):
            first = (FIRST_STAGED if k % 4 < 2 else FIRST_RAW)[base]
            return row_in[k % 4], 16 * (first + k // 4 + 1)

        @block.sync
        def _(sp):
            def load_slab(turn, slot, src, dst=raw):
                ge(sp, w_hi, 2 * turn + slot - 1)
                ge(sp, w_lo, 2 * turn + slot - 1)
                sp.dma_start(dst[slot][:], src).then_inc(raw_in[slot], 16)

            def load_row(base, k, src):
                if k >= 2:
                    last_raw = 1 if base == N_OUT or k >= 4 else 3
                    sp.wait_ge(w_hi, base + k - 2 - last_raw)
                    sp.wait_ge(w_lo, base + k - 2 - last_raw)
                sp.dma_start(row_buf[k % 4][:], src).then_inc(row_in[k % 4], 16)

            sp.dma_start(x_tiles[:, 0, :], x_t[0]).then_inc(x_in[0], 16)
            sp.dma_start(gain[:], g_mix.to_broadcast([P, D])).then_inc(gain_in, 16)
            sp.dma_start(ident[:], ident_in).then_inc(ident_ld, 16)
            for t in range(1, TT):
                sp.dma_start(x_tiles[:, t, :], x_t[t]).then_inc(x_in[t], 16)
                if t in (2, 4):
                    load_slab(0, t // 2 - 1, slab_cols(w_in[0], (t // 2 - 1) * P))
            sp.wait_ge(n_xn, 3)
            sp.dma_start(chan_raw[:], chan_dft_in).then_inc(dft_in, 16)
            sp.dma_start(pos_raw[:], pos_dft_in).then_inc(dft_in, 16)
            sp.dma_start(head_consts[:], head_consts_in).then_inc(consts_in, 16)
            sp.dma_start(sub_gain[:], g_subln.rearrange("a e -> e a"),
                         allow_slow_non_contiguous=True).then_inc(consts_in, 16)
            for r, lam in enumerate((lambda_q1, lambda_k1, lambda_q2, lambda_k2)):
                sp.dma_start(lam_rows[:, r, :], lam.to_broadcast([P, HD])).then_inc(consts_in, 16)
            sp.dma_start(gate_bias[:], b_branch_gate[0].rearrange("(c p) -> p c", p=P),
                         allow_slow_non_contiguous=True).then_inc(consts_in, 16)
            sp.wait_ge(n_xn, TT)
            sp.wait_ge(n_tp, 2 * TT)
            sp.dma_start(gain[:], g_ffn.to_broadcast([P, D])).then_inc(gain_in, 16)
            sp.dma_start(distance[:], distance_in).then_inc(distance_ld, 16)

            with sp.Fori(1, GROUPS // 2) as m:
                for j in range(2):
                    load_slab(m, j, slab_cols(w_in[0], (2 * m + j) * P))

            with sp.Fori(0, PAIRS) as m:
                for s in range(6):
                    j, which = s // 3, s % 3
                    load_slab(3 * m + N_ATTN // 2 + s // 2, s % 2,
                              slab_cols(w_in[0], (2 * m + GROUPS + HEADS * which + j) * P))

            def gate_slabs(m, b, order=(0, 1)):
                w_b = (w_fourier_out[0], w_attn_out[0])[b]
                for place_, what in enumerate(order):
                    for j in range(2):
                        turn = 2 * m + (N_GATE // 2 + KT * b + place_)
                        if what == 0:
                            load_slab(turn, j, slab_cols(w_branch_gate[0], (2 * m + j + KT * b) * P))
                        else:
                            load_slab(turn, j, slab_cols(w_b, (2 * m + j) * P))

            def branch_tile(b, t):
                if t >= 2:
                    sp.wait_ge(b_his, KT * b + t - 1)
                    sp.wait_ge(b_los, KT * b + t - 1)
                sp.dma_start(stage[t % 2][:], branch_scr[b][t]).then_inc(stage_in[t % 2], 16)

            for b in range(2):
                if b == 0:
                    load_slab(N_GATE // 2, 0, slab_cols(w_branch_gate[0], 0))
                    load_slab(N_GATE // 2, 1, slab_cols(w_branch_gate[0], P))
                    for r in range(2):
                        load_slab(N_GATE // 2 + 1, r, slab_cols(w_fourier_out[0], r * P))
                    for r in range(2):
                        sp.wait_ge(y_stored[r], 16 * GROUPS // 2)
                    sp.wait_ge(pv_done, PAIRS * HEADS)
                    for t in range(KT):
                        if t == KT - 1:
                            sp.wait_ge(o_done, PAIRS * HEADS)
                        sp.dma_start(x_tiles[:, t, :], branch_scr[b][t]).then_inc(x_in[t], 16)
                else:
                    for r in range(2):
                        sp.wait_ge(o_stored[r], 16 * HEADS // 2)
                        branch_tile(b, r)
                    gate_slabs(0, b, (0,))
                    for t in range(2, KT):
                        if t == 4 or t == 6:
                            load_slab(N_GATE // 2 + KT + 1, t // 2 - 2,
                                      slab_cols(w_attn_out[0], (t // 2 - 2) * P))
                        branch_tile(b, t)
                with sp.Fori(1, KT // 2 - b) as m:
                    gate_slabs(m, b)
            sp.wait_ge(b_his, 2 * KT)
            sp.wait_ge(b_los, 2 * KT)
            for k in range(2):
                load_row(N_OUT, k, slab_rows(w_o[0], k * P))
            gate_slabs(KT // 2 - 1, 1, (1, 0))

            for k in range(2, KT):
                load_row(N_OUT, k, slab_rows(w_o[0], k * P))
            for t in range(2):
                sp.wait_ge(w_hi, N_OUT + 5 + t)
                sp.wait_ge(w_lo, N_OUT + 5 + t)
                sp.dma_start(stage[t][:], x_t[t]).then_inc(stage_in[t], 16)
            def ffn_slabs(i, e):
                for slot, w in enumerate((w_ffn_gate[0], w_ffn_up[0])):
                    src = slab_cols(w, (2 * i + e) * P)
                    held = 6 * i + N_FFN + 2 * e + slot - (2 if e else 4)
                    ge(sp, w_hi, held + 1)
                    ge(sp, w_lo, held + 1)
                    sp.nop(nofuse=True)
                    sp.dma_start(raw[slot][:], src).then_inc(raw_in[slot], 16)

            def down_rows(i, first=False):
                for e in range(2):
                    src = slab_rows(w_ffn_down[0], (2 * i + e) * P)
                    if not first:
                        sp.wait_ge(w_hi, 6 * i + N_FFN + e - 1)
                        sp.wait_ge(w_lo, 6 * i + N_FFN + e - 1)
                    sp.dma_start(stage[e][:], src).then_inc(stage_in[e], 16)

            def ffn_turn(i):
                ffn_slabs(i, 0)
                down_rows(i)
                ffn_slabs(i, 1)
            load_slab(N_FFN // 2, 0, slab_cols(w_ffn_gate[0], 0))
            load_slab(N_FFN // 2, 1, slab_cols(w_ffn_up[0], 0))
            for t in range(2, TT):
                sp.wait_ge(x1_done, 2 * (t - 1))
                sp.dma_start(stage[t % 2][:], x_t[t]).then_inc(stage_in[t % 2], 16)
            ffn_slabs(0, 1)
            sp.wait_ge(x1_done, 2 * TT)
            down_rows(0, first=True)
            sp.wait_ge(n_xn, 2 * TT)
            sp.dma_start(gain[:], g_ple.to_broadcast([P, D])).then_inc(gain_in, 16)
            for t in range(2):
                sp.dma_start(p_raw[t][:], p_t[t]).then_inc(p_in[t], 16)
            with sp.Fori(1, FFN_TURNS) as i:
                ffn_turn(i)

            for k in (2, 3, 0, 1, 4, 5, 6, 7):
                if k < 2:
                    sp.wait_ge(w_hi, N_PLE - 1 + k)
                    sp.wait_ge(w_lo, N_PLE - 1 + k)
                load_row(N_PLE, k, slab_rows(w_ple_gate[0], k * P))
            for k in range(2):
                load_row(N_PLE, KT + k, slab_rows(w_ple_proj[0], k * P))
            sp.wait_ge(down_done, 16 * FFN_TURNS)
            sp.dma_start(gain_final[:], g_final.rearrange("(a d) -> a d", a=1).to_broadcast([P, D]))\
              .then_inc(gain_in, 16)
            for t in range(TT):
                if t + 2 < TT:
                    sp.wait_ge(p_tp, t + 1)
                    sp.dma_start(p_raw[t % 2][:], p_t[t + 2]).then_inc(p_in[t % 2], 16)
                sp.wait_ge(y_final, t + 1)
                sp.dma_start(out_t[t], stage[t % 2][:]).then_inc(out_stored[t % 2], 16)
            for r in range(2):
                sp.wait_ge(out_stored[r], 16 * TT // 2)

        @block.gpsimd
        def _(pool):
            def split_lo(turn, slot, dst=None, src=None):
                pool.wait_ge(w_hi, 2 * turn + slot + 1)
                if src is None:
                    src = (raw if dst is None else raw_row)[slot][:]
                hi, lo = (st_hi[slot][:], st_lo[slot][:]) if dst is None else dst
                nc.gpsimd.tensor_tensor(lo, src, hi.bitcast(F32), ALU.subtract).then_inc(w_lo, 1)

            def row_lo(base, k, hi, lo):
                n = base + k
                pool.wait_ge(w_lo, n)
                split_lo(n // 2, n % 2, (hi, lo), row_buf[k % 4][:])

            def inv_rms(count, means, shifted, outs, summed, shift_ready, done):
                width = means.shape[1]
                pool.wait_ge(summed, count)
                nc.gpsimd.tensor_tensor(shifted, means, eps_col[:, 0:width], ALU.add)\
                    .then_inc(shift_ready, 1)
                pool.wait_ge(shift_ready, count)
                nc.gpsimd.tensor_tensor(outs, shifted, neg_half[:, 0:width], ALU.pow)\
                    .then_inc(done, 1)

            def tile_norm(t, j):
                sl = slice(j, j + 1)
                inv_rms(t + 1, mean_sq[:, sl], shifted[:, sl], rstd[:, sl], n_sq, n_ms, n_rstd)

            nc.gpsimd.memset(neg_half[:], -0.5).then_inc(pool_ready, 1)
            nc.gpsimd.memset(mean_col[:], 1.0 / P).then_inc(pool_ready, 1)
            nc.gpsimd.memset(eps_col[:], EPS).then_inc(pool_ready, 1)
            pool.wait_ge(pool_ready, 3)
            for j in range(2):
                tile_norm(j, j)
            split_lo(0, 0)
            with pool.Fori(1, TT // 2) as m:
                for j in range(2):
                    tile_norm(2 * m + j, j)
            split_lo(0, 1)

            def mirror(g2, j):
                g = 2 * g2 + j
                pool.wait_ge(combo_done, 4 * g + 4)
                ge(pool, y_stored[j], 16 * g2)
                (em, om), (ep, op) = combo
                y = y_out[j]
                near, back = slice(0, QUART), slice(QUART, 0, -1)
                quarters = ((em, om, near, ALU.add), (ep, op, back, ALU.subtract),
                            (em, om, near, ALU.subtract), (ep, op, back, ALU.add))
                for q, (a, b, part, op_) in enumerate(quarters):
                    nc.gpsimd.tensor_tensor(y[:, q * QUART:(q + 1) * QUART], a[:, part], b[:, part], op_)\
                        .then_inc(y_quarters, 1)
                pool.wait_ge(y_quarters, 4 * g + 4)
                pool.dma_start(one(branch_scr[0][bass.ds(g, 1)]), y[:]).then_inc(y_stored[j], 16)

            def fourier_pair(g2):
                for j in range(2):
                    split_lo(g2 + 1, j)
                    mirror(g2, j)
            fourier_pair(0)
            with pool.Fori(1, GROUPS // 2) as m:
                fourier_pair(m)

            split_lo(5, 0)
            split_lo(5, 1)

            def sub_norm(count):
                inv_rms(count, o_mean_sq[:], o_shifted[:], o_rstd[:], o_ss_read, o_ms_ready, o_rstd_ready)

            def store_o(h, j):
                pool.wait_ge(o_done, PAIRS * (h + 1))
                pool.dma_start(one(branch_scr[1][bass.ds(h, 1)]), stage[j][:])\
                    .then_inc(o_stored[j], 16)

            def head(h2, j, first=False, last=False):
                h = 2 * h2 + j
                slab = lambda s: (3 * h2 + 6 + (3 * j + s) // 2, (3 * j + s) % 2)
                split_lo(*slab(0))
                if not first:
                    sub_norm(PAIRS * h - 1)
                    sub_norm(PAIRS * h)
                if not last:
                    split_lo(*slab(1))
                if not first:
                    store_o(h - 1, 1 - j)
                sub_norm(PAIRS * h + 1)
                if not last:
                    split_lo(*slab(2))
                sub_norm(PAIRS * h + 2)
            head(0, 0, first=True)
            with pool.Fori(0, 3) as m:
                head(m, 1)
                head(m + 1, 0)
            head(3, 1, last=True)
            sub_norm(PAIRS * HEADS - 1)
            sub_norm(PAIRS * HEADS)
            store_o(HEADS - 1, 1)

            with pool.Fori(1, 2 * KT) as e:
                for s in range(2):
                    split_lo(e + N_GATE // 2, s)

            for k in range(0, KT, 2):
                row_lo(N_OUT, k, wo_hi[:, k, :], wo_lo[:, k, :])
            with pool.Fori(TT // 2, TT - 1) as m:
                for j in range(2):
                    tile_norm(2 * m + j, j)
            for j in range(2):
                tile_norm(2 * TT - 2 + j, j)
                split_lo(N_FFN // 2, j)

            def ffn_turn(i, first=False):
                for e in range(1 if first else 0, 2):
                    for s in range(2):
                        split_lo(3 * i + N_FFN // 2 + e, s)
                for e in range(2):
                    split_lo(3 * i + N_FFN // 2 + 2, e, (wd_hi[:, e, :], wd_lo[:, e, :]), stage[e][:])
            ffn_turn(0, first=True)
            with pool.Fori(1, FFN_TURNS) as i:
                ffn_turn(i)

            for k in range(0, KT, 2):
                row_lo(N_PLE, k, wpg_hi[:, k, :], wpg_lo[:, k, :])
                if k == 0:
                    tile_norm(2 * TT, 0)
            row_lo(N_PLE, KT, wpp_hi[:, 0, :], wpp_lo[:, 0, :])

            def final_norm(t, j):
                sl = slice(j, j + 1)
                inv_rms(t + 1, f_mean_sq[:, sl], f_shifted[:, sl], f_rstd[:, sl], f_sq, f_ms, f_rstd_ready)
            tile_norm(2 * TT + 1, 1)
            final_norm(0, 0)
            with pool.Fori(0, TT // 2 - 1) as m:
                tile_norm(2 * m + 2 * TT + 2, 0)
                final_norm(2 * m + 1, 1)
                tile_norm(2 * m + 2 * TT + 3, 1)
                final_norm(2 * m + 2, 0)
            final_norm(TT - 1, 1)

        @block.scalar
        def _(act):
            def split_hi(turn, slot, free=None, dst=None):
                act.wait_ge(raw_in[slot], 16 * (turn + 1))
                if free is not None:
                    ge(act, *free)
                if dst is None:
                    nc.scalar.copy(st_hi[slot][:], raw[slot][:]).then_inc(w_hi, 1)
                else:
                    nc.scalar.copy(dst, raw_row[slot][:]).then_inc(w_hi, 1)

            def row_hi(base, k, free, dst):
                act.wait_ge(*row_landed(base, k))
                ge(act, *free)
                nc.scalar.copy(dst, row_buf[k % 4][:]).then_inc(w_hi, 1)

            def square(src, junk, mean, done):
                nc.scalar.activation(junk, src, ACT.Square, scale=D ** -0.5, accum_out=mean)\
                    .then_inc(done, 1)

            def split_wait():
                act.nop(nofuse=True)

            def transposed_hi(t, dst, bank0):
                for n in range(2):
                    act.wait_ge(n_tp, 2 * t + n + 1)
                    nc.scalar.copy(dst(4 * n), bank(bank0 + n).rearrange("p (f c) -> p f c", f=4))\
                        .then_inc(n_hi, 1)

            def h_cols(t):
                return lambda f: h_hi[:, f:f + 4, bass.ds(t * P, P)]

            def norm_square(m, j):
                t = 2 * m + j
                act.wait_ge(x_in[t], 16)
                ge(act, n_tp, 4 * m + 2 * j - 2)
                square(x_tiles[:, t, :], xn[j][:], mean_sq[:, j:j + 1], n_sq)
            norm_square(0, 0)
            norm_square(0, 1)
            for t in range(TT):
                transposed_hi(t, h_cols(t), 2 * (t % 2))
                if t + 2 < TT:
                    norm_square(t // 2 + 1, t % 2)
                if t == 0:
                    split_hi(0, 0)
                if t == 4:
                    split_hi(0, 1)
            act.wait_ge(dft_in, 32)
            nc.scalar.copy(chan_hi[:], chan_raw[:]).then_inc(dft_hi, 1)
            nc.scalar.copy(pos_hi[:], pos_raw[:]).then_inc(dft_hi, 1)
            act.wait_ge(lam_dots, 2)
            nc.scalar.activation(lam_exp[:], lam_dot[:], ACT.Exp).then_inc(lam_exped, 1)

            def u_evac(g, j, n, first_bank=0):
                act.wait_ge(u_done, 2 * g + n + 1)
                nc.scalar.copy(u_hi[j][:, n * HALF:(n + 1) * HALF], bank(first_bank + n)).then_inc(u_his, 1)

            def fold_split(g, c):
                act.wait_ge(fold_done, 4 * g + c + 1)
                ge(act, pos_done, 2 * g)
                nc.scalar.copy(fold_hi[:, :, c, :], folded[c % 2][:]).then_inc(fold_his, 1)

            def fourier_group(g2, j, last=False):
                g = 2 * g2 + j
                split_hi(g2 + 1, j, (u_done, 2 * g + 2))
                if not last:
                    u_evac(g + 1, 1 - j, 0)
                for c in range(4):
                    act.wait_ge(chan_done, 4 * g + c + 1)
                    ge(act, fold_done, 4 * g + c - 1)
                    nc.scalar.copy(far_half[c % 2][:], bank(2 + c % 2, 256, 512)).then_inc(far_copied, 1)
                    if c >= 1:
                        fold_split(g, c - 1)
                fold_split(g, 3)
                if not last:
                    u_evac(g + 1, 1 - j, 1)
                for par in range(2):
                    act.wait_ge(pos_done, 2 * g + par + 1)
                    ge(act, combo_done, 4 * g)
                    nc.scalar.copy(sin_part[par][:].rearrange("p (m k) -> p m k", k=2),
                                   in_order(5 + 2 * par)).then_inc(sin_copied, 1)

            u_evac(0, 0, 0, 4)
            u_evac(0, 0, 1, 4)
            fourier_group(0, 0)
            with act.Fori(0, 3) as m:
                fourier_group(m, 1)
                fourier_group(m + 1, 0)
            fourier_group(3, 1, last=True)

            def proj_evac(h, j, g, src):
                which, n = g // 2, g % 2
                act.wait_ge(proj_done, 6 * h + g + 1)
                dst = ((q_hi[j], k_hi[j], v_t)[which])[:, n * HALF:(n + 1) * HALF]
                if which == 0:
                    split_wait()
                    nc.scalar.activation(dst, src, ACT.Copy, scale=qscale[:, bass.ds(h, 1)])\
                        .then_inc(proj_hi, 1)
                else:
                    nc.scalar.copy(dst, src).then_inc(proj_hi, 1)

            def wt_evac(s, i):
                pair = (i // 2) % 2
                for n in range(2):
                    act.wait_ge(wt_done, 2 * s + n + 1)
                    nc.scalar.copy(wt_hi[pair][:, 4 * n:4 * n + 4, (i % 2) * P:(i % 2 + 1) * P],
                                   bank(4 + n).rearrange("p (f c) -> p f c", f=4)).then_inc(wt_his, 1)

            def value_hi(h, k):
                act.wait_ge(vt_done, 2 * h + k + 1)
                nc.scalar.copy(v_hi[:, 4 * k:4 * k + 4, :],
                               bank(4 + k).rearrange("p (f c) -> p f c", f=4)).then_inc(v_his, 1)

            def out_square(pair_no):
                act.wait_ge(pv_done, pair_no + 1)
                ge(act, o_ss_done, pair_no)
                nc.scalar.activation(o_sq[:], bank(7, 0, 2 * P), ACT.Square).then_inc(o_squared, 1)

            def head(h2, j, first=False, last=False):
                h = 2 * h2 + j
                slab = lambda r: (3 * h2 + 6 + (3 * j + r) // 2, (3 * j + r) % 2)
                for i in range(TT):
                    s = TT * h + i
                    pr = probs[i % 2]
                    if i == 0:
                        split_hi(*slab(0), (proj_done, 6 * h + 6))
                    if i == 2:
                        for k in range(2):
                            value_hi(h, k)
                    if i == 3 and not last:
                        split_hi(*slab(1), (proj_done, 6 * h + 8))
                    if i == 5 and not last:
                        split_hi(*slab(2), (proj_done, 6 * h + 10))
                    for c in range(2):
                        col = slice(2 * (i % 2) + c, 2 * (i % 2) + c + 1)
                        act.wait_ge(max_ready, 2 * s + c + 1)
                        ge(act, inv_ready, 2 * s + c - 3)
                        split_wait()
                        nc.scalar.activation(pr[c][:], pr[c][:], ACT.Exp, bias=neg_max[:, col],
                                             scale=slope[:, bass.ds(h, 1)], accum_out=exp_sum[:, col])\
                            .then_inc(exped, 1)
                    short = len(FILL[i][1]) < KT
                    if not last and i in FILL_END and short:
                        proj_evac(h + 1, 1 - j, FILL_END[i], bank(6))
                    act.wait_ge(inv_ready, 2 * s + 1)
                    nc.scalar.activation(pr[0][:], pr[0][:], ACT.Copy,
                                         scale=inv_sum[:, 2 * (i % 2):2 * (i % 2) + 1]).then_inc(scaled, 1)
                    if not last and i in FILL_END and not short:
                        proj_evac(h + 1, 1 - j, FILL_END[i], bank(6))
                    if not (first and i == 0):
                        wt_evac(s - 1, (i - 1) % TT)
                    if i % 2 == 1 and not (first and i == 1):
                        out_square(PAIRS * h + (i - 3) // 2)

            for r in range(2):
                act.wait_ge(y_stored[r], 16 * GROUPS // 2)
            for g in range(6):
                proj_evac(0, 0, g, bank(6 + g % 2))
                if g == 1:
                    split_hi(5, 0, (proj_done, 2))
                if g == 3:
                    split_hi(5, 1, (proj_done, 4))
            head(0, 0, first=True)
            with act.Fori(0, 3) as m:
                head(m, 1)
                head(m + 1, 0)
            head(3, 1, last=True)
            wt_evac(TT * HEADS - 1, TT - 1)
            out_square(PAIRS * HEADS - 1)

            def sigmoids(m, j, ns=range(2)):
                e = 2 * m + j
                for n in ns:
                    act.wait_ge(gate_done, 2 * e + n + 1)
                    ge(act, sig_read, 2 * e + n - 3)
                    split_wait()
                    nc.scalar.activation(sig[j][n][:], bank(4 * j + n), ACT.Sigmoid,
                                         bias=gate_bias[:, bass.ds(e, 1)]).then_inc(sig_done, 1)

            def branch_split(b):
                if b == 0:
                    act.wait_ge(pv_done, PAIRS * HEADS)
                else:
                    act.wait_ge(branch_done, 2 * KT)
                for t in range(KT):
                    if b == 0:
                        act.wait_ge(x_in[t], 32)
                        nc.scalar.copy(b_hi[:, t, :], x_tiles[:, t, :]).then_inc(b_his, 1)
                    else:
                        act.wait_ge(stage_in[t % 2], 16 * (t // 2 + 1))
                        nc.scalar.copy(b_hi[:, t, :], stage[t % 2][:]).then_inc(b_his, 1)
                    if t % 4 == 3:
                        sigmoids(KT // 2 * b, t // 4)
                        split_hi(KT * b + N_GATE // 2 + 1, t // 4)

            def gate_turn(m, split=True):
                turn = 2 * m + N_GATE // 2
                if split:
                    for j in range(2):
                        sigmoids(m, j)
                        split_hi(turn + 1, j)
                for j in range(2):
                    split_hi(turn + 2, j, (branch_done, 4 * m + 2 * j + 2))

            branch_split(0)
            gate_turn(0, split=False)
            with act.Fori(1, KT // 2) as m:
                gate_turn(m)
            branch_split(1)
            gate_turn(KT // 2, split=False)
            with act.Fori(KT // 2 + 1, KT - 1) as m:
                gate_turn(m)
            for j in range(2):
                split_hi(N_OUT // 2 - 1, j, (branch_done, 4 * KT - 2 + 2 * j))

            for k in range(KT):
                row_hi(N_OUT, k, (branch_done, 4 * KT), wo_hi[:, k, :])
                if k == KT // 2 - 1:
                    sigmoids(KT - 1, 0)

            def merged_hi(t, j, free):
                ge(act, *free)
                nc.scalar.copy(st_hi[j][:], one_mid(merged[:, bass.ds(t, 1), :, :])).then_inc(m_hi, 1)

            def out_tile(m, j, more=True):
                t = 2 * m + j
                act.wait_ge(x1_done, 2 * t + 2)
                ge(act, n_tp, 2 * t + 2 * TT - 2)
                split_wait()
                square(resid[:, bass.ds(t, 1), :].rearrange("p o n -> p (o n)"), xn[j][:],
                       mean_sq[:, j:j + 1], n_sq)
                if more:
                    merged_hi(t + 2, j, (wo_done, 2 * t + 2))
                else:
                    split_hi(N_FFN // 2 - STAGED, j, (wo_done, 2 * t + 2))
                transposed_hi(t + TT, h_cols(t), 4 + 2 * j)

            sigmoids(KT - 1, 1, (0,))
            act.wait_ge(sig_read, 4 * KT - 1)
            merged_hi(0, 0, (gate_done, 4 * KT - 2))
            sigmoids(KT - 1, 1, (1,))
            merged_hi(1, 1, (gate_done, 4 * KT))
            out_tile(0, 0)
            act.wait_ge(sig_read, 4 * KT)
            out_tile(0, 1)
            with act.Fori(1, TT // 2 - 1) as m:
                for j in range(2):
                    out_tile(m, j)
            for j in range(2):
                out_tile(TT // 2 - 1, j, more=False)

            def ffn_turn(i, parity, last=False):
                turn = 2 * i + N_FFN // 2 - STAGED
                for e in range(2):
                    f = 2 * i + e
                    for n in range(2):
                        act.wait_ge(g_done, 2 * f + n + 1)
                        ge(act, gu_done, 2 * f + n - 1)
                        nc.scalar.activation(silu[n][:], bank(n), ACT.Silu).then_inc(silu_done, 1)
                    if e == 1:
                        for k in range(2):
                            act.wait_ge(stage_in[k], 16 * (i + DOWN_STAGED + 1))
                            ge(act, down_done, 2 * TT * i)
                            nc.scalar.copy(wd_hi[:, k, :], stage[k][:]).then_inc(w_hi, 1)
                    following = turn + 1 + e
                    if e == 0 or not last:
                        split_hi(following, 0)
                    for n in range(2):
                        act.wait_ge(gu_done, 2 * f + n + 1)
                        nc.scalar.copy(gu_hi[parity][:, e, n * HALF:(n + 1) * HALF], gu[n][:])\
                            .then_inc(gu_his, 1)
                    if e == 0 or not last:
                        split_hi(following, 1)

            ffn_turn(0, 0)
            with act.Fori(0, FFN_TURNS // 2 - 1) as m:
                ffn_turn(2 * m + 1, 1)
                ffn_turn(2 * m + 2, 0)
            ffn_turn(FFN_TURNS - 2, 1)
            ffn_turn(FFN_TURNS - 1, 0, last=True)

            def gate_rows(ks):
                for k in ks:
                    row_hi(N_PLE, k, (up_done, 2 * FT), wpg_hi[:, k, :])
            def ple_square(t, j):
                act.wait_ge(down_added, 2 * TT * (FFN_TURNS - 1) + 2 * t + 2)
                ge(act, n_tp, 2 * t + 4 * TT - 2)
                split_wait()
                square(resid[:, bass.ds(t, 1), :].rearrange("p o n -> p (o n)"), xn[j][:],
                       mean_sq[:, j:j + 1], n_sq)

            def ple_hi(t, j, bank_x=6, bank_p=6):
                transposed_hi(t + 2 * TT, lambda f: st_hi[j][:, f:f + 4, :], bank_x)
                act.wait_ge(p_tp, t + 1)
                nc.scalar.copy(pt_hi[j][:], bank(bank_p, 0, PLE).rearrange("p (k c) -> p k c", k=2))\
                    .then_inc(p_his, 1)

            def ple_tile(m, j, more=True):
                t = 2 * m + j
                if more:
                    ple_square(t + 1, 1 - j)
                for n in range(2):
                    act.wait_ge(pg_done, 2 * t + n + 1)
                    ge(act, x3_done, t)
                    nc.scalar.activation(pgate[:, n * HALF:(n + 1) * HALF], bank(2 * j + n),
                                         ACT.Sigmoid).then_inc(pg_sig, 1)
                if more:
                    ple_hi(t + 1, 1 - j)
                act.wait_ge(x3_done, t + 1)
                ge(act, f_rstd_ready, t)
                square(x3[j][:], sq_junk[:], f_mean_sq[:, j:j + 1], f_sq)

            gate_rows(range(KT // 2))
            ple_square(0, 0)
            gate_rows(range(KT // 2, KT))
            ple_hi(0, 0, 0, 2)
            for k in range(2):
                row_hi(N_PLE, KT + k, (down_done, 2 * TT * (FFN_TURNS - 1)), wpp_hi[:, k, :])
            ple_tile(0, 0)
            ple_tile(0, 1)
            ple_tile(1, 0)
            with act.Fori(1, TT // 2 - 1) as m:
                ple_tile(m, 1)
                ple_tile(m + 1, 0)
            ple_tile(TT // 2 - 1, 1, more=False)

        @block.vector
        def _(dve):
            sub = ALU.subtract

            def lo(dst, src, hi, done):
                nc.vector.tensor_tensor(dst, src, hi.bitcast(F32), sub).then_inc(done, 1)

            def normed(t, j, src, gains):
                dve.wait_ge(n_rstd, t + 1)
                dve.wait_ge(gain_in, 16 * gains)
                nc.vector.scalar_tensor_tensor(xn[j][:], src, rstd[:, j:j + 1], gain[:],
                                               ALU.mult, ALU.mult).then_inc(n_xn, 1)

            def transposed_lo(t, dst_lo, dst_hi, bank0):
                for n in range(2):
                    dve.wait_ge(n_hi, 2 * t + n + 1)
                    lo(dst_lo(4 * n), bank(bank0 + n).rearrange("p (f c) -> p f c", f=4),
                       dst_hi(4 * n), n_lo)

            def h_cols(buf, t):
                return lambda f: buf[:, f:f + 4, bass.ds(t * P, P)]

            def tile_of(buf, t):
                return buf[:, bass.ds(t, 1), :].rearrange("p o n -> p (o n)")

            normed(0, 0, x_tiles[:, 0, :], 1)
            normed(1, 1, x_tiles[:, 1, :], 1)
            for t in range(TT):
                transposed_lo(t, h_cols(h_lo, t), h_cols(h_hi, t), 2 * (t % 2))
                if t + 2 < TT:
                    normed(t + 2, t % 2, x_tiles[:, t + 2, :], 1)
            dve.wait_ge(dft_hi, 2)
            lo(chan_lo[:], chan_raw[:], chan_hi[:], dft_lo)
            lo(pos_lo[:], pos_raw[:], pos_hi[:], dft_lo)

            dve.wait_ge(consts_in, 16 * 7)
            for r in range(2):
                nc.vector.tensor_tensor_reduce(lam_rows[:, 2 * r, :], lam_rows[:, 2 * r, :],
                                               lam_rows[:, 2 * r + 1, :], 1.0, 0.0, ALU.mult, ALU.add,
                                               lam_dot[:, r:r + 1]).then_inc(lam_dots, 1)
            dve.wait_ge(lam_exped, 1)
            nc.vector.scalar_tensor_tensor(neg_lam[:], lam_exp[:, 1:2], -LAMBDA_INIT, lam_exp[:, 0:1],
                                           ALU.add, sub).then_inc(lam_ready, 1)
            nc.vector.tensor_scalar(sub_gain[:], sub_gain[:], 1.0 - LAMBDA_INIT, None, ALU.mult)\
                .then_inc(lam_ready, 1)

            def u_split(g, j, n, first_bank=0):
                dve.wait_ge(u_his, 2 * g + n + 1)
                half = slice(n * HALF, (n + 1) * HALF)
                lo(u_lo[j][:, half], bank(first_bank + n), u_hi[j][:, half], u_los)

            def fold_split(g, c):
                dve.wait_ge(fold_his, 4 * g + c + 1)
                lo(fold_lo[:, :, c, :], folded[c % 2][:], fold_hi[:, :, c, :], fold_los)

            def fourier_group(g2, j, last=False):
                g = 2 * g2 + j
                if not last:
                    u_split(g + 1, 1 - j, 0)
                for c in range(4):
                    dve.wait_ge(far_copied, 4 * g + c + 1)
                    ge(dve, fold_los, 4 * g + c - 1)
                    near = bank(2 + c % 2, 0, 256)
                    nc.vector.tensor_tensor(folded[c % 2][:, 0, :], near, far_half[c % 2][:], ALU.add)
                    nc.vector.tensor_tensor(folded[c % 2][:, 1, :], near, far_half[c % 2][:], sub)\
                        .then_inc(fold_done, 1)
                    if c >= 1:
                        fold_split(g, c - 1)
                fold_split(g, 3)
                if not last:
                    u_split(g + 1, 1 - j, 1)
                for par in range(2):
                    dve.wait_ge(sin_copied, 2 * g + par + 1)
                    ge(dve, y_quarters, 4 * g)
                    for a, op in enumerate((sub, ALU.add)):
                        nc.vector.tensor_tensor(combo[a][par][:].rearrange("p (m k) -> p m k", k=2),
                                                in_order(4 + 2 * par),
                                                sin_part[par][:].rearrange("p (m k) -> p m k", k=2), op)\
                            .then_inc(combo_done, 1)

            u_split(0, 0, 0, 4)
            u_split(0, 0, 1, 4)
            fourier_group(0, 0)
            with dve.Fori(0, 3) as m:
                fourier_group(m, 1)
                fourier_group(m + 1, 0)
            fourier_group(3, 1, last=True)

            def proj_split(h, j, g, src):
                which, n = g // 2, g % 2
                half = slice(n * HALF, (n + 1) * HALF)
                dve.wait_ge(proj_hi, 6 * h + g + 1)
                if which == 0:
                    nc.vector.scalar_tensor_tensor(q_lo[j][:, half], src, qscale[:, bass.ds(h, 1)],
                                                   q_hi[j][:, half].bitcast(F32), ALU.mult, sub)\
                        .then_inc(proj_lo, 1)
                else:
                    lo(k_lo[j][:, half], src, k_hi[j][:, half], proj_lo)

            def wt_split(s, i):
                pair = (i // 2) % 2
                for n in range(2):
                    dve.wait_ge(wt_his, 2 * s + n + 1)
                    part = (slice(None), slice(4 * n, 4 * n + 4), slice((i % 2) * P, (i % 2 + 1) * P))
                    lo(wt_lo[pair][part], bank(4 + n).rearrange("p (f c) -> p f c", f=4),
                       wt_hi[pair][part], wt_los)

            def value_lo(h, k):
                dve.wait_ge(v_his, 2 * h + k + 1)
                lo(v_lo[:, 4 * k:4 * k + 4, :], bank(4 + k).rearrange("p (f c) -> p f c", f=4),
                   v_hi[:, 4 * k:4 * k + 4, :], v_los)

            def out_copy(pair_no):
                dve.wait_ge(pv_done, pair_no + 1)
                dve.wait_ge(o_squared, pair_no + 1)
                nc.vector.tensor_scalar(o_raw[:], bank(7, 0, 2 * P), sub_gain[:], None, ALU.mult)\
                    .then_inc(o_copied, 1)

            def sums_read(pair_no):
                dve.wait_ge(o_ss_done, pair_no + 1)
                nc.vector.tensor_copy(o_mean_sq[:], bank(7, 2 * P, 2 * P + 2)).then_inc(o_ss_read, 1)

            def out_norm(pair_no, slot, p, stored):
                dve.wait_ge(o_bcast, pair_no + 1)
                if p == 0:
                    ge(dve, o_stored[slot], stored)
                nc.vector.tensor_tensor(stage[slot][:, 2 * P * p:2 * P * (p + 1)], o_raw[:],
                                        bank(7, 2 * P, 4 * P), ALU.mult).then_inc(o_done, 1)

            def head(h2, j, first=False, last=False):
                h = 2 * h2 + j
                for i in range(TT):
                    s = TT * h + i
                    pr = probs[i % 2]
                    start = ALIBI_0 - P * i
                    for c in range(2):
                        col = slice(2 * (i % 2) + c, 2 * (i % 2) + c + 1)
                        dve.wait_ge(score_done, 2 * s + c + 1)
                        ge(dve, wt_done, 2 * s - 2)
                        dve.nop(nofuse=True)
                        nc.vector.tensor_tensor_reduce(
                            pr[c][:], banks[:, 2 * c:2 * c + 2, :].rearrange("p b n -> p (b n)"),
                            distance[:, start:start + SEQ], 1.0, -3.0e38, ALU.add, ALU.max,
                            row_max[:, c:c + 1]).then_inc(biased, 1)
                        dve.wait_ge(biased, 2 * s + c + 1)
                        nc.vector.tensor_tensor(neg_max[:, col], row_max[:, c:c + 1],
                                                neg_slope[:, bass.ds(h, 1)], ALU.mult)\
                            .then_inc(max_ready, 1)
                    if i == 2:
                        for k in range(2):
                            value_lo(h, k)
                    pair_even = PAIRS * h + (i - 4) // 2
                    if i % 2 == 0 and not (first and i < 4):
                        sums_read(pair_even)
                    split_now = not last and FILL_END.get(i, 4) < 4
                    short = len(FILL[i][1]) < KT
                    if split_now and short:
                        proj_split(h + 1, 1 - j, FILL_END[i], bank(6))
                    dve.wait_ge(exped, 2 * s + 1)
                    col = 2 * (i % 2)
                    nc.vector.reciprocal(inv_sum[:, col:col + 1], exp_sum[:, col:col + 1])\
                        .then_inc(inv_ready, 1)
                    dve.wait_ge(exped, 2 * s + 2)
                    nc.vector.reciprocal(inv_raw[:], exp_sum[:, col + 1:col + 2]).then_inc(inv_step, 1)
                    dve.wait_ge(inv_step, s + 1)
                    nc.vector.tensor_tensor(inv_sum[:, col + 1:col + 2], neg_lam[:], inv_raw[:],
                                            ALU.mult).then_inc(inv_ready, 1)
                    dve.wait_ge(inv_ready, 2 * s + 2)
                    dve.wait_ge(scaled, s + 1)
                    nc.vector.scalar_tensor_tensor(pr[0][:], pr[1][:], inv_sum[:, col + 1:col + 2],
                                                   pr[0][:], ALU.mult, ALU.add).then_inc(diff_done, 1)
                    if split_now and not short:
                        proj_split(h + 1, 1 - j, FILL_END[i], bank(6))
                    if not (first and i == 0):
                        wt_split(s - 1, (i - 1) % TT)
                    if i % 2 == 1 and not (first and i == 1):
                        out_copy(PAIRS * h + (i - 3) // 2)
                    if i % 2 == 0 and not (first and i < 4):
                        if i < 4:
                            out_norm(pair_even, 1 - j, 2 + i // 2, 0)
                        else:
                            out_norm(pair_even, j, i // 2 - 2, 16 * h2)

            for r in range(2):
                dve.wait_ge(y_stored[r], 16 * GROUPS // 2)
            dve.wait_ge(distance_ld, 16)
            for g in range(4):
                proj_split(0, 0, g, bank(6 + g % 2))
            dve.wait_ge(lam_ready, 2)
            head(0, 0, first=True)
            with dve.Fori(0, 3) as m:
                head(m, 1)
                head(m + 1, 0)
            head(3, 1, last=True)
            last_pair = PAIRS * HEADS - 1
            wt_split(TT * HEADS - 1, TT - 1)
            sums_read(last_pair - 1)
            out_norm(last_pair - 1, 1, 2, 0)
            out_copy(last_pair)
            sums_read(last_pair)

            def branch_split(b):
                for t in range(KT):
                    if b == 0 and t == 4:
                        out_norm(last_pair, 1, 3, 0)
                    dve.wait_ge(b_his, KT * b + t + 1)
                    lo(b_lo[:, t, :], stage[t % 2][:] if b else x_tiles[:, t, :], b_hi[:, t, :], b_los)

            def gated(b, m, j, d, ns=range(2)):
                e = 2 * m + j
                for n in ns:
                    dst = merged[:, 4 * n:4 * n + 4, bass.ds(d, 1), :].rearrange("p t o c -> p t (o c)")
                    gate = sig[j][n]
                    dve.wait_ge(sig_done, 2 * e + n + 1)
                    dve.wait_ge(branch_done, 2 * e + n + 1)
                    src = bank(4 * j + 2 + n)
                    if b == 0:
                        nc.vector.tensor_tensor(dst, src.rearrange("p (t c) -> p t c", c=P),
                                                gate[:].rearrange("p (t c) -> p t c", c=P), ALU.mult)\
                            .then_inc(sig_read, 1)
                    else:
                        nc.vector.tensor_tensor(gate[:], src, gate[:], ALU.mult).then_inc(gated_done, 1)
                        dve.wait_ge(gated_done, 2 * d + n + 1)
                        nc.vector.tensor_tensor(dst, dst, gate[:].rearrange("p (t c) -> p t c", c=P),
                                                ALU.add).then_inc(sig_read, 1)

            for b in range(2):
                branch_split(b)
                with dve.Fori(0, KT // 2 - b) as m:
                    for j in range(2):
                        gated(b, m + KT // 2 * b, j, 2 * m + j)

            def row_lo(base, k, hi, lo_part):
                dve.wait_ge(w_hi, base + k + 1)
                dve.wait_ge(w_lo, base + k)
                lo(lo_part, row_buf[k % 4][:], hi, w_lo)
            def out_row(k):
                row_lo(N_OUT, k, wo_hi[:, k, :], wo_lo[:, k, :])

            def merged_lo(t, j):
                dve.wait_ge(m_hi, t + 1)
                lo(st_lo[j][:], one_mid(merged[:, bass.ds(t, 1), :, :]), st_hi[j][:], m_lo)

            def out_tile(m, j, more=True):
                t = 2 * m + j
                for n in range(2):
                    half = slice(n * HALF, (n + 1) * HALF)
                    dve.wait_ge(wo_done, 2 * t + n + 1)
                    dve.wait_ge(stage_in[j], 16 * (m + KT // 2 + STAGED + 1))
                    nc.vector.tensor_tensor(resid[:, bass.ds(t, 1), half].rearrange("p o n -> p (o n)"),
                                            bank(2 * j + n), stage[j][:, half], ALU.add)\
                        .then_inc(x1_done, 1)
                if more:
                    merged_lo(t + 2, j)
                normed(t + TT, j, tile_of(resid, t), 2)
                transposed_lo(t + TT, h_cols(h_lo, t), h_cols(h_hi, t), 4 + 2 * j)

            out_row(1)
            out_row(3)
            gated(1, KT - 1, 0, KT - 2)
            out_row(5)
            gated(1, KT - 1, 1, KT - 1, (0,))
            merged_lo(0, 0)
            out_row(7)
            gated(1, KT - 1, 1, KT - 1, (1,))
            merged_lo(1, 1)
            with dve.Fori(0, TT // 2 - 1) as m:
                for j in range(2):
                    out_tile(m, j)
            for j in range(2):
                out_tile(TT // 2 - 1, j, more=False)

            def hidden(i, e, parity):
                f = 2 * i + e
                for n in range(2):
                    dve.wait_ge(silu_done, 2 * f + n + 1)
                    dve.wait_ge(up_done, 2 * f + n + 1)
                    ge(dve, gu_his, 2 * f + n - 1)
                    ge(dve, gu_los, 2 * f + n - 1)
                    nc.vector.tensor_tensor(gu[n][:], bank(2 + n), silu[n][:], ALU.mult)\
                        .then_inc(gu_done, 1)
                    half = slice(n * HALF, (n + 1) * HALF)
                    dve.wait_ge(gu_his, 2 * f + n + 1)
                    lo(gu_lo[parity][:, e, half], gu[n][:], gu_hi[parity][:, e, half], gu_los)

            def down_add(i, ts=range(TT)):
                for t in ts:
                    for n in range(2):
                        dst = resid[:, t, n * HALF:(n + 1) * HALF]
                        dve.wait_ge(down_done, 2 * TT * i + 2 * t + n + 1)
                        nc.vector.tensor_tensor(dst, bank(4 + (2 * t + n) % 4), dst, ALU.add)\
                            .then_inc(down_added, 1)

            def ffn_turn(i, parity):
                hidden(i, 0, parity)
                down_add(i - 1)
                hidden(i, 1, parity)
            hidden(0, 0, 0)
            hidden(0, 1, 0)
            with dve.Fori(0, FFN_TURNS // 2) as m:
                ffn_turn(2 * m + 1, 1)
                ffn_turn(2 * m + 2, 0)
            def ple_lo(t, j, bank_x=6):
                transposed_lo(t + 2 * TT, lambda f: st_lo[j][:, f:f + 4, :],
                              lambda f: st_hi[j][:, f:f + 4, :], bank_x)

            def ple_lo_p(t, j, bank_p=6):
                dve.wait_ge(p_his, t + 1)
                lo(pt_lo[j][:], bank(bank_p, 0, PLE).rearrange("p (k c) -> p k c", k=2), pt_hi[j][:], p_los)

            def ple_tile(m, j, more=True):
                t = 2 * m + j
                if more:
                    normed(t + 1 + 2 * TT, 1 - j, tile_of(resid, t + 1), 3)
                    ple_lo(t + 1, 1 - j)
                for n in range(2):
                    half = slice(n * HALF, (n + 1) * HALF)
                    dve.wait_ge(pg_sig, 2 * t + n + 1)
                    dve.wait_ge(pp_done, 2 * t + n + 1)
                    nc.vector.tensor_tensor(pgate[:, half], bank(4 + n), pgate[:, half], ALU.mult)\
                        .then_inc(ple_mul, 1)
                if more:
                    ple_lo_p(t + 1, 1 - j)
                dve.wait_ge(ple_mul, 2 * t + 2)
                ge(dve, y_final, t - 1)
                nc.vector.tensor_tensor(x3[j][:], tile_of(resid, t), pgate[:], ALU.add)\
                    .then_inc(x3_done, 1)
                dve.wait_ge(f_rstd_ready, t + 1)
                dve.wait_ge(gain_in, 16 * 4)
                ge(dve, out_stored[j], 16 * m)
                nc.vector.scalar_tensor_tensor(stage[j][:], x3[j][:], f_rstd[:, j:j + 1], gain_final[:],
                                               ALU.mult, ALU.mult).then_inc(y_final, 1)

            last = FFN_TURNS - 1
            for t in range(TT):
                down_add(last, (t,))
                if t in (0, 2, 4, 6):
                    row_lo(N_PLE, t + 1, wpg_hi[:, t + 1, :], wpg_lo[:, t + 1, :])
                if t == 2:
                    normed(2 * TT, 0, tile_of(resid, 0), 3)
                if t == 5:
                    ple_lo(0, 0, 0)
                    ple_lo_p(0, 0, 2)
            row_lo(N_PLE, KT + 1, wpp_hi[:, 1, :], wpp_lo[:, 1, :])
            ple_tile(0, 0)
            ple_tile(0, 1)
            ple_tile(1, 0)
            with dve.Fori(1, TT // 2 - 1) as m:
                ple_tile(m, 1)
                ple_tile(m + 1, 0)
            ple_tile(TT // 2 - 1, 1, more=False)

        @block.tensor
        def _(pe):
            def passes(out_ap, a_hi, a_lo, b_hi_, b_lo_, first, last):
                terms = ((a_hi, b_hi_), (a_hi, b_lo_), (a_lo, b_hi_))
                for q, (a, b) in enumerate(terms):
                    ins = nc.tensor.matmul(out_ap, a, b, start=first and q == 0, stop=last and q == 2)
                return ins

            def weights(n):
                pe.wait_ge(w_hi, n + 1)
                pe.wait_ge(w_lo, n + 1)

            def slab_product(out_ap, slot, n, ks=range(KT)):
                half = slice(n * HALF, (n + 1) * HALF)
                for k in ks:
                    ins = passes(out_ap, st_hi[slot][:, k, :], st_lo[slot][:, k, :],
                                 h_hi[:, k, half], h_lo[:, k, half], k == 0, k == KT - 1)
                return ins

            def norm_transpose(t, j, bank0):
                pe.wait_ge(n_xn, t + 1)
                for n in range(2):
                    for f in range(4):
                        ins = nc.tensor.transpose(bank(bank0 + n, f * P, (f + 1) * P),
                                                  xn[j][:, (4 * n + f) * P:(4 * n + f + 1) * P], ident[:])
                    ins.then_inc(n_tp, 1)

            pe.wait_ge(ident_ld, 16)
            def first_transposes(ts):
                for t in ts:
                    ge(pe, n_lo, 2 * t - 2)
                    norm_transpose(t, t % 2, 2 * (t % 2))
            first_transposes(range(TT // 2 + 1))

            def project_u(g, j, n, first_bank=0):
                weights(g)
                ge(pe, u_los, 2 * g + n - 1)
                slab_product(bank(first_bank + n), j, n).then_inc(u_done, 1)

            def channel_dft(g, j):
                pe.wait_ge(u_los, 2 * g + 2)
                for c in range(4):
                    par, tile = c // 2, c % 2
                    ge(pe, fold_done, 4 * g + c - 1)
                    for far in range(2):
                        at = 2 * P * (tile + 2 * far) + par
                        tok = slice(at, at + 2 * P - 1, 2)
                        ins = passes(bank(2 + c % 2, 256 * far, 256 * far + 256),
                                     u_hi[j][:, tok], u_lo[j][:, tok], chan_hi[:], chan_lo[:],
                                     True, True)
                    ins.then_inc(chan_done, 1)

            def position_dft(g):
                pe.wait_ge(fold_los, 4 * g + 4)
                if isinstance(g, int) and g == 0:
                    pe.wait_ge(u_los, 2)
                ge(pe, combo_done, 4 * g)
                for par in range(2):
                    for trig in range(2):
                        for k_odd in range(2):
                            for tile in range(2):
                                c = 2 * par + tile
                                chans = slice(P * trig, P * (trig + 1))
                                tab = 4 * c + 2 * k_odd + trig
                                ins = passes(bank(4 + 2 * par + trig, KW * k_odd, KW * (k_odd + 1)),
                                             fold_hi[:, k_odd, c, chans], fold_lo[:, k_odd, c, chans],
                                             pos_hi[:, tab, :], pos_lo[:, tab, :],
                                             tile == 0, tile == 1)
                    ins.then_inc(pos_done, 1)

            pe.wait_ge(n_lo, TT)
            project_u(0, 0, 0, 4)
            first_transposes(range(TT // 2 + 1, TT))
            pe.wait_ge(n_lo, 2 * TT)
            project_u(0, 0, 1, 4)
            pe.wait_ge(dft_lo, 2)

            def fourier_group(g2, j, last=False):
                g = 2 * g2 + j
                if not last:
                    project_u(g + 1, 1 - j, 0)
                channel_dft(g, j)
                if not last:
                    project_u(g + 1, 1 - j, 1)
                position_dft(g)
            fourier_group(0, 0)
            with pe.Fori(0, 3) as m:
                fourier_group(m, 1)
                fourier_group(m + 1, 0)
            fourier_group(3, 1, last=True)

            def project(h, n_slab, slot, g, out_bank, ks=range(KT)):
                if ks[0] == 0:
                    weights(n_slab)
                ins = slab_product(bank(out_bank), slot, g % 2, ks)
                if ks[-1] == KT - 1:
                    ins.then_inc(proj_done, 1)

            def scores(s, j, i):
                ge(pe, biased, 2 * s)
                tok = slice(i * P, (i + 1) * P)
                for n in range(2):
                    half = slice(n * HALF, (n + 1) * HALF)
                    for q, (a, b) in enumerate(((q_hi, k_hi), (q_hi, k_lo), (q_lo, k_hi))):
                        for c in range(2):
                            rows = slice(HD * c, HD * (c + 1))
                            ins = nc.tensor.matmul(bank(2 * c + n), a[j][rows, tok], b[j][rows, half],
                                                   start=q == 0, stop=q == 2)
                            if n == 1 and q == 2:
                                ins.then_inc(score_done, 1)

            def transpose_diff(s, i, h=None):
                pe.wait_ge(diff_done, s + 1)
                for n in range(2):
                    ge(pe, wt_los, 2 * s + n - 1)
                    if h is not None:
                        pe.wait_ge(v_los, 2 * h + n + 1)
                    for f in range(4):
                        kt = 4 * n + f
                        ins = nc.tensor.transpose(bank(4 + n, f * P, (f + 1) * P),
                                                  probs[i % 2][0][:, kt * P:(kt + 1) * P], ident[:])
                    ins.then_inc(wt_done, 1)

            def values(pair_no, p):
                pe.wait_ge(wt_los, 4 * pair_no + 4)
                ge(pe, o_done, pair_no)
                for kt in range(TT):
                    ins = passes(bank(7, 0, 2 * P), v_hi[:, kt, :], v_lo[:, kt, :],
                                 wt_hi[p % 2][:, kt, :], wt_lo[p % 2][:, kt, :], kt == 0, kt == TT - 1)
                ins.then_inc(pv_done, 1)

            def sums_of_squares(pair_no):
                pe.wait_ge(o_squared, pair_no + 1)
                pe.wait_ge(o_copied, pair_no + 1)
                for q in range(2):
                    ins = nc.tensor.matmul(bank(7, 2 * P + q, 2 * P + q + 1), o_sq[:, q * P:(q + 1) * P],
                                           mean_col[:], start=True, stop=True)
                ins.then_inc(o_ss_done, 1)

            def spread_rstd(pair_no):
                pe.wait_ge(o_rstd_ready, pair_no + 1)
                for q in range(2):
                    ins = nc.tensor.transpose(bank(7, (2 + q) * P, (3 + q) * P),
                                              o_rstd[:, q:q + 1].to_broadcast([P, P]), ident[:])
                ins.then_inc(o_bcast, 1)

            def transpose_v(s):
                for n in range(2):
                    pe.wait_ge(wt_los, 2 * s + n - 3)
                    for f in range(4):
                        tok = (4 * n + f) * P
                        ins = nc.tensor.transpose(bank(4 + n, f * P, (f + 1) * P), v_t[:, tok:tok + P],
                                                  ident[:])
                    ins.then_inc(vt_done, 1)

            def fill(h2, j, i, part):
                h1 = 2 * h2 + j + 1
                g, ks = FILL[i]
                which = g // 2
                r = 3 * (j + 1) + which
                if ks[0] == 0 and part == 0:
                    pe.wait_ge(proj_hi, 6 * h1 + g)
                    pe.wait_ge(proj_lo, 4 * h1 + min(g, 4))
                mid = len(ks) // 2
                project(h1, N_ATTN + 6 * h2 + r, r % 2, g, 6, ks[mid:] if part else ks[:mid])

            def head(h2, j, first=False, last=False):
                h = 2 * h2 + j
                for i in range(TT):
                    s = TT * h + i
                    if i == 0:
                        pe.wait_ge(proj_lo, 4 * h + 4)
                    scores(s, j, i)
                    if i == 2:
                        pe.wait_ge(proj_hi, 6 * h + 6)
                        transpose_v(s)
                    pair_even = PAIRS * h + (i - 4) // 2
                    normed_pair = i % 2 == 0 and not (first and i < 4)
                    if not last:
                        fill(h2, j, i, 0)
                    if normed_pair:
                        sums_of_squares(pair_even)
                    if not last:
                        fill(h2, j, i, 1)
                    if not (first and i == 0):
                        transpose_diff(s - 1, (i - 1) % TT, h if i == 2 else None)
                    if i % 2 == 1 and not (first and i == 1):
                        if i == 3:
                            pe.wait_ge(v_los, 2 * h + 2)
                        values(PAIRS * h + (i - 3) // 2, (i - 3) // 2)
                    if normed_pair:
                        spread_rstd(pair_even)

            pe.wait_ge(combo_done, 4 * GROUPS)
            for g in range(6):
                if g >= 2:
                    pe.wait_ge(proj_hi, g - 1)
                    pe.wait_ge(proj_lo, min(g - 1, 4))
                project(0, N_ATTN + g // 2, (g // 2) % 2, g, 6 + g % 2)
            pe.wait_ge(proj_hi, 6)
            head(0, 0, first=True)
            with pe.Fori(0, 3) as m:
                head(m, 1)
                head(m + 1, 0)
            head(3, 1, last=True)
            def gate_product(m, j, n_slab, ns=range(2)):
                e = 2 * m + j
                weights(n_slab)
                for n in ns:
                    ge(pe, sig_done, 2 * e + n - 3)
                    slab_product(bank(4 * j + n), j, n).then_inc(gate_done, 1)

            last_pair = PAIRS * HEADS - 1
            transpose_diff(TT * HEADS - 1, TT - 1)
            pe.wait_ge(biased, 2 * TT * HEADS)
            sums_of_squares(last_pair - 1)
            gate_product(0, 0, N_GATE, (0,))
            spread_rstd(last_pair - 1)
            values(last_pair, 1)
            gate_product(0, 0, N_GATE, (1,))
            sums_of_squares(last_pair)

            def branch_product(m, j, n_slab, b=None):
                e = 2 * m + j
                weights(n_slab)
                for n in range(2):
                    half = slice(n * HALF, (n + 1) * HALF)
                    ge(pe, sig_read, 2 * e + n - 3)
                    if b == 0:
                        pe.wait_ge(o_done, PAIRS * HEADS)
                    for k in range(KT):
                        if b is not None and n == 0:
                            pe.wait_ge(b_los, KT * b + k + 1)
                        ins = passes(bank(4 * j + 2 + n), st_hi[j][:, k, :], st_lo[j][:, k, :],
                                     b_hi[:, k, half], b_lo[:, k, half], k == 0, k == KT - 1)
                    ins.then_inc(branch_done, 1)

            def gate_turn(m, b=None):
                for j in range(2):
                    if b == 0:
                        if j == 1:
                            gate_product(m, j, 4 * m + N_GATE + j, (0,))
                            spread_rstd(PAIRS * HEADS - 1)
                            gate_product(m, j, 4 * m + N_GATE + j, (1,))
                    else:
                        gate_product(m, j, 4 * m + N_GATE + j)
                for j in range(2):
                    branch_product(m, j, 4 * m + N_GATE + 2 + j, b if j == 0 else None)

            pe.wait_ge(wt_los, 2 * TT * HEADS)
            gate_turn(0, 0)
            with pe.Fori(1, KT // 2) as m:
                gate_turn(m)
            gate_turn(KT // 2, 1)
            with pe.Fori(KT // 2 + 1, KT - 1) as m:
                gate_turn(m)
            for j in range(2):
                branch_product(KT - 1, j, N_OUT - 4 + j)
            for j in range(2):
                gate_product(KT - 1, j, N_OUT - 2 + j)

            def out_tile(m, j, first=False):
                t = 2 * m + j
                pe.wait_ge(m_lo, t + 1)
                for n in range(2):
                    half = slice(n * HALF, (n + 1) * HALF)
                    ge(pe, x1_done, 2 * t + n - 3)
                    for k in range(KT):
                        if first and n == 0:
                            weights(N_OUT + k)
                        ins = passes(bank(2 * j + n), st_hi[j][:, k, :], st_lo[j][:, k, :],
                                     wo_hi[:, k, half], wo_lo[:, k, half], k == 0, k == KT - 1)
                    ins.then_inc(wo_done, 1)

            def out_transpose(t, j):
                ge(pe, n_lo, 2 * t + 2 * TT - 2)
                norm_transpose(t + TT, j, 4 + 2 * j)

            pe.wait_ge(sig_read, 4 * KT - 2)
            out_tile(0, 0, first=True)
            out_tile(0, 1)
            pe.wait_ge(sig_read, 4 * KT)
            out_transpose(0, 0)
            out_tile(1, 0)
            out_transpose(1, 1)
            with pe.Fori(1, TT // 2 - 1) as m:
                out_tile(m, 1)
                out_transpose(2 * m, 0)
                out_tile(m + 1, 0)
                out_transpose(2 * m + 1, 1)
            out_tile(TT // 2 - 1, 1)
            out_transpose(TT - 2, 0)

            def gate_side(i, e, n):
                weights(6 * i + N_FFN + 2 * e)
                ge(pe, silu_done, 4 * i + 2 * e + n - 1)
                slab_product(bank(n), 0, n).then_inc(g_done, 1)

            def up_side(i, e, n):
                weights(6 * i + N_FFN + 2 * e + 1)
                ge(pe, gu_done, 4 * i + 2 * e + n - 1)
                slab_product(bank(2 + n), 1, n).then_inc(up_done, 1)

            def hidden(i, e):
                for n in range(2):
                    gate_side(i, e, n)
                for n in range(2):
                    up_side(i, e, n)

            def down(i, parity, ts=range(TT)):
                weights(6 * i + N_FFN + 5)
                for t in ts:
                    if t == ts[0] or t == TT // 2:
                        pe.wait_ge(gu_los, 4 * i + (3 if t < TT // 2 else 4))
                    for n in range(2):
                        half = slice(n * HALF, (n + 1) * HALF)
                        ge(pe, down_added, 2 * TT * i + 2 * t + n - 3)
                        for e in range(2):
                            tok = slice(t * P, (t + 1) * P)
                            ins = passes(bank(4 + (2 * t + n) % 4), gu_hi[parity][:, e, tok],
                                         gu_lo[parity][:, e, tok], wd_hi[:, e, half], wd_lo[:, e, half],
                                         e == 0, e == 1)
                        ins.then_inc(down_done, 1)

            def ffn_turn(i, parity):
                hidden(i, 0)
                down(i - 1, 1 - parity)
                hidden(i, 1)
            pe.wait_ge(n_lo, 3 * TT)
            pe.wait_ge(x1_done, 2 * TT - 2)
            gate_side(0, 0, 0)
            out_transpose(TT - 1, 1)
            pe.wait_ge(x1_done, 2 * TT)
            up_side(0, 0, 0)
            pe.wait_ge(n_lo, 4 * TT)
            gate_side(0, 0, 1)
            up_side(0, 0, 1)
            hidden(0, 1)
            ffn_turn(1, 1)
            ffn_turn(2, 0)
            with pe.Fori(1, FFN_TURNS // 2) as m:
                ffn_turn(2 * m + 1, 1)
                ffn_turn(2 * m + 2, 0)

            def ple_transpose(t, j, bank_x=6, bank_p=6):
                ge(pe, p_los, t)
                norm_transpose(t + 2 * TT, j, bank_x)
                if bank_p != bank_x:
                    ple_transpose_p(t, j, bank_p)

            def ple_transpose_p(t, j, bank_p=6):
                if bank_p == 6:
                    pe.wait_ge(n_lo, 2 * t + 4 * TT + 1)
                if isinstance(t, int):
                    pe.wait_ge(p_in[j], 16 * (t // 2 + 1))
                else:
                    pe.wait_ge(p_in[j], 8 * (t - j) + 16)
                for k in range(2):
                    ins = nc.tensor.transpose(bank(bank_p, k * P, (k + 1) * P), p_raw[j][:, k * P:(k + 1) * P],
                                              ident[:])
                ins.then_inc(p_tp, 1)

            def ple_tile(m, j, more=True, first=False):
                t = 2 * m + j
                pe.wait_ge(n_lo, 2 * t + 4 * TT + 2)
                for n in range(2):
                    half = slice(n * HALF, (n + 1) * HALF)
                    ge(pe, pg_sig, 2 * t + n - 3)
                    for k in range(KT):
                        if first and n == 0:
                            weights(N_PLE + k)
                        ins = passes(bank(2 * j + n), st_hi[j][:, k, :], st_lo[j][:, k, :],
                                     wpg_hi[:, k, half], wpg_lo[:, k, half], k == 0, k == KT - 1)
                    ins.then_inc(pg_done, 1)
                if first:
                    pe.wait_ge(down_added, 2 * TT * FFN_TURNS)
                if more:
                    ple_transpose(t + 1, 1 - j)
                pe.wait_ge(p_los, t + 1)
                if first:
                    weights(N_PLE + KT + 1)
                for n in range(2):
                    half = slice(n * HALF, (n + 1) * HALF)
                    ge(pe, ple_mul, 2 * t + n - 1)
                    for k in range(2):
                        ins = passes(bank(4 + n), pt_hi[j][:, k, :], pt_lo[j][:, k, :],
                                     wpp_hi[:, k, half], wpp_lo[:, k, half], k == 0, k == 1)
                    ins.then_inc(pp_done, 1)
                if more:
                    ple_transpose_p(t + 1, 1 - j)

            down(FFN_TURNS - 1, 0, range(TT - 2))
            pe.wait_ge(gu_done, 2 * FT)
            ple_transpose(0, 0, 0, 2)
            down(FFN_TURNS - 1, 0, range(TT - 2, TT))
            ple_tile(0, 0, first=True)
            ple_tile(0, 1)
            ple_tile(1, 0)
            with pe.Fori(1, TT // 2 - 1) as m:
                ple_tile(m, 1)
                ple_tile(m + 1, 0)
            ple_tile(TT // 2 - 1, 1, more=False)


_INS = ['x', 'p', 'g_mix', 'w_in', 'lambda_q1', 'lambda_k1', 'lambda_q2', 'lambda_k2', 'g_subln',
        'w_fourier_out', 'w_attn_out', 'w_branch_gate', 'b_branch_gate', 'w_o', 'g_ffn',
        'w_ffn_gate', 'w_ffn_up', 'w_ffn_down', 'g_ple', 'w_ple_gate', 'w_ple_proj', 'g_final']


def shape_constants():
    import numpy as np
    row = np.arange(P)
    turn = 2 * np.pi * np.outer(row, row) / P
    chan = np.concatenate([np.cos(turn), np.sin(turn)], 1) / np.sqrt(P)
    pos = np.zeros((P, 16, KW))
    for parity in range(2):
        for tile in range(2):
            s = 2 * (P * tile + row) + parity
            for k_odd in range(2):
                k = 2 * np.arange(KW) + k_odd
                turn = 2 * np.pi * (np.outer(s, k) % SEQ) / SEQ
                for trig, table in enumerate((np.cos(turn), np.sin(turn))):
                    pos[:, 4 * (2 * parity + tile) + 2 * k_odd + trig] = table / np.sqrt(SEQ)
    distance = -np.abs(row[:, None] + ALIBI_0 - np.arange(ALIBI_W)[None])
    slope = 2.0 ** (-8.0 * np.arange(1, HEADS + 1) / HEADS)
    consts = np.concatenate([HD ** -0.5 / slope, slope, -slope])
    out = {"ident": np.eye(P), "chan_dft": chan, "pos_dft": pos, "distance": distance,
           "head_consts": np.repeat(consts[None], P, 0)}
    return {k: np.ascontiguousarray(v, dtype=np.float32) for k, v in out.items()}


def kernel(**inputs):
    import numpy as _np
    import concourse.bacc as _bacc
    from concourse import mybir as _mybir
    from concourse.bass_utils import run_bass_kernel_spmd as _run

    nc = _bacc.Bacc("TRN2", target_bir_lowering=False, num_devices=1)
    arrays = {f"in_{n}_dram": _np.ascontiguousarray(inputs[n]) for n in _INS}
    arrays.update({f"const_{n}_dram": v for n, v in shape_constants().items()})
    args = [nc.dram_tensor(n, a.shape, _mybir.dt.from_np(a.dtype), kind="ExternalInput").ap()
            for n, a in arrays.items()]
    args.append(nc.dram_tensor("out_0_dram", (1, SEQ, D), _mybir.dt.float32, kind="ExternalOutput").ap())
    encoder_layer(nc, *args)
    r = _run(nc, [arrays], core_ids=[0])
    return r.results[0]["out_0_dram"]
```

```python
from contextlib import ExitStack

import concourse.bass as bass
from concourse import mybir

F32 = mybir.dt.float32
F32R = mybir.dt.float32r
ALU = mybir.AluOpType
ACT = mybir.ActivationFunctionType

P = 128
SEQ = 1024
D = 1024
KT = D // P
TT = SEQ // P
HALF = 512
GROUPS = 8
HEADS = 8
HD = 64
D_FF = 2816
FT = D_FF // P
PLE = 256
EPS = 1e-6
LAMBDA_INIT = 0.8 - 0.6
KW = 130
QUART = 256
ALIBI_W = 2 * SEQ - P
ALIBI_0 = SEQ - P
PAIRS = HEADS // 2

N_FOURIER = 0
N_ATTN = N_FOURIER + GROUPS
N_GATE = N_ATTN + 3 * HEADS
N_OUT = N_GATE + 4 * KT
N_FFN = N_OUT + KT
FFN_TURNS = FT // 2
N_PLE = N_FFN + 6 * FFN_TURNS


def ge(eng, sem, value):
    if isinstance(value, int) and value <= 0:
        return
    eng.wait_ge(sem, value)


def encoder_layer(nc, x, p, g_mix, w_in, lambda_q1, lambda_k1, lambda_q2, lambda_k2, g_subln,
                  w_fourier_out, w_attn_out, w_branch_gate, b_branch_gate, w_o, g_ffn,
                  w_ffn_gate, w_ffn_up, w_ffn_down, g_ple, w_ple_gate, w_ple_proj, g_final,
                  ident_in, chan_dft_in, pos_dft_in, distance_in, head_consts_in, out):
    x_t = x[0].rearrange("(t p) d -> t p d", p=P)
    p_t = p[0, 0].rearrange("(t p) d -> t p d", p=P)
    out_t = out[0].rearrange("(t p) d -> t p d", p=P)
    branch_scr = [nc.dram_tensor(f"branch{b}_scratch", (KT, P, SEQ), F32, kind="Internal").ap()
                  for b in range(2)]

    ctx = ExitStack()
    with ctx:
        arena_bytes = 212736
        ctx.enter_context(nc.sbuf_tensor("arena", [P, arena_bytes // 4], F32))
        base = 16512

        def place(name, at, shape, dt=F32):
            size = 4
            for n in shape[1:]:
                size *= n
            assert at % 32 == 0 and at + size <= arena_bytes, (name, at, size)
            return nc.alloc_sbuf_tensor_at(name, shape, dt, offset=base + at)

        def sem(name):
            return ctx.enter_context(nc.semaphore(name))

        K = 1024
        R1 = 64 * K
        R2 = 128 * K
        RING = 160 * K
        MISC = 184 * K
        h_hi = place("h_hi", 0, [P, KT, SEQ], F32R)
        h_lo = place("h_lo", 32 * K, [P, KT, SEQ], F32R)
        raw = [place(f"raw{r}", RING + 4 * K * r, [P, KT, P]) for r in range(2)]
        st_hi = [place(f"st_hi{r}", RING + (8 + 4 * r) * K, [P, KT, P], F32R) for r in range(2)]
        st_lo = [place(f"st_lo{r}", RING + (16 + 4 * r) * K, [P, KT, P], F32R) for r in range(2)]
        raw_row = [place(f"raw_row{r}", RING + 4 * K * r, [P, D]) for r in range(2)]
        stage = [place(f"stage{r}", MISC + 4 * K * r, [P, SEQ]) for r in range(2)]
        gain = place("gain", MISC + 8 * K, [P, D])
        xn = [place(f"xn{r}", MISC + (12 + 4 * r) * K, [P, D]) for r in range(2)]
        distance = place("distance", MISC + 12 * K, [P, ALIBI_W])
        ident = place("ident", MISC + 20 * K, [P, P])
        C = MISC + 20 * K + 512
        gate_bias = place("gate_bias", C, [P, 16])
        head_consts = place("head_consts", C + 64, [P, 24])
        mean_sq = place("mean_sq", C + 160, [P, 2])
        shifted = place("shifted", C + 192, [P, 2])
        rstd = place("rstd", C + 224, [P, 2])
        neg_half = place("neg_half", C + 256, [P, 2])
        mean_col = place("mean_col", C + 288, [P, 1])
        eps_col = place("eps_col", C + 320, [P, 2])
        lam_exp = place("lam_exp", C + 352, [P, 2])
        neg_lam = place("neg_lam", C + 384, [P, 1])
        sub_gain = place("sub_gain", C + 416, [P, 1])
        row_max = place("row_max", C + 448, [P, 2])
        neg_max = place("neg_max", C + 480, [P, 4])
        exp_sum = place("exp_sum", C + 512, [P, 4])
        o_eps = place("o_eps", C + 544, [P, TT])
        o_mean_sq = place("o_mean_sq", C + 576, [P, 2])
        o_rstd = place("o_rstd", C + 608, [P, 2])
        o_shifted = place("o_shifted", C + 640, [P, 2])
        f_mean_sq = place("f_mean_sq", C + 672, [P, 2])
        f_shifted = place("f_shifted", C + 704, [P, 2])
        f_rstd = place("f_rstd", C + 736, [P, 2])
        inv_sum = place("inv_sum", C + 768, [P, 1])
        lam_rows = place("lam_rows", C + 800, [P, 4, HD])
        lam_dot = place("lam_dot", C + 1856, [P, 2])
        coef = place("coef", C + 1888, [P, 2])
        qscale = head_consts[:, 0:8]
        slope = head_consts[:, 8:16]
        neg_slope = head_consts[:, 16:24]

        x_tiles = place("x_tiles", R2, [P, TT, D])
        x_junk = place("x_junk", R1, [P, TT, D])
        x_mean, x_shifted, x_rstd = (place(f"x_col{r}", C + 1920 + 32 * r, [P, TT]) for r in range(3))

        u_hi = [place(f"u_hi{r}", R1 + 8 * K * r, [P, SEQ], F32R) for r in range(2)]
        u_lo = [place(f"u_lo{r}", R1 + 8 * K * r + 4 * K, [P, SEQ], F32R) for r in range(2)]
        fold_hi = place("fold_hi", R1 + 16 * K, [P, 2, 4, 256], F32R)
        fold_lo = place("fold_lo", R1 + 24 * K, [P, 2, 4, 256], F32R)
        TAB = 16 * KW * 4
        pos_hi = place("pos_hi", R1 + 32 * K, [P, 16, KW], F32R)
        pos_lo = place("pos_lo", R1 + 32 * K + TAB, [P, 16, KW], F32R)
        F0 = R1 + 32 * K + 2 * TAB
        chan_hi = place("chan_hi", F0, [P, 256], F32R)
        chan_lo = place("chan_lo", F0 + K, [P, 256], F32R)
        far_half = [place(f"far_half{r}", F0 + 2 * K + K * r, [P, 256]) for r in range(2)]
        folded = [place(f"folded{r}", F0 + 4 * K + 2 * K * r, [P, 2, 256]) for r in range(2)]
        sin_part = [place(f"sin_part{r}", F0 + 8 * K + 1056 * r, [P, 258]) for r in range(2)]
        combo = [[place(f"combo{a}{b}", F0 + 10 * K + 64 + 1056 * (2 * a + b), [P, 258])
                  for b in range(2)] for a in range(2)]
        y_out = [place(f"y_out{r}", F0 + 16 * K + 4 * K * r, [P, SEQ]) for r in range(2)]
        pos_raw = place("pos_raw", F0 + 16 * K, [P, 16, KW])
        chan_raw = place("chan_raw", F0 + 16 * K + 8 * K + 512, [P, 256])

        q2 = [place(f"q2_{r}", R1 + 20 * K * r, [P, 2, SEQ], F32R) for r in range(2)]
        k2 = [place(f"k2_{r}", R1 + 20 * K * r + 8 * K, [P, 2, SEQ], F32R) for r in range(2)]
        k_lo = [place(f"k_lo{r}", R1 + 20 * K * r + 16 * K, [P, SEQ], F32R) for r in range(2)]
        v_hi = place("v_hi", R1 + 40 * K, [P, TT, P], F32R)
        v_lo = place("v_lo", R1 + 44 * K, [P, TT, P], F32R)
        v_t = place("v_t", R1 + 48 * K, [P, SEQ])
        probs = [[place(f"probs{r}{c}", R1 + 52 * K + 4 * K * (2 * r + c), [P, SEQ])
                  for c in range(2)] for r in range(2)]
        wt_hi = place("wt_hi", R1 + 68 * K, [P, TT, 2 * P], F32R)
        wt_lo = place("wt_lo", R1 + 76 * K, [P, TT, 2 * P], F32R)
        o_raw = place("o_raw", R1 + 92 * K, [P, 2 * P])
        o_sq = place("o_sq", R1 + 93 * K, [P, 2 * P])

        b_hi = place("b_hi", R1, [P, KT, SEQ], F32R)
        b_lo = place("b_lo", R1 + 32 * K, [P, KT, SEQ], F32R)
        merged = place("merged", R2, [P, TT, KT, P])
        sig = [[place(f"sig{j}{n}", MISC + 12 * K + 2 * K * (2 * j + n), [P, HALF])
                for n in range(2)] for j in range(2)]
        wo_hi = place("wo_hi", R1, [P, KT, D], F32R)
        wo_lo = place("wo_lo", R1 + 32 * K, [P, KT, D], F32R)
        resid = place("resid", R2, [P, TT, D])

        gu_hi = [place(f"gu_hi{r}", R1 + 16 * K * r, [P, 2, SEQ], F32R) for r in range(2)]
        gu_lo = [place(f"gu_lo{r}", R1 + 16 * K * r + 8 * K, [P, 2, SEQ], F32R) for r in range(2)]
        wd_hi = place("wd_hi", R1 + 32 * K, [P, 2, D], F32R)
        wd_lo = place("wd_lo", R1 + 40 * K, [P, 2, D], F32R)
        silu = [place(f"silu{n}", R1 + 48 * K + 2 * K * n, [P, HALF]) for n in range(2)]
        gu = [place(f"gu{n}", R1 + 52 * K + 2 * K * n, [P, HALF]) for n in range(2)]

        wpg_hi = place("wpg_hi", 0, [P, KT, D], F32R)
        wpg_lo = place("wpg_lo", 32 * K, [P, KT, D], F32R)
        wpp_hi = place("wpp_hi", R1 + 16 * K, [P, 2, D], F32R)
        wpp_lo = place("wpp_lo", R1 + 24 * K, [P, 2, D], F32R)
        pt_hi = [place(f"pt_hi{r}", R1 + 56 * K + 2 * K * r, [P, 2, P], F32R) for r in range(2)]
        pt_lo = [place(f"pt_lo{r}", R1 + 57 * K + 2 * K * r, [P, 2, P], F32R) for r in range(2)]
        p_raw = [place(f"p_raw{r}", R1 + 60 * K + K * r, [P, PLE]) for r in range(2)]
        gain_final = place("gain_final", R1, [P, D])
        pgate = place("pgate", R1 + 4 * K, [P, D])
        x3 = [place(f"x3_{r}", R1 + 32 * K + 4 * K * r, [P, D]) for r in range(2)]
        sq_junk = place("sq_junk", R1 + 40 * K, [P, D])

        banks = ctx.enter_context(nc.psum_tensor("banks", [P, 8, HALF], F32))

        def bank(i, lo=0, hi=HALF):
            return banks[:, i, lo:hi]

        ident_ld = sem("ident_ld")
        consts_in = sem("consts_in")
        dft_in = sem("dft_in")
        dft_hi = sem("dft_hi")
        dft_lo = sem("dft_lo")
        gain_in = sem("gain_in")
        distance_ld = sem("distance_ld")
        raw_in = [sem(f"raw_in{r}") for r in range(2)]
        w_hi = sem("w_hi")
        w_lo = sem("w_lo")
        x_in = [sem(f"x_in{t}") for t in range(TT)]
        stage_in = [sem(f"stage_in{r}") for r in range(2)]
        pool_ready = sem("pool_ready")
        lam_dots = sem("lam_dots")
        lam_exped = sem("lam_exped")
        lam_ready = sem("lam_ready")
        n_sq = sem("n_sq")
        n_ms = sem("n_ms")
        n_rstd = sem("n_rstd")
        n_xn = sem("n_xn")
        n_tp = sem("n_tp")
        n_hi = sem("n_hi")
        n_lo = sem("n_lo")
        u_done = sem("u_done")
        u_his = sem("u_his")
        u_los = sem("u_los")
        chan_done = sem("chan_done")
        far_copied = sem("far_copied")
        fold_done = sem("fold_done")
        fold_his = sem("fold_his")
        fold_los = sem("fold_los")
        pos_done = sem("pos_done")
        sin_copied = sem("sin_copied")
        combo_done = sem("combo_done")
        y_quarters = sem("y_quarters")
        y_stored = [sem(f"y_stored{r}") for r in range(2)]
        proj_done = sem("proj_done")
        proj_hi = sem("proj_hi")
        proj_lo = sem("proj_lo")
        k_spread = sem("k_spread")
        vt_done = sem("vt_done")
        v_his = sem("v_his")
        v_los = sem("v_los")
        score_done = sem("score_done")
        biased = sem("biased")
        max_ready = sem("max_ready")
        exped = sem("exped")
        inv_step = sem("inv_step")
        coef_ready = sem("coef_ready")
        diff_done = sem("diff_done")
        wt_done = sem("wt_done")
        wt_his = sem("wt_his")
        wt_los = sem("wt_los")
        pv_done = sem("pv_done")
        o_squared = sem("o_squared")
        o_copied = sem("o_copied")
        o_ss_done = sem("o_ss_done")
        o_ss_read = sem("o_ss_read")
        o_ms_ready = sem("o_ms_ready")
        o_rstd_ready = sem("o_rstd_ready")
        o_bcast = sem("o_bcast")
        o_done = sem("o_done")
        o_stored = sem("o_stored")
        b_his = sem("b_his")
        b_los = sem("b_los")
        gate_done = sem("gate_done")
        branch_done = sem("branch_done")
        sig_done = sem("sig_done")
        gated_done = sem("gated_done")
        sig_read = sem("sig_read")
        m_hi = sem("m_hi")
        m_lo = sem("m_lo")
        wo_done = sem("wo_done")
        x1_done = sem("x1_done")
        g_done = sem("g_done")
        up_done = sem("up_done")
        silu_done = sem("silu_done")
        gu_done = sem("gu_done")
        gu_his = sem("gu_his")
        gu_los = sem("gu_los")
        down_done = sem("down_done")
        down_added = sem("down_added")
        p_in = [sem(f"p_in{r}") for r in range(2)]
        p_tp = sem("p_tp")
        p_his = sem("p_his")
        p_los = sem("p_los")
        pg_done = sem("pg_done")
        pp_done = sem("pp_done")
        pg_sig = sem("pg_sig")
        ple_mul = sem("ple_mul")
        x3_done = sem("x3_done")
        f_sq = sem("f_sq")
        f_ms = sem("f_ms")
        f_rstd_ready = sem("f_rstd_ready")
        y_final = sem("y_final")
        out_stored = [sem(f"out_stored{r}") for r in range(2)]

        block = ctx.enter_context(nc.Block())

        def slab_cols(w, c0):
            return w[:, bass.ds(c0, P)].rearrange("(t p) n -> p t n", p=P)

        def slab_rows(w, r0):
            return w[bass.ds(r0, P), :]

        def one(ap):
            return ap.rearrange("o p n -> (o p) n")

        def one_mid(ap):
            return ap.rearrange("p o a c -> p (o a) c")

        def in_order(i):
            return bank(i, 0, 2 * KW).rearrange("p (k m) -> p m k", k=2)[:, 0:KW - 1, :]

        own = (slice(0, HD), slice(HD, P))

        FILL = {0: (0, range(KT)), 1: (1, range(KT // 2)), 2: (1, range(KT // 2, KT)),
                3: (2, range(KT)), 4: (3, range(KT)), 5: (4, range(KT // 2)),
                6: (4, range(KT // 2, KT)), 7: (5, range(KT))}
        FILL_END = {i: g for i, (g, ks) in FILL.items() if ks[-1] == KT - 1}

        row_buf = stage + raw_row
        row_in = stage_in + raw_in
        STAGED = KT // 4
        DOWN_STAGED = KT // 2 + STAGED + TT // 2
        FIRST_STAGED = {N_OUT: KT // 2, N_PLE: DOWN_STAGED + FFN_TURNS}
        FIRST_RAW = {N_OUT: N_OUT // 2, N_PLE: N_FFN // 2 - STAGED + 2 * FFN_TURNS}

        def row_landed(base, k):
            first = (FIRST_STAGED if k % 4 < 2 else FIRST_RAW)[base]
            return row_in[k % 4], 16 * (first + k // 4 + 1)

        @block.sync
        def _(sp):
            def load_slab(turn, slot, src):
                ge(sp, w_hi, 2 * turn + slot - 1)
                ge(sp, w_lo, 2 * turn + slot - 1)
                sp.dma_start(raw[slot][:], src).then_inc(raw_in[slot], 16)

            def load_row(base, k, src):
                if k >= 2:
                    back = 5 if base == N_PLE and k < 4 else 3
                    sp.wait_ge(w_hi, base + k - back)
                    sp.wait_ge(w_lo, base + k - back)
                sp.dma_start(row_buf[k % 4][:], src).then_inc(row_in[k % 4], 16)

            sp.dma_start(x_tiles[:, 0, :], x_t[0]).then_inc(x_in[0], 16)
            sp.dma_start(gain[:], g_mix.to_broadcast([P, D])).then_inc(gain_in, 16)
            sp.dma_start(ident[:], ident_in).then_inc(ident_ld, 16)
            for t in range(1, TT):
                sp.dma_start(x_tiles[:, t, :], x_t[t]).then_inc(x_in[t], 16)
                if t in (3, 6):
                    load_slab(0, t // 3 - 1, slab_cols(w_in[0], (t // 3 - 1) * P))
            sp.wait_ge(n_xn, 3)
            sp.dma_start(chan_raw[:], chan_dft_in).then_inc(dft_in, 16)
            sp.dma_start(pos_raw[:], pos_dft_in).then_inc(dft_in, 16)
            sp.dma_start(head_consts[:], head_consts_in).then_inc(consts_in, 16)
            sp.dma_start(sub_gain[:], g_subln.rearrange("a e -> e a"),
                         allow_slow_non_contiguous=True).then_inc(consts_in, 16)
            for r, lam in enumerate((lambda_q1, lambda_k1, lambda_q2, lambda_k2)):
                sp.dma_start(lam_rows[:, r, :], lam.to_broadcast([P, HD])).then_inc(consts_in, 16)
            sp.dma_start(gate_bias[:], b_branch_gate[0].rearrange("(c p) -> p c", p=P),
                         allow_slow_non_contiguous=True).then_inc(consts_in, 16)
            sp.wait_ge(n_xn, TT)
            sp.wait_ge(n_tp, 2 * TT)
            sp.dma_start(gain[:], g_ffn.to_broadcast([P, D])).then_inc(gain_in, 16)
            sp.dma_start(distance[:], distance_in).then_inc(distance_ld, 16)

            with sp.Fori(1, GROUPS // 2) as m:
                for j in range(2):
                    load_slab(m, j, slab_cols(w_in[0], (2 * m + j) * P))

            with sp.Fori(0, PAIRS) as m:
                for s in range(6):
                    j, which = s // 3, s % 3
                    load_slab(3 * m + N_ATTN // 2 + s // 2, s % 2,
                              slab_cols(w_in[0], (2 * m + GROUPS + HEADS * which + j) * P))

            def gate_slabs(m, b, order=(0, 1)):
                w_b = (w_fourier_out[0], w_attn_out[0])[b]
                for place_, what in enumerate(order):
                    for j in range(2):
                        turn = 2 * m + (N_GATE // 2 + KT * b + place_)
                        if what == 0:
                            load_slab(turn, j, slab_cols(w_branch_gate[0], (2 * m + j + KT * b) * P))
                        else:
                            load_slab(turn, j, slab_cols(w_b, (2 * m + j) * P))

            def branch_tile(b, t):
                if t >= 2:
                    sp.wait_ge(b_his, KT * b + t - 1)
                    sp.wait_ge(b_los, KT * b + t - 1)
                sp.dma_start(stage[t % 2][:], branch_scr[b][t]).then_inc(stage_in[t % 2], 16)

            for b in range(2):
                if b == 0:
                    load_slab(N_GATE // 2, 0, slab_cols(w_branch_gate[0], 0))
                    load_slab(N_GATE // 2, 1, slab_cols(w_branch_gate[0], P))
                    for r in range(2):
                        load_slab(N_GATE // 2 + 1, r, slab_cols(w_fourier_out[0], r * P))
                    for r in range(2):
                        sp.wait_ge(y_stored[r], 16 * GROUPS // 2)
                    sp.wait_ge(pv_done, PAIRS * HEADS)
                    for t in range(KT):
                        if t == KT - 1:
                            sp.wait_ge(o_done, PAIRS * HEADS)
                        sp.dma_start(x_tiles[:, t, :], branch_scr[b][t]).then_inc(x_in[t], 16)
                else:
                    sp.wait_ge(o_stored, 16 * HEADS)
                    for r in range(2):
                        branch_tile(b, r)
                    gate_slabs(0, b, (0,))
                    for t in range(2, KT):
                        if t == 4 or t == 6:
                            load_slab(N_GATE // 2 + KT + 1, t // 2 - 2,
                                      slab_cols(w_attn_out[0], (t // 2 - 2) * P))
                        branch_tile(b, t)
                with sp.Fori(1, KT // 2 - b) as m:
                    gate_slabs(m, b)
            sp.wait_ge(b_his, 2 * KT)
            sp.wait_ge(b_los, 2 * KT)
            for k in range(2):
                load_row(N_OUT, k, slab_rows(w_o[0], k * P))
            gate_slabs(KT // 2 - 1, 1, (1, 0))

            for k in range(2, KT):
                load_row(N_OUT, k, slab_rows(w_o[0], k * P))
            for t in range(2):
                sp.wait_ge(w_hi, N_OUT + 5 + t)
                sp.wait_ge(w_lo, N_OUT + 5 + t)
                sp.dma_start(stage[t][:], x_t[t]).then_inc(stage_in[t], 16)
            def ffn_slabs(i, e):
                for slot, w in enumerate((w_ffn_gate[0], w_ffn_up[0])):
                    src = slab_cols(w, (2 * i + e) * P)
                    held = 6 * i + N_FFN + 2 * e + slot - (2 if e else 4)
                    ge(sp, w_hi, held + 1)
                    ge(sp, w_lo, held + 1)
                    sp.nop(nofuse=True)
                    sp.dma_start(raw[slot][:], src).then_inc(raw_in[slot], 16)

            def down_rows(i, first=False):
                for e in range(2):
                    src = slab_rows(w_ffn_down[0], (2 * i + e) * P)
                    if not first:
                        sp.wait_ge(w_hi, 6 * i + N_FFN + e - 1)
                        sp.wait_ge(w_lo, 6 * i + N_FFN + e - 1)
                    sp.dma_start(stage[e][:], src).then_inc(stage_in[e], 16)

            def ffn_turn(i):
                ffn_slabs(i, 0)
                down_rows(i)
                ffn_slabs(i, 1)
            load_slab(N_FFN // 2, 0, slab_cols(w_ffn_gate[0], 0))
            load_slab(N_FFN // 2, 1, slab_cols(w_ffn_up[0], 0))
            for t in range(2, TT):
                sp.wait_ge(x1_done, 2 * (t - 1))
                sp.dma_start(stage[t % 2][:], x_t[t]).then_inc(stage_in[t % 2], 16)
            ffn_slabs(0, 1)
            sp.wait_ge(x1_done, 2 * TT)
            down_rows(0, first=True)
            sp.wait_ge(n_xn, 2 * TT)
            sp.dma_start(gain[:], g_ple.to_broadcast([P, D])).then_inc(gain_in, 16)
            for t in range(2):
                sp.dma_start(p_raw[t][:], p_t[t]).then_inc(p_in[t], 16)
            with sp.Fori(1, FFN_TURNS) as i:
                ffn_turn(i)

            for k in (2, 3, 0, 1, 4, 5, 6, 7):
                if k < 2:
                    sp.wait_ge(w_hi, N_PLE - 1 + k)
                    sp.wait_ge(w_lo, N_PLE - 1 + k)
                load_row(N_PLE, k, slab_rows(w_ple_gate[0], k * P))
            for k in range(2):
                load_row(N_PLE, KT + k, slab_rows(w_ple_proj[0], k * P))
            sp.wait_ge(down_done, 16 * FFN_TURNS)
            sp.dma_start(gain_final[:], g_final.rearrange("(a d) -> a d", a=1).to_broadcast([P, D]))\
              .then_inc(gain_in, 16)
            for t in range(TT):
                if t + 2 < TT:
                    sp.wait_ge(p_tp, t + 1)
                    sp.dma_start(p_raw[t % 2][:], p_t[t + 2]).then_inc(p_in[t % 2], 16)
                sp.wait_ge(y_final, t + 1)
                sp.dma_start(out_t[t], stage[t % 2][:]).then_inc(out_stored[t % 2], 16)
            for r in range(2):
                sp.wait_ge(out_stored[r], 16 * TT // 2)

        @block.gpsimd
        def _(pool):
            def split_lo(turn, slot, dst=None, src=None):
                pool.wait_ge(w_hi, 2 * turn + slot + 1)
                src = raw[slot][:] if src is None else src
                hi, lo = (st_hi[slot][:], st_lo[slot][:]) if dst is None else dst
                nc.gpsimd.tensor_tensor(lo, src, hi.bitcast(F32), ALU.subtract).then_inc(w_lo, 1)

            def row_lo(base, k, hi, lo):
                n = base + k
                pool.wait_ge(w_lo, n)
                split_lo(n // 2, n % 2, (hi, lo), row_buf[k % 4][:])

            def inv_rms(count, means, shifted, outs, summed, shift_ready, done, eps=eps_col):
                width = means.shape[1]
                pool.wait_ge(summed, count)
                nc.gpsimd.tensor_tensor(shifted, means, eps[:, 0:width], ALU.add)\
                    .then_inc(shift_ready, 1)
                pool.wait_ge(shift_ready, count)
                nc.gpsimd.tensor_tensor(outs, shifted, neg_half[:, 0:width], ALU.pow)\
                    .then_inc(done, 1)

            def tile_norm(t, j):
                sl = slice(j, j + 1)
                inv_rms(t + 1, mean_sq[:, sl], shifted[:, sl], rstd[:, sl], n_sq, n_ms, n_rstd)

            nc.gpsimd.memset(neg_half[:], -0.5).then_inc(pool_ready, 1)
            nc.gpsimd.memset(mean_col[:], 1.0 / P).then_inc(pool_ready, 1)
            nc.gpsimd.memset(eps_col[:], EPS).then_inc(pool_ready, 1)
            pool.wait_ge(pool_ready, 3)
            for t in range(TT):
                col = slice(t, t + 1)
                inv_rms(t + 1, x_mean[:, col], x_shifted[:, col], x_rstd[:, col], n_sq, n_ms, n_rstd)
                if t == TT // 2:
                    split_lo(0, 0)
            split_lo(0, 1)

            def mirror(g2, j):
                g = 2 * g2 + j
                pool.wait_ge(combo_done, 4 * g + 4)
                ge(pool, y_stored[j], 16 * g2)
                (em, om), (ep, op) = combo
                y = y_out[j]
                near, back = slice(0, QUART), slice(QUART, 0, -1)
                quarters = ((em, om, near, ALU.add), (ep, op, back, ALU.subtract),
                            (em, om, near, ALU.subtract), (ep, op, back, ALU.add))
                for q, (a, b, part, op_) in enumerate(quarters):
                    nc.gpsimd.tensor_tensor(y[:, q * QUART:(q + 1) * QUART], a[:, part], b[:, part], op_)\
                        .then_inc(y_quarters, 1)
                pool.wait_ge(y_quarters, 4 * g + 4)
                pool.dma_start(one(branch_scr[0][bass.ds(g, 1)]), y[:]).then_inc(y_stored[j], 16)

            def fourier_pair(g2):
                for j in range(2):
                    split_lo(g2 + 1, j)
                    mirror(g2, j)
            fourier_pair(0)
            with pool.Fori(1, GROUPS // 2) as m:
                fourier_pair(m)

            split_lo(5, 0)
            split_lo(5, 1)

            def sub_norm(count, p):
                inv_rms(count, o_mean_sq[:], o_shifted[:], o_rstd[:], o_ss_read, o_ms_ready,
                        o_rstd_ready, o_eps[:, 2 * p:2 * p + 2])

            def store_o(h, j):
                pool.wait_ge(o_done, PAIRS * (h + 1))
                pool.dma_start(one(branch_scr[1][bass.ds(h, 1)]), stage[j][:])\
                    .then_inc(o_stored, 16)

            def head(h2, j, first=False, last=False):
                h = 2 * h2 + j
                slab = lambda s: (3 * h2 + 6 + (3 * j + s) // 2, (3 * j + s) % 2)
                split_lo(*slab(0))
                if not first:
                    sub_norm(PAIRS * h - 1, 2)
                    sub_norm(PAIRS * h, 3)
                if not last:
                    split_lo(*slab(1))
                if not first:
                    store_o(h - 1, 1 - j)
                sub_norm(PAIRS * h + 1, 0)
                if not last:
                    split_lo(*slab(2))
                sub_norm(PAIRS * h + 2, 1)
            head(0, 0, first=True)
            with pool.Fori(0, 3) as m:
                head(m, 1)
                head(m + 1, 0)
            head(3, 1, last=True)
            sub_norm(PAIRS * HEADS - 1, 2)
            split_lo(N_GATE // 2 + 1, 0)
            sub_norm(PAIRS * HEADS, 3)
            store_o(HEADS - 1, 1)

            split_lo(N_GATE // 2 + 1, 1)
            with pool.Fori(2, 2 * KT) as e:
                for s in range(2):
                    split_lo(e + N_GATE // 2, s)

            for k in range(0, KT, 2):
                row_lo(N_OUT, k, wo_hi[:, k, :], wo_lo[:, k, :])
            with pool.Fori(TT // 2, TT - 1) as m:
                for j in range(2):
                    tile_norm(2 * m + j, j)
            for j in range(2):
                tile_norm(2 * TT - 2 + j, j)
                split_lo(N_FFN // 2, j)

            def ffn_turn(i, first=False):
                for e in range(1 if first else 0, 2):
                    for s in range(2):
                        split_lo(3 * i + N_FFN // 2 + e, s)
                for e in range(2):
                    split_lo(3 * i + N_FFN // 2 + 2, e, (wd_hi[:, e, :], wd_lo[:, e, :]), stage[e][:])
            ffn_turn(0, first=True)
            with pool.Fori(1, FFN_TURNS) as i:
                ffn_turn(i)

            for k in range(0, KT, 2):
                row_lo(N_PLE, k, wpg_hi[:, k, :], wpg_lo[:, k, :])
                if k == 0:
                    tile_norm(2 * TT, 0)
            row_lo(N_PLE, KT, wpp_hi[:, 0, :], wpp_lo[:, 0, :])

            def final_norm(t, j):
                sl = slice(j, j + 1)
                inv_rms(t + 1, f_mean_sq[:, sl], f_shifted[:, sl], f_rstd[:, sl], f_sq, f_ms, f_rstd_ready)
            tile_norm(2 * TT + 1, 1)
            final_norm(0, 0)
            with pool.Fori(0, TT // 2 - 1) as m:
                tile_norm(2 * m + 2 * TT + 2, 0)
                final_norm(2 * m + 1, 1)
                tile_norm(2 * m + 2 * TT + 3, 1)
                final_norm(2 * m + 2, 0)
            final_norm(TT - 1, 1)

        @block.scalar
        def _(act):
            def split_hi(turn, slot, free=None):
                act.wait_ge(raw_in[slot], 16 * (turn + 1))
                if free is not None:
                    ge(act, *free)
                nc.scalar.copy(st_hi[slot][:], raw[slot][:]).then_inc(w_hi, 1)

            def row_hi(base, k, free, dst):
                act.wait_ge(*row_landed(base, k))
                ge(act, *free)
                nc.scalar.copy(dst, row_buf[k % 4][:]).then_inc(w_hi, 1)

            def square(src, junk, mean, done):
                nc.scalar.activation(junk, src, ACT.Square, scale=D ** -0.5, accum_out=mean)\
                    .then_inc(done, 1)

            def split_wait():
                act.nop(nofuse=True)

            def transposed_hi(t, dst, bank0):
                for n in range(2):
                    act.wait_ge(n_tp, 2 * t + n + 1)
                    nc.scalar.copy(dst(4 * n), bank(bank0 + n).rearrange("p (f c) -> p f c", f=4))\
                        .then_inc(n_hi, 1)

            def h_cols(t):
                return lambda f: h_hi[:, f:f + 4, bass.ds(t * P, P)]

            def norm_square(t):
                act.wait_ge(x_in[t], 16)
                square(x_tiles[:, t, :], x_junk[:, t, :], x_mean[:, t:t + 1], n_sq)
            for t in range(3):
                norm_square(t)
            for t in range(TT):
                transposed_hi(t, h_cols(t), 2 * (t % 2))
                if t + 3 < TT:
                    norm_square(t + 3)
                if t == 1:
                    split_hi(0, 0)
                if t == TT - 2:
                    split_hi(0, 1)
            act.wait_ge(dft_in, 32)
            nc.scalar.copy(chan_hi[:], chan_raw[:]).then_inc(dft_hi, 1)
            nc.scalar.copy(pos_hi[:], pos_raw[:]).then_inc(dft_hi, 1)
            act.wait_ge(lam_dots, 2)
            nc.scalar.activation(lam_exp[:], lam_dot[:], ACT.Exp).then_inc(lam_exped, 1)

            def u_evac(g, j, n, first_bank=0):
                act.wait_ge(u_done, 2 * g + n + 1)
                nc.scalar.copy(u_hi[j][:, n * HALF:(n + 1) * HALF], bank(first_bank + n)).then_inc(u_his, 1)

            def fold_split(g, c):
                act.wait_ge(fold_done, 4 * g + c + 1)
                ge(act, pos_done, 2 * g)
                nc.scalar.copy(fold_hi[:, :, c, :], folded[c % 2][:]).then_inc(fold_his, 1)

            def fourier_group(g2, j, last=False):
                g = 2 * g2 + j
                split_hi(g2 + 1, j, (u_done, 2 * g + 2))
                if not last:
                    u_evac(g + 1, 1 - j, 0)
                for c in range(4):
                    act.wait_ge(chan_done, 4 * g + c + 1)
                    ge(act, fold_done, 4 * g + c - 1)
                    nc.scalar.copy(far_half[c % 2][:], bank(2 + c % 2, 256, 512)).then_inc(far_copied, 1)
                    if c >= 1:
                        fold_split(g, c - 1)
                fold_split(g, 3)
                if not last:
                    u_evac(g + 1, 1 - j, 1)
                for par in range(2):
                    act.wait_ge(pos_done, 2 * g + par + 1)
                    ge(act, combo_done, 4 * g)
                    nc.scalar.copy(sin_part[par][:].rearrange("p (m k) -> p m k", k=2),
                                   in_order(5 + 2 * par)).then_inc(sin_copied, 1)

            u_evac(0, 0, 0, 4)
            u_evac(0, 0, 1, 4)
            fourier_group(0, 0)
            with act.Fori(0, 3) as m:
                fourier_group(m, 1)
                fourier_group(m + 1, 0)
            fourier_group(3, 1, last=True)

            def proj_evac(h, j, g, src):
                which, n = g // 2, g % 2
                half = slice(n * HALF, (n + 1) * HALF)
                act.wait_ge(proj_done, 6 * h + g + 1)
                if which == 0:
                    split_wait()
                    for c in range(2):
                        ins = nc.scalar.activation(q2[j][own[c], c, half], src[own[c], :], ACT.Copy,
                                                   scale=qscale[own[c], bass.ds(h, 1)])
                elif which == 1:
                    for c in range(2):
                        ins = nc.scalar.copy(k2[j][own[c], c, half], src[own[c], :])
                else:
                    ins = nc.scalar.copy(v_t[:, half], src)
                ins.then_inc(proj_hi, 1)

            def spread_k(h, j, c):
                act.wait_ge(proj_hi, 6 * h + 4)
                nc.scalar.copy(k2[j][own[1 - c], c, :], k2[j][own[c], c, :].bitcast(F32))\
                    .then_inc(k_spread, 1)

            def wt_evac(s, i):
                for n in range(2):
                    act.wait_ge(wt_done, 2 * s + n + 1)
                    nc.scalar.copy(wt_hi[:, 4 * n:4 * n + 4, (i % 2) * P:(i % 2 + 1) * P],
                                   bank(4 + n).rearrange("p (f c) -> p f c", f=4)).then_inc(wt_his, 1)

            def value_hi(h, k):
                act.wait_ge(vt_done, 2 * h + k + 1)
                nc.scalar.copy(v_hi[:, 4 * k:4 * k + 4, :],
                               bank(4 + k).rearrange("p (f c) -> p f c", f=4)).then_inc(v_his, 1)

            def out_square(pair_no):
                act.wait_ge(pv_done, pair_no + 1)
                ge(act, o_ss_done, pair_no)
                nc.scalar.activation(o_sq[:], bank(7, 0, 2 * P), ACT.Square).then_inc(o_squared, 1)
                ge(act, o_done, pair_no)
                nc.scalar.activation(o_raw[:], bank(7, 0, 2 * P), ACT.Copy, scale=sub_gain[:])\
                    .then_inc(o_copied, 1)

            def head(h2, j, first=False, last=False):
                h = 2 * h2 + j
                slab = lambda r: (3 * h2 + 6 + (3 * j + r) // 2, (3 * j + r) % 2)
                for i in range(TT):
                    s = TT * h + i
                    pr = probs[i % 2]
                    if i == 0:
                        split_hi(*slab(0), (proj_done, 6 * h + 6))
                    if i == 3 and not last:
                        split_hi(*slab(1), (proj_done, 6 * h + 8))
                    if i == 5 and not last:
                        split_hi(*slab(2), (proj_done, 6 * h + 10))
                    early = i % 2 == 0
                    before = not (first and i == 0)
                    if early and before:
                        wt_evac(s - 1, (i - 1) % TT)
                    for c in range(2):
                        col = slice(2 * (i % 2) + c, 2 * (i % 2) + c + 1)
                        act.wait_ge(max_ready, 2 * s + c + 1)
                        ge(act, coef_ready, s - 1)
                        split_wait()
                        nc.scalar.activation(pr[c][:], pr[c][:], ACT.Exp, bias=neg_max[:, col],
                                             scale=slope[:, bass.ds(h, 1)], accum_out=exp_sum[:, col])\
                            .then_inc(exped, 1)
                    if not last and i in (5, 6):
                        spread_k(h + 1, 1 - j, i - 5)
                    if not last and i in FILL_END:
                        proj_evac(h + 1, 1 - j, FILL_END[i], bank(6))
                    if i % 2 == 1 and not (first and i == 1):
                        out_square(PAIRS * h + (i - 3) // 2)
                    if not early:
                        wt_evac(s - 1, (i - 1) % TT)
                    if i == 2:
                        for k in range(2):
                            value_hi(h, k)

            for r in range(2):
                act.wait_ge(y_stored[r], 16 * GROUPS // 2)
            for g in range(6):
                proj_evac(0, 0, g, bank(g if g < 2 else 6 + g % 2))
                if g == 1:
                    split_hi(5, 0, (proj_done, 2))
                if g == 3:
                    split_hi(5, 1, (proj_done, 4))
                    for c in range(2):
                        spread_k(0, 0, c)
            head(0, 0, first=True)
            with act.Fori(0, 3) as m:
                head(m, 1)
                head(m + 1, 0)
            head(3, 1, last=True)
            wt_evac(TT * HEADS - 1, TT - 1)
            out_square(PAIRS * HEADS - 1)

            def sigmoids(m, j, ns=range(2)):
                e = 2 * m + j
                for n in ns:
                    act.wait_ge(gate_done, 2 * e + n + 1)
                    ge(act, sig_read, 2 * e + n - 3)
                    split_wait()
                    src = bank(6 if isinstance(e, int) and e == n == 0 else 4 * j + n)
                    nc.scalar.activation(sig[j][n][:], src, ACT.Sigmoid,
                                         bias=gate_bias[:, bass.ds(e, 1)]).then_inc(sig_done, 1)

            def branch_split(b):
                if b == 0:
                    act.wait_ge(pv_done, PAIRS * HEADS)
                else:
                    act.wait_ge(branch_done, 2 * KT)
                def gates(j):
                    sigmoids(KT // 2 * b, j)
                    split_hi(KT * b + N_GATE // 2 + 1, j)
                if b == 0:
                    gates(0)
                for t in range(KT):
                    if b == 0:
                        act.wait_ge(x_in[t], 32)
                        nc.scalar.copy(b_hi[:, t, :], x_tiles[:, t, :]).then_inc(b_his, 1)
                    else:
                        act.wait_ge(stage_in[t % 2], 16 * (t // 2 + 1))
                        nc.scalar.copy(b_hi[:, t, :], stage[t % 2][:]).then_inc(b_his, 1)
                    if t == KT - 1 or t == KT // 2 - 1 and b == 1:
                        gates(t // (KT // 2))

            def gate_turn(m, split=True):
                turn = 2 * m + N_GATE // 2
                if split:
                    for j in range(2):
                        sigmoids(m, j)
                        split_hi(turn + 1, j)
                for j in range(2):
                    split_hi(turn + 2, j, (branch_done, 4 * m + 2 * j + 2))

            branch_split(0)
            gate_turn(0, split=False)
            with act.Fori(1, KT // 2) as m:
                gate_turn(m)
            branch_split(1)
            gate_turn(KT // 2, split=False)
            with act.Fori(KT // 2 + 1, KT - 1) as m:
                gate_turn(m)
            for j in range(2):
                split_hi(N_OUT // 2 - 1, j, (branch_done, 4 * KT - 2 + 2 * j))

            for k in range(KT):
                row_hi(N_OUT, k, (branch_done, 4 * KT), wo_hi[:, k, :])
                if k == KT // 2 - 1:
                    sigmoids(KT - 1, 0)

            def merged_hi(t, j, free):
                ge(act, *free)
                nc.scalar.copy(st_hi[j][:], one_mid(merged[:, bass.ds(t, 1), :, :])).then_inc(m_hi, 1)

            def out_tile(m, j, more=True):
                t = 2 * m + j
                act.wait_ge(x1_done, 2 * t + 2)
                ge(act, n_tp, 2 * t + 2 * TT - 2)
                split_wait()
                square(resid[:, bass.ds(t, 1), :].rearrange("p o n -> p (o n)"), xn[j][:],
                       mean_sq[:, j:j + 1], n_sq)
                if more:
                    merged_hi(t + 2, j, (wo_done, 2 * t + 2))
                else:
                    split_hi(N_FFN // 2 - STAGED, j, (wo_done, 2 * t + 2))
                transposed_hi(t + TT, h_cols(t), 4 + 2 * j)

            sigmoids(KT - 1, 1, (0,))
            act.wait_ge(sig_read, 4 * KT - 1)
            merged_hi(0, 0, (gate_done, 4 * KT - 2))
            sigmoids(KT - 1, 1, (1,))
            merged_hi(1, 1, (gate_done, 4 * KT))
            out_tile(0, 0)
            act.wait_ge(sig_read, 4 * KT)
            out_tile(0, 1)
            with act.Fori(1, TT // 2 - 1) as m:
                for j in range(2):
                    out_tile(m, j)
            for j in range(2):
                out_tile(TT // 2 - 1, j, more=False)

            def ffn_turn(i, parity, last=False):
                turn = 2 * i + N_FFN // 2 - STAGED
                for e in range(2):
                    f = 2 * i + e
                    for n in range(2):
                        act.wait_ge(g_done, 2 * f + n + 1)
                        ge(act, gu_done, 2 * f + n - 1)
                        nc.scalar.activation(silu[n][:], bank(n), ACT.Silu).then_inc(silu_done, 1)
                    if e == 1:
                        for k in range(2):
                            act.wait_ge(stage_in[k], 16 * (i + DOWN_STAGED + 1))
                            ge(act, down_done, 2 * TT * i)
                            nc.scalar.copy(wd_hi[:, k, :], stage[k][:]).then_inc(w_hi, 1)
                    following = turn + 1 + e
                    if e == 0 or not last:
                        split_hi(following, 0)
                    for n in range(2):
                        act.wait_ge(gu_done, 2 * f + n + 1)
                        nc.scalar.copy(gu_hi[parity][:, e, n * HALF:(n + 1) * HALF], gu[n][:])\
                            .then_inc(gu_his, 1)
                    if e == 0 or not last:
                        split_hi(following, 1)

            ffn_turn(0, 0)
            with act.Fori(0, FFN_TURNS // 2 - 1) as m:
                ffn_turn(2 * m + 1, 1)
                ffn_turn(2 * m + 2, 0)
            ffn_turn(FFN_TURNS - 2, 1)
            ffn_turn(FFN_TURNS - 1, 0, last=True)

            def gate_rows(ks):
                for k in ks:
                    row_hi(N_PLE, k, (up_done, 2 * FT), wpg_hi[:, k, :])
            def ple_square(t, j):
                act.wait_ge(down_added, 2 * TT * (FFN_TURNS - 1) + 2 * t + 2)
                ge(act, n_tp, 2 * t + 4 * TT - 2)
                split_wait()
                square(resid[:, bass.ds(t, 1), :].rearrange("p o n -> p (o n)"), xn[j][:],
                       mean_sq[:, j:j + 1], n_sq)

            def ple_hi(t, j, bank_x=6, bank_p=6):
                transposed_hi(t + 2 * TT, lambda f: st_hi[j][:, f:f + 4, :], bank_x)
                act.wait_ge(p_tp, t + 1)
                nc.scalar.copy(pt_hi[j][:], bank(bank_p, 0, PLE).rearrange("p (k c) -> p k c", k=2))\
                    .then_inc(p_his, 1)

            def ple_tile(m, j, more=True):
                t = 2 * m + j
                if more:
                    ple_square(t + 1, 1 - j)
                for n in range(2):
                    act.wait_ge(pg_done, 2 * t + n + 1)
                    ge(act, x3_done, t)
                    nc.scalar.activation(pgate[:, n * HALF:(n + 1) * HALF], bank(2 * j + n),
                                         ACT.Sigmoid).then_inc(pg_sig, 1)
                if more:
                    ple_hi(t + 1, 1 - j)
                act.wait_ge(x3_done, t + 1)
                ge(act, f_rstd_ready, t)
                square(x3[j][:], sq_junk[:], f_mean_sq[:, j:j + 1], f_sq)

            gate_rows(range(KT // 2))
            ple_square(0, 0)
            gate_rows(range(KT // 2, KT))
            ple_hi(0, 0, 0, 2)
            for k in range(2):
                row_hi(N_PLE, KT + k, (down_done, 2 * TT * (FFN_TURNS - 1)), wpp_hi[:, k, :])
            ple_tile(0, 0)
            ple_tile(0, 1)
            ple_tile(1, 0)
            with act.Fori(1, TT // 2 - 1) as m:
                ple_tile(m, 1)
                ple_tile(m + 1, 0)
            ple_tile(TT // 2 - 1, 1, more=False)

        @block.vector
        def _(dve):
            sub = ALU.subtract

            def lo(dst, src, hi, done):
                nc.vector.tensor_tensor(dst, src, hi.bitcast(F32), sub).then_inc(done, 1)

            def normed(t, j, src, gains, scale=None):
                scale = rstd[:, j:j + 1] if scale is None else scale
                dve.wait_ge(n_rstd, t + 1)
                dve.wait_ge(gain_in, 16 * gains)
                nc.vector.scalar_tensor_tensor(xn[j][:], src, scale, gain[:],
                                               ALU.mult, ALU.mult).then_inc(n_xn, 1)

            def transposed_lo(t, dst_lo, dst_hi, bank0):
                for n in range(2):
                    dve.wait_ge(n_hi, 2 * t + n + 1)
                    lo(dst_lo(4 * n), bank(bank0 + n).rearrange("p (f c) -> p f c", f=4),
                       dst_hi(4 * n), n_lo)

            def h_cols(buf, t):
                return lambda f: buf[:, f:f + 4, bass.ds(t * P, P)]

            def tile_of(buf, t):
                return buf[:, bass.ds(t, 1), :].rearrange("p o n -> p (o n)")

            for t in range(2):
                normed(t, t, x_tiles[:, t, :], 1, x_rstd[:, t:t + 1])
            for t in range(TT):
                transposed_lo(t, h_cols(h_lo, t), h_cols(h_hi, t), 2 * (t % 2))
                if t + 2 < TT:
                    normed(t + 2, t % 2, x_tiles[:, t + 2, :], 1, x_rstd[:, t + 2:t + 3])
            dve.wait_ge(dft_hi, 2)
            lo(chan_lo[:], chan_raw[:], chan_hi[:], dft_lo)
            lo(pos_lo[:], pos_raw[:], pos_hi[:], dft_lo)

            dve.wait_ge(consts_in, 16 * 7)
            for r in range(2):
                nc.vector.tensor_tensor_reduce(lam_rows[:, 2 * r, :], lam_rows[:, 2 * r, :],
                                               lam_rows[:, 2 * r + 1, :], 1.0, 0.0, ALU.mult, ALU.add,
                                               lam_dot[:, r:r + 1]).then_inc(lam_dots, 1)
            dve.wait_ge(lam_exped, 1)
            nc.vector.scalar_tensor_tensor(neg_lam[:], lam_exp[:, 1:2], -LAMBDA_INIT, lam_exp[:, 0:1],
                                           ALU.add, sub).then_inc(lam_ready, 1)
            nc.vector.tensor_scalar(sub_gain[:], sub_gain[:], 1.0 - LAMBDA_INIT, None, ALU.mult)\
                .then_inc(lam_ready, 1)

            def u_split(g, j, n, first_bank=0):
                dve.wait_ge(u_his, 2 * g + n + 1)
                half = slice(n * HALF, (n + 1) * HALF)
                lo(u_lo[j][:, half], bank(first_bank + n), u_hi[j][:, half], u_los)

            def fold_split(g, c):
                dve.wait_ge(fold_his, 4 * g + c + 1)
                lo(fold_lo[:, :, c, :], folded[c % 2][:], fold_hi[:, :, c, :], fold_los)

            def fourier_group(g2, j, last=False):
                g = 2 * g2 + j
                if not last:
                    u_split(g + 1, 1 - j, 0)
                for c in range(4):
                    dve.wait_ge(far_copied, 4 * g + c + 1)
                    ge(dve, fold_los, 4 * g + c - 1)
                    near = bank(2 + c % 2, 0, 256)
                    nc.vector.tensor_tensor(folded[c % 2][:, 0, :], near, far_half[c % 2][:], ALU.add)
                    nc.vector.tensor_tensor(folded[c % 2][:, 1, :], near, far_half[c % 2][:], sub)\
                        .then_inc(fold_done, 1)
                    if c >= 1:
                        fold_split(g, c - 1)
                fold_split(g, 3)
                if not last:
                    u_split(g + 1, 1 - j, 1)
                for par in range(2):
                    dve.wait_ge(sin_copied, 2 * g + par + 1)
                    ge(dve, y_quarters, 4 * g)
                    for a, op in enumerate((sub, ALU.add)):
                        nc.vector.tensor_tensor(combo[a][par][:].rearrange("p (m k) -> p m k", k=2),
                                                in_order(4 + 2 * par),
                                                sin_part[par][:].rearrange("p (m k) -> p m k", k=2), op)\
                            .then_inc(combo_done, 1)

            u_split(0, 0, 0, 4)
            u_split(0, 0, 1, 4)
            fourier_group(0, 0)
            with dve.Fori(0, 3) as m:
                fourier_group(m, 1)
                fourier_group(m + 1, 0)
            fourier_group(3, 1, last=True)

            def proj_split(h, j, g, src):
                which, n = g // 2, g % 2
                half = slice(n * HALF, (n + 1) * HALF)
                dve.wait_ge(proj_hi, 6 * h + g + 1)
                for c in range(2):
                    rows = own[c]
                    if which == 0:
                        ins = nc.vector.scalar_tensor_tensor(
                            q2[j][own[1 - c], c, half], src[rows, :], qscale[rows, bass.ds(h, 1)],
                            q2[j][rows, c, half].bitcast(F32), ALU.mult, sub)
                    else:
                        ins = nc.vector.tensor_tensor(k_lo[j][rows, half], src[rows, :],
                                                      k2[j][rows, c, half].bitcast(F32), sub)
                ins.then_inc(proj_lo, 1)

            def wt_split(s, i):
                for n in range(2):
                    dve.wait_ge(wt_his, 2 * s + n + 1)
                    part = (slice(None), slice(4 * n, 4 * n + 4), slice((i % 2) * P, (i % 2 + 1) * P))
                    lo(wt_lo[part], bank(4 + n).rearrange("p (f c) -> p f c", f=4), wt_hi[part], wt_los)

            def value_lo(h, k):
                dve.wait_ge(v_his, 2 * h + k + 1)
                lo(v_lo[:, 4 * k:4 * k + 4, :], bank(4 + k).rearrange("p (f c) -> p f c", f=4),
                   v_hi[:, 4 * k:4 * k + 4, :], v_los)

            def sums_read(pair_no):
                dve.wait_ge(o_ss_done, pair_no + 1)
                nc.vector.tensor_copy(o_mean_sq[:], bank(7, 2 * P, 2 * P + 2)).then_inc(o_ss_read, 1)

            def out_norm(pair_no, slot, p, stored):
                dve.wait_ge(o_bcast, pair_no + 1)
                if p == 0:
                    ge(dve, o_stored, stored)
                nc.vector.tensor_tensor(stage[slot][:, 2 * P * p:2 * P * (p + 1)], o_raw[:],
                                        bank(7, 2 * P, 4 * P), ALU.mult).then_inc(o_done, 1)

            def head(h2, j, first=False, last=False):
                h = 2 * h2 + j
                for i in range(TT):
                    s = TT * h + i
                    pr = probs[i % 2]
                    start = ALIBI_0 - P * i
                    for c in range(2):
                        col = slice(2 * (i % 2) + c, 2 * (i % 2) + c + 1)
                        dve.wait_ge(score_done, 2 * s + c + 1)
                        ge(dve, wt_done, 2 * s - 2)
                        dve.nop(nofuse=True)
                        nc.vector.tensor_tensor_reduce(
                            pr[c][:], banks[:, 2 * c:2 * c + 2, :].rearrange("p b n -> p (b n)"),
                            distance[:, start:start + SEQ], 1.0, -3.0e38, ALU.add, ALU.max,
                            row_max[:, c:c + 1]).then_inc(biased, 1)
                        dve.wait_ge(biased, 2 * s + c + 1)
                        nc.vector.tensor_tensor(neg_max[:, col], row_max[:, c:c + 1],
                                                neg_slope[:, bass.ds(h, 1)], ALU.mult)\
                            .then_inc(max_ready, 1)
                    early = i % 2 == 0
                    before = not (first and i == 0)
                    pair_even = PAIRS * h + (i - 4) // 2
                    norm_pair = i % 2 == 0 and not (first and i < 4)
                    if norm_pair:
                        sums_read(pair_even)
                    if early and before:
                        wt_split(s - 1, (i - 1) % TT)
                    sum0, sum1 = (exp_sum[:, 2 * (i % 2) + c:2 * (i % 2) + c + 1] for c in range(2))
                    factor = coef[:, i % 2:i % 2 + 1]
                    dve.wait_ge(exped, 2 * s + 2)
                    nc.vector.reciprocal(inv_sum[:], sum1).then_inc(inv_step, 1)
                    nc.vector.scalar_tensor_tensor(o_eps[:, i:i + 1], sum0, EPS, sum0, ALU.mult, ALU.mult)
                    dve.wait_ge(inv_step, s + 1)
                    nc.vector.scalar_tensor_tensor(factor, sum0, neg_lam[:], inv_sum[:],
                                                   ALU.mult, ALU.mult).then_inc(coef_ready, 1)
                    dve.wait_ge(coef_ready, s + 1)
                    nc.vector.scalar_tensor_tensor(pr[0][:], pr[1][:], factor, pr[0][:],
                                                   ALU.mult, ALU.add).then_inc(diff_done, 1)
                    if norm_pair and i != 2:
                        if i == 0:
                            out_norm(pair_even, 1 - j, 2, 0)
                        else:
                            out_norm(pair_even, j, i // 2 - 2, 16 * h)
                    if not last and FILL_END.get(i, 4) < 4:
                        proj_split(h + 1, 1 - j, FILL_END[i], bank(6))
                    if i == 2 and norm_pair:
                        out_norm(pair_even, 1 - j, 3, 0)
                    if not early:
                        wt_split(s - 1, (i - 1) % TT)
                    if i == 2:
                        for k in range(2):
                            value_lo(h, k)

            for r in range(2):
                dve.wait_ge(y_stored[r], 16 * GROUPS // 2)
            dve.wait_ge(distance_ld, 16)
            for g in range(4):
                proj_split(0, 0, g, bank(g if g < 2 else 6 + g % 2))
            dve.wait_ge(lam_ready, 2)
            head(0, 0, first=True)
            with dve.Fori(0, 3) as m:
                head(m, 1)
                head(m + 1, 0)
            head(3, 1, last=True)
            last_pair = PAIRS * HEADS - 1
            wt_split(TT * HEADS - 1, TT - 1)
            sums_read(last_pair - 1)
            out_norm(last_pair - 1, 1, 2, 0)
            sums_read(last_pair)

            def branch_split(b):
                for t in range(KT):
                    if b == 0 and t == 4:
                        out_norm(last_pair, 1, 3, 0)
                    dve.wait_ge(b_his, KT * b + t + 1)
                    lo(b_lo[:, t, :], stage[t % 2][:] if b else x_tiles[:, t, :], b_hi[:, t, :], b_los)

            def gated(b, m, j, d, ns=range(2)):
                e = 2 * m + j
                for n in ns:
                    dst = merged[:, 4 * n:4 * n + 4, bass.ds(d, 1), :].rearrange("p t o c -> p t (o c)")
                    gate = sig[j][n]
                    dve.wait_ge(sig_done, 2 * e + n + 1)
                    dve.wait_ge(branch_done, 2 * e + n + 1)
                    src = bank(4 * j + 2 + n)
                    if b == 0:
                        nc.vector.tensor_tensor(dst, src.rearrange("p (t c) -> p t c", c=P),
                                                gate[:].rearrange("p (t c) -> p t c", c=P), ALU.mult)\
                            .then_inc(sig_read, 1)
                    else:
                        nc.vector.tensor_tensor(gate[:], src, gate[:], ALU.mult).then_inc(gated_done, 1)
                        dve.wait_ge(gated_done, 2 * d + n + 1)
                        nc.vector.tensor_tensor(dst, dst, gate[:].rearrange("p (t c) -> p t c", c=P),
                                                ALU.add).then_inc(sig_read, 1)

            for b in range(2):
                branch_split(b)
                with dve.Fori(0, KT // 2 - b) as m:
                    for j in range(2):
                        gated(b, m + KT // 2 * b, j, 2 * m + j)

            def row_lo(base, k, hi, lo_part):
                dve.wait_ge(w_hi, base + k + 1)
                dve.wait_ge(w_lo, base + k)
                lo(lo_part, row_buf[k % 4][:], hi, w_lo)
            def out_row(k):
                row_lo(N_OUT, k, wo_hi[:, k, :], wo_lo[:, k, :])

            def merged_lo(t, j):
                dve.wait_ge(m_hi, t + 1)
                lo(st_lo[j][:], one_mid(merged[:, bass.ds(t, 1), :, :]), st_hi[j][:], m_lo)

            def out_tile(m, j, more=True):
                t = 2 * m + j
                for n in range(2):
                    half = slice(n * HALF, (n + 1) * HALF)
                    dve.wait_ge(wo_done, 2 * t + n + 1)
                    dve.wait_ge(stage_in[j], 16 * (m + KT // 2 + STAGED + 1))
                    nc.vector.tensor_tensor(resid[:, bass.ds(t, 1), half].rearrange("p o n -> p (o n)"),
                                            bank(2 * j + n), stage[j][:, half], ALU.add)\
                        .then_inc(x1_done, 1)
                if more:
                    merged_lo(t + 2, j)
                normed(t + TT, j, tile_of(resid, t), 2)
                transposed_lo(t + TT, h_cols(h_lo, t), h_cols(h_hi, t), 4 + 2 * j)

            out_row(1)
            out_row(3)
            gated(1, KT - 1, 0, KT - 2)
            out_row(5)
            gated(1, KT - 1, 1, KT - 1, (0,))
            merged_lo(0, 0)
            out_row(7)
            gated(1, KT - 1, 1, KT - 1, (1,))
            merged_lo(1, 1)
            with dve.Fori(0, TT // 2 - 1) as m:
                for j in range(2):
                    out_tile(m, j)
            for j in range(2):
                out_tile(TT // 2 - 1, j, more=False)

            def hidden(i, e, parity):
                f = 2 * i + e
                for n in range(2):
                    dve.wait_ge(silu_done, 2 * f + n + 1)
                    dve.wait_ge(up_done, 2 * f + n + 1)
                    ge(dve, gu_his, 2 * f + n - 1)
                    ge(dve, gu_los, 2 * f + n - 1)
                    nc.vector.tensor_tensor(gu[n][:], bank(2 + n), silu[n][:], ALU.mult)\
                        .then_inc(gu_done, 1)
                    half = slice(n * HALF, (n + 1) * HALF)
                    dve.wait_ge(gu_his, 2 * f + n + 1)
                    lo(gu_lo[parity][:, e, half], gu[n][:], gu_hi[parity][:, e, half], gu_los)

            def down_add(i, ts=range(TT)):
                for t in ts:
                    for n in range(2):
                        dst = resid[:, t, n * HALF:(n + 1) * HALF]
                        dve.wait_ge(down_done, 2 * TT * i + 2 * t + n + 1)
                        nc.vector.tensor_tensor(dst, bank(4 + (2 * t + n) % 4), dst, ALU.add)\
                            .then_inc(down_added, 1)

            def ffn_turn(i, parity):
                hidden(i, 0, parity)
                down_add(i - 1)
                hidden(i, 1, parity)
            hidden(0, 0, 0)
            hidden(0, 1, 0)
            with dve.Fori(0, FFN_TURNS // 2) as m:
                ffn_turn(2 * m + 1, 1)
                ffn_turn(2 * m + 2, 0)
            def ple_lo(t, j, bank_x=6):
                transposed_lo(t + 2 * TT, lambda f: st_lo[j][:, f:f + 4, :],
                              lambda f: st_hi[j][:, f:f + 4, :], bank_x)

            def ple_lo_p(t, j, bank_p=6):
                dve.wait_ge(p_his, t + 1)
                lo(pt_lo[j][:], bank(bank_p, 0, PLE).rearrange("p (k c) -> p k c", k=2), pt_hi[j][:], p_los)

            def ple_tile(m, j, more=True):
                t = 2 * m + j
                if more:
                    normed(t + 1 + 2 * TT, 1 - j, tile_of(resid, t + 1), 3)
                    ple_lo(t + 1, 1 - j)
                for n in range(2):
                    half = slice(n * HALF, (n + 1) * HALF)
                    dve.wait_ge(pg_sig, 2 * t + n + 1)
                    dve.wait_ge(pp_done, 2 * t + n + 1)
                    nc.vector.tensor_tensor(pgate[:, half], bank(4 + n), pgate[:, half], ALU.mult)\
                        .then_inc(ple_mul, 1)
                if more:
                    ple_lo_p(t + 1, 1 - j)
                dve.wait_ge(ple_mul, 2 * t + 2)
                ge(dve, y_final, t - 1)
                nc.vector.tensor_tensor(x3[j][:], tile_of(resid, t), pgate[:], ALU.add)\
                    .then_inc(x3_done, 1)
                dve.wait_ge(f_rstd_ready, t + 1)
                dve.wait_ge(gain_in, 16 * 4)
                ge(dve, out_stored[j], 16 * m)
                nc.vector.scalar_tensor_tensor(stage[j][:], x3[j][:], f_rstd[:, j:j + 1], gain_final[:],
                                               ALU.mult, ALU.mult).then_inc(y_final, 1)

            last = FFN_TURNS - 1
            for t in range(TT):
                down_add(last, (t,))
                if t in (0, 2, 4, 6):
                    row_lo(N_PLE, t + 1, wpg_hi[:, t + 1, :], wpg_lo[:, t + 1, :])
                if t == 2:
                    normed(2 * TT, 0, tile_of(resid, 0), 3)
                if t == 5:
                    ple_lo(0, 0, 0)
                    ple_lo_p(0, 0, 2)
            row_lo(N_PLE, KT + 1, wpp_hi[:, 1, :], wpp_lo[:, 1, :])
            ple_tile(0, 0)
            ple_tile(0, 1)
            ple_tile(1, 0)
            with dve.Fori(1, TT // 2 - 1) as m:
                ple_tile(m, 1)
                ple_tile(m + 1, 0)
            ple_tile(TT // 2 - 1, 1, more=False)

        @block.tensor
        def _(pe):
            def passes(out_ap, a_hi, a_lo, b_hi_, b_lo_, first, last):
                terms = ((a_hi, b_hi_), (a_hi, b_lo_), (a_lo, b_hi_))
                for q, (a, b) in enumerate(terms):
                    ins = nc.tensor.matmul(out_ap, a, b, start=first and q == 0, stop=last and q == 2)
                return ins

            def weights(n):
                pe.wait_ge(w_hi, n + 1)
                pe.wait_ge(w_lo, n + 1)

            def slab_product(out_ap, slot, n, ks=range(KT)):
                half = slice(n * HALF, (n + 1) * HALF)
                for k in ks:
                    ins = passes(out_ap, st_hi[slot][:, k, :], st_lo[slot][:, k, :],
                                 h_hi[:, k, half], h_lo[:, k, half], k == 0, k == KT - 1)
                return ins

            def norm_transpose(t, j, bank0):
                pe.wait_ge(n_xn, t + 1)
                for n in range(2):
                    for f in range(4):
                        ins = nc.tensor.transpose(bank(bank0 + n, f * P, (f + 1) * P),
                                                  xn[j][:, (4 * n + f) * P:(4 * n + f + 1) * P], ident[:])
                    ins.then_inc(n_tp, 1)

            pe.wait_ge(ident_ld, 16)
            def first_transposes(ts):
                for t in ts:
                    ge(pe, n_lo, 2 * t - 2)
                    norm_transpose(t, t % 2, 2 * (t % 2))
            first_transposes(range(TT // 2 + 1))

            def project_u(g, j, n, first_bank=0, ks=range(KT)):
                weights(g)
                ge(pe, u_los, 2 * g + n - 1)
                ins = slab_product(bank(first_bank + n), j, n, ks)
                if ks[-1] == KT - 1:
                    ins.then_inc(u_done, 1)

            def channel_dft(g, j):
                pe.wait_ge(u_los, 2 * g + 2)
                for c in range(4):
                    par, tile = c // 2, c % 2
                    ge(pe, fold_done, 4 * g + c - 1)
                    for far in range(2):
                        at = 2 * P * (tile + 2 * far) + par
                        tok = slice(at, at + 2 * P - 1, 2)
                        ins = passes(bank(2 + c % 2, 256 * far, 256 * far + 256),
                                     u_hi[j][:, tok], u_lo[j][:, tok], chan_hi[:], chan_lo[:],
                                     True, True)
                    ins.then_inc(chan_done, 1)

            def position_dft(g):
                pe.wait_ge(fold_los, 4 * g + 4)
                if isinstance(g, int) and g == 0:
                    pe.wait_ge(u_los, 2)
                ge(pe, combo_done, 4 * g)
                for par in range(2):
                    for trig in range(2):
                        for k_odd in range(2):
                            for tile in range(2):
                                c = 2 * par + tile
                                chans = slice(P * trig, P * (trig + 1))
                                tab = 4 * c + 2 * k_odd + trig
                                ins = passes(bank(4 + 2 * par + trig, KW * k_odd, KW * (k_odd + 1)),
                                             fold_hi[:, k_odd, c, chans], fold_lo[:, k_odd, c, chans],
                                             pos_hi[:, tab, :], pos_lo[:, tab, :],
                                             tile == 0, tile == 1)
                    ins.then_inc(pos_done, 1)

            pe.wait_ge(n_lo, TT)
            project_u(0, 0, 0, 4, range(KT // 2))
            first_transposes((TT // 2 + 1,))
            project_u(0, 0, 0, 4, range(KT // 2, KT))
            first_transposes(range(TT // 2 + 2, TT))
            pe.wait_ge(n_lo, 2 * TT)
            project_u(0, 0, 1, 4)
            pe.wait_ge(dft_lo, 2)

            def project(h, n_slab, slot, g, out_bank, ks=range(KT)):
                if ks[0] == 0:
                    weights(n_slab)
                ins = slab_product(bank(out_bank), slot, g % 2, ks)
                if ks[-1] == KT - 1:
                    ins.then_inc(proj_done, 1)

            def fourier_group(g2, j, last=False):
                g = 2 * g2 + j
                for n in range(2):
                    if last:
                        pe.wait_ge(u_los, 2 * GROUPS)
                        project(0, N_ATTN, 0, n, n)
                    else:
                        project_u(g + 1, 1 - j, n)
                    if n == 0:
                        channel_dft(g, j)
                position_dft(g)
            fourier_group(0, 0)
            with pe.Fori(0, 3) as m:
                fourier_group(m, 1)
                fourier_group(m + 1, 0)
            fourier_group(3, 1, last=True)

            def scores(s, j, i):
                ge(pe, biased, 2 * s)
                tok = slice(i * P, (i + 1) * P)
                for n in range(2):
                    half = slice(n * HALF, (n + 1) * HALF)
                    for c in range(2):
                        nc.tensor.matmul(bank(2 * c + n), q2[j][:, c, tok], k2[j][:, c, half],
                                         start=True, stop=False)
                    for c, rows in enumerate(own):
                        ins = nc.tensor.matmul(bank(2 * c + n), q2[j][rows, c, tok], k_lo[j][rows, half],
                                               start=False, stop=True)
                        if n == 1:
                            ins.then_inc(score_done, 1)

            def transpose_diff(s, i, h=None):
                pe.wait_ge(diff_done, s + 1)
                for n in range(2):
                    ge(pe, wt_los, 2 * s + n - 1)
                    if h is not None:
                        pe.wait_ge(v_los, 2 * h + n + 1)
                    for f in range(4):
                        kt = 4 * n + f
                        ins = nc.tensor.transpose(bank(4 + n, f * P, (f + 1) * P),
                                                  probs[i % 2][0][:, kt * P:(kt + 1) * P], ident[:])
                    ins.then_inc(wt_done, 1)

            def values(pair_no):
                pe.wait_ge(wt_los, 4 * pair_no + 4)
                ge(pe, o_done, pair_no)
                for kt in range(TT):
                    ins = passes(bank(7, 0, 2 * P), v_hi[:, kt, :], v_lo[:, kt, :],
                                 wt_hi[:, kt, :], wt_lo[:, kt, :], kt == 0, kt == TT - 1)
                ins.then_inc(pv_done, 1)

            def sums_of_squares(pair_no):
                pe.wait_ge(o_squared, pair_no + 1)
                pe.wait_ge(o_copied, pair_no + 1)
                for q in range(2):
                    ins = nc.tensor.matmul(bank(7, 2 * P + q, 2 * P + q + 1), o_sq[:, q * P:(q + 1) * P],
                                           mean_col[:], start=True, stop=True)
                ins.then_inc(o_ss_done, 1)

            def spread_rstd(pair_no):
                pe.wait_ge(o_rstd_ready, pair_no + 1)
                for q in range(2):
                    ins = nc.tensor.transpose(bank(7, (2 + q) * P, (3 + q) * P),
                                              o_rstd[:, q:q + 1].to_broadcast([P, P]), ident[:])
                ins.then_inc(o_bcast, 1)

            def transpose_v(s):
                for n in range(2):
                    pe.wait_ge(wt_los, 2 * s + n - 1)
                    for f in range(4):
                        tok = (4 * n + f) * P
                        ins = nc.tensor.transpose(bank(4 + n, f * P, (f + 1) * P), v_t[:, tok:tok + P],
                                                  ident[:])
                    ins.then_inc(vt_done, 1)

            def fill(h2, j, i):
                h1 = 2 * h2 + j + 1
                g, ks = FILL[i]
                which = g // 2
                r = 3 * (j + 1) + which
                if ks[0] == 0:
                    pe.wait_ge(proj_hi, 6 * h1 + g)
                    pe.wait_ge(proj_lo, 4 * h1 + min(g, 4))
                project(h1, N_ATTN + 6 * h2 + r, r % 2, g, 6, ks)

            def head(h2, j, first=False, last=False):
                h = 2 * h2 + j
                for i in range(TT):
                    s = TT * h + i
                    if i == 0:
                        pe.wait_ge(proj_lo, 4 * h + 4)
                        pe.wait_ge(k_spread, 2 * h + 2)
                    scores(s, j, i)
                    before = not (first and i == 0)
                    pair_even = PAIRS * h + (i - 4) // 2
                    norm_pair = i % 2 == 0 and not (first and i < 4)
                    if norm_pair:
                        sums_of_squares(pair_even)
                    if i % 2 == 0 and before:
                        transpose_diff(s - 1, (i - 1) % TT)
                    if i % 4 == 1 and not (first and i == 1):
                        values(PAIRS * h + (i - 3) // 2)
                    if last:
                        if i == 0:
                            weights(N_GATE)
                            pe.wait_ge(proj_hi, 6 * HEADS)
                        ins = slab_product(bank(6), 0, 0, (i,))
                        if i == TT - 1:
                            ins.then_inc(gate_done, 1)
                    else:
                        fill(h2, j, i)
                    if i == 2:
                        pe.wait_ge(proj_hi, 6 * h + 6)
                        transpose_v(s)
                    if i % 4 == 3:
                        if i == 3:
                            pe.wait_ge(v_los, 2 * h + 2)
                        values(PAIRS * h + (i - 3) // 2)
                    if i % 2 == 1:
                        transpose_diff(s - 1, (i - 1) % TT, h if i == 3 else None)
                    if norm_pair:
                        spread_rstd(pair_even)

            pe.wait_ge(combo_done, 4 * GROUPS)
            for g in range(2, 6):
                if g >= 4:
                    pe.wait_ge(proj_hi, g - 1)
                    pe.wait_ge(proj_lo, min(g - 1, 4))
                project(0, N_ATTN + g // 2, (g // 2) % 2, g, 6 + g % 2)
            pe.wait_ge(proj_hi, 6)
            head(0, 0, first=True)
            with pe.Fori(0, 3) as m:
                head(m, 1)
                head(m + 1, 0)
            head(3, 1, last=True)

            def gate_product(m, j, n_slab, ns=range(2)):
                e = 2 * m + j
                weights(n_slab)
                for n in ns:
                    ge(pe, sig_done, 2 * e + n - 3)
                    slab_product(bank(4 * j + n), j, n).then_inc(gate_done, 1)

            last_pair = PAIRS * HEADS - 1
            transpose_diff(TT * HEADS - 1, TT - 1)
            pe.wait_ge(biased, 2 * TT * HEADS)
            sums_of_squares(last_pair - 1)
            gate_product(0, 0, N_GATE, (1,))
            spread_rstd(last_pair - 1)
            values(last_pair)
            gate_product(0, 1, N_GATE + 1, (0,))
            sums_of_squares(last_pair)

            def branch_product(m, j, n_slab, b=None):
                e = 2 * m + j
                weights(n_slab)
                for n in range(2):
                    half = slice(n * HALF, (n + 1) * HALF)
                    ge(pe, sig_read, 2 * e + n - 3)
                    for k in range(KT):
                        if b is not None and n == 0:
                            pe.wait_ge(b_los, KT * b + k + 1)
                        ins = passes(bank(4 * j + 2 + n), st_hi[j][:, k, :], st_lo[j][:, k, :],
                                     b_hi[:, k, half], b_lo[:, k, half], k == 0, k == KT - 1)
                    ins.then_inc(branch_done, 1)

            def branch_pair(m, b=None):
                branch_product(m, 0, 4 * m + N_GATE + 2, b)
                if b == 0:
                    pe.wait_ge(o_done, PAIRS * HEADS)
                    pe.wait_ge(sig_done, 1)
                branch_product(m, 1, 4 * m + N_GATE + 3)

            def gate_turn(m, b=None):
                for j in range(2):
                    gate_product(m, j, 4 * m + N_GATE + j)
                branch_pair(m, b)

            gate_product(0, 1, N_GATE + 1, (1,))
            spread_rstd(last_pair)
            branch_pair(0, 0)
            with pe.Fori(1, KT // 2) as m:
                gate_turn(m)
            gate_turn(KT // 2, 1)
            with pe.Fori(KT // 2 + 1, KT - 1) as m:
                gate_turn(m)
            for j in range(2):
                branch_product(KT - 1, j, N_OUT - 4 + j)
            for j in range(2):
                gate_product(KT - 1, j, N_OUT - 2 + j)

            def out_tile(m, j, first=False):
                t = 2 * m + j
                pe.wait_ge(m_lo, t + 1)
                for n in range(2):
                    half = slice(n * HALF, (n + 1) * HALF)
                    ge(pe, x1_done, 2 * t + n - 3)
                    for k in range(KT):
                        if first and n == 0:
                            weights(N_OUT + k)
                        ins = passes(bank(2 * j + n), st_hi[j][:, k, :], st_lo[j][:, k, :],
                                     wo_hi[:, k, half], wo_lo[:, k, half], k == 0, k == KT - 1)
                    ins.then_inc(wo_done, 1)

            def out_transpose(t, j):
                ge(pe, n_lo, 2 * t + 2 * TT - 2)
                norm_transpose(t + TT, j, 4 + 2 * j)

            pe.wait_ge(sig_read, 4 * KT - 2)
            out_tile(0, 0, first=True)
            out_tile(0, 1)
            pe.wait_ge(sig_read, 4 * KT)
            out_transpose(0, 0)
            out_tile(1, 0)
            out_transpose(1, 1)
            with pe.Fori(1, TT // 2 - 1) as m:
                out_tile(m, 1)
                out_transpose(2 * m, 0)
                out_tile(m + 1, 0)
                out_transpose(2 * m + 1, 1)
            out_tile(TT // 2 - 1, 1)
            out_transpose(TT - 2, 0)

            def gate_side(i, e, n):
                weights(6 * i + N_FFN + 2 * e)
                ge(pe, silu_done, 4 * i + 2 * e + n - 1)
                slab_product(bank(n), 0, n).then_inc(g_done, 1)

            def up_side(i, e, n):
                weights(6 * i + N_FFN + 2 * e + 1)
                ge(pe, gu_done, 4 * i + 2 * e + n - 1)
                slab_product(bank(2 + n), 1, n).then_inc(up_done, 1)

            def hidden(i, e):
                for n in range(2):
                    gate_side(i, e, n)
                for n in range(2):
                    up_side(i, e, n)

            def down(i, parity, ts=range(TT)):
                weights(6 * i + N_FFN + 5)
                for t in ts:
                    if t == ts[0] or t == TT // 2:
                        pe.wait_ge(gu_los, 4 * i + (3 if t < TT // 2 else 4))
                    for n in range(2):
                        half = slice(n * HALF, (n + 1) * HALF)
                        ge(pe, down_added, 2 * TT * i + 2 * t + n - 3)
                        for e in range(2):
                            tok = slice(t * P, (t + 1) * P)
                            ins = passes(bank(4 + (2 * t + n) % 4), gu_hi[parity][:, e, tok],
                                         gu_lo[parity][:, e, tok], wd_hi[:, e, half], wd_lo[:, e, half],
                                         e == 0, e == 1)
                        ins.then_inc(down_done, 1)

            def ffn_turn(i, parity):
                hidden(i, 0)
                down(i - 1, 1 - parity)
                hidden(i, 1)
            pe.wait_ge(n_lo, 3 * TT)
            pe.wait_ge(x1_done, 2 * TT - 2)
            gate_side(0, 0, 0)
            out_transpose(TT - 1, 1)
            pe.wait_ge(x1_done, 2 * TT)
            up_side(0, 0, 0)
            pe.wait_ge(n_lo, 4 * TT)
            gate_side(0, 0, 1)
            up_side(0, 0, 1)
            hidden(0, 1)
            ffn_turn(1, 1)
            ffn_turn(2, 0)
            with pe.Fori(1, FFN_TURNS // 2) as m:
                ffn_turn(2 * m + 1, 1)
                ffn_turn(2 * m + 2, 0)

            def ple_transpose(t, j, bank_x=6, bank_p=6):
                ge(pe, p_los, t)
                norm_transpose(t + 2 * TT, j, bank_x)
                if bank_p != bank_x:
                    ple_transpose_p(t, j, bank_p)

            def ple_transpose_p(t, j, bank_p=6):
                if bank_p == 6:
                    pe.wait_ge(n_lo, 2 * t + 4 * TT + 1)
                if isinstance(t, int):
                    pe.wait_ge(p_in[j], 16 * (t // 2 + 1))
                else:
                    pe.wait_ge(p_in[j], 8 * (t - j) + 16)
                for k in range(2):
                    ins = nc.tensor.transpose(bank(bank_p, k * P, (k + 1) * P), p_raw[j][:, k * P:(k + 1) * P],
                                              ident[:])
                ins.then_inc(p_tp, 1)

            def ple_tile(m, j, more=True, first=False):
                t = 2 * m + j
                pe.wait_ge(n_lo, 2 * t + 4 * TT + 2)
                for n in range(2):
                    half = slice(n * HALF, (n + 1) * HALF)
                    ge(pe, pg_sig, 2 * t + n - 3)
                    for k in range(KT):
                        if first and n == 0:
                            weights(N_PLE + k)
                        ins = passes(bank(2 * j + n), st_hi[j][:, k, :], st_lo[j][:, k, :],
                                     wpg_hi[:, k, half], wpg_lo[:, k, half], k == 0, k == KT - 1)
                    ins.then_inc(pg_done, 1)
                if first:
                    pe.wait_ge(down_added, 2 * TT * FFN_TURNS)
                if more:
                    ple_transpose(t + 1, 1 - j)
                pe.wait_ge(p_los, t + 1)
                if first:
                    weights(N_PLE + KT + 1)
                for n in range(2):
                    half = slice(n * HALF, (n + 1) * HALF)
                    ge(pe, ple_mul, 2 * t + n - 1)
                    for k in range(2):
                        ins = passes(bank(4 + n), pt_hi[j][:, k, :], pt_lo[j][:, k, :],
                                     wpp_hi[:, k, half], wpp_lo[:, k, half], k == 0, k == 1)
                    ins.then_inc(pp_done, 1)
                if more:
                    ple_transpose_p(t + 1, 1 - j)

            down(FFN_TURNS - 1, 0, range(TT - 2))
            pe.wait_ge(gu_done, 2 * FT)
            ple_transpose(0, 0, 0, 2)
            down(FFN_TURNS - 1, 0, range(TT - 2, TT))
            ple_tile(0, 0, first=True)
            ple_tile(0, 1)
            ple_tile(1, 0)
            with pe.Fori(1, TT // 2 - 1) as m:
                ple_tile(m, 1)
                ple_tile(m + 1, 0)
            ple_tile(TT // 2 - 1, 1, more=False)


_INS = ['x', 'p', 'g_mix', 'w_in', 'lambda_q1', 'lambda_k1', 'lambda_q2', 'lambda_k2', 'g_subln',
        'w_fourier_out', 'w_attn_out', 'w_branch_gate', 'b_branch_gate', 'w_o', 'g_ffn',
        'w_ffn_gate', 'w_ffn_up', 'w_ffn_down', 'g_ple', 'w_ple_gate', 'w_ple_proj', 'g_final']


def shape_constants():
    import numpy as np
    row = np.arange(P)
    turn = 2 * np.pi * np.outer(row, row) / P
    chan = np.concatenate([np.cos(turn), np.sin(turn)], 1) / np.sqrt(P)
    pos = np.zeros((P, 16, KW))
    for parity in range(2):
        for tile in range(2):
            s = 2 * (P * tile + row) + parity
            for k_odd in range(2):
                k = 2 * np.arange(KW) + k_odd
                turn = 2 * np.pi * (np.outer(s, k) % SEQ) / SEQ
                for trig, table in enumerate((np.cos(turn), np.sin(turn))):
                    pos[:, 4 * (2 * parity + tile) + 2 * k_odd + trig] = table / np.sqrt(SEQ)
    distance = -np.abs(row[:, None] + ALIBI_0 - np.arange(ALIBI_W)[None])
    slope = 2.0 ** (-8.0 * np.arange(1, HEADS + 1) / HEADS)
    consts = np.concatenate([HD ** -0.5 / slope, slope, -slope])
    out = {"ident": np.eye(P), "chan_dft": chan, "pos_dft": pos, "distance": distance,
           "head_consts": np.repeat(consts[None], P, 0)}
    return {k: np.ascontiguousarray(v, dtype=np.float32) for k, v in out.items()}


def kernel(**inputs):
    import numpy as _np
    import concourse.bacc as _bacc
    from concourse import mybir as _mybir
    from concourse.bass_utils import run_bass_kernel_spmd as _run

    nc = _bacc.Bacc("TRN2", target_bir_lowering=False, num_devices=1)
    arrays = {f"in_{n}_dram": _np.ascontiguousarray(inputs[n]) for n in _INS}
    arrays.update({f"const_{n}_dram": v for n, v in shape_constants().items()})
    args = [nc.dram_tensor(n, a.shape, _mybir.dt.from_np(a.dtype), kind="ExternalInput").ap()
            for n, a in arrays.items()]
    args.append(nc.dram_tensor("out_0_dram", (1, SEQ, D), _mybir.dt.float32, kind="ExternalOutput").ap())
    encoder_layer(nc, *args)
    r = _run(nc, [arrays], core_ids=[0])
    return r.results[0]["out_0_dram"]
```
